# Optimizing a Trainium2 kernel written in Bass

```python
import jax, jax.numpy as jnp
from jax import lax
import numpy as np

D_MODEL = 1024
BATCH = 1
SEQ = 128
DEPTH = 2
DEC_BATCH = 1
DEC_SEQ = 256
PAST_LEN = 128

GRID_W = 64
HEAD_DIM = 64
ATTN_SCALE = HEAD_DIM ** -0.5
H_A = 4
W_A = H_A * HEAD_DIM
RET_CHUNK = 64
GN_EPS = 1e-5
H_B = 6
KV_B = 2
W_B = H_B * HEAD_DIM
KV_W_B = KV_B * HEAD_DIM
WINDOW = 128
BAND_BLOCK = 128
ROPE_BASE = 10000.0
H_C = 6
W_C = H_C * HEAD_DIM
NA_ROWS = 8
NA_COLS = 16
NA_QBLK = 16
NA_KCOLS = 32
MIX_WIDTH = W_A + W_B + W_C
SPLIT_POINTS = (W_A, 2 * W_A, 3 * W_A, 4 * W_A, 4 * W_A + W_B, 4 * W_A + W_B + KV_W_B,
                4 * W_A + W_B + 2 * KV_W_B, 4 * W_A + W_B + 2 * KV_W_B + W_C,
                4 * W_A + W_B + 2 * KV_W_B + 2 * W_C)
IN_WIDTH = 4 * W_A + W_B + 2 * KV_W_B + 3 * W_C
N_EXPERTS = 64
TOP_K = 6
N_GROUPS = 8
TOPK_GROUPS = 4
D_EXPERT = 256
D_SHARED = 256
ROUTE_SCALE = 2.5
MOE_BLOCK = 128
ALPHA = (2 * DEPTH) ** 0.25
BETA = (8 * DEPTH) ** -0.25
LN_EPS = 1e-5
NEG_INF = -1e30

kernel_name = "hybrid_ret_win_na_moe_diffusion_step"

def layer_norm(x, g, b):
    xf = x.astype(jnp.float32)
    mu = jnp.mean(xf, -1, keepdims=True)
    var = jnp.mean(jnp.square(xf - mu), -1, keepdims=True)
    return ((xf - mu) * lax.rsqrt(var + LN_EPS) * g + b).astype(x.dtype)

def heads(t, n):
    b, l, _ = t.shape
    return t.reshape(b, l, n, HEAD_DIM).transpose(0, 2, 1, 3)

def merge_heads(t):
    b, n, l, d = t.shape
    return t.transpose(0, 2, 1, 3).reshape(b, l, n * d)

def ada_params(cond, w_mod, b_mod):
    m = jax.nn.silu(cond) @ w_mod + b_mod
    return jnp.split(m[:, None, :], 6, axis=-1)

def axial_rope(l):
    t = jnp.arange(l)
    n_freq = HEAD_DIM // 4
    inv = ROPE_BASE ** (-jnp.arange(n_freq, dtype=jnp.float32) / n_freq)
    row = (t // GRID_W).astype(jnp.float32)[:, None] * inv
    col = (t % GRID_W).astype(jnp.float32)[:, None] * inv
    ang = jnp.concatenate([row, col], -1)
    return jnp.cos(ang), jnp.sin(ang)

def apply_rope(x, cos, sin):
    half = HEAD_DIM // 2
    xf = x.astype(jnp.float32)
    x1, x2 = xf[..., :half], xf[..., half:]
    return jnp.concatenate([x1 * cos - x2 * sin, x1 * sin + x2 * cos], -1).astype(x.dtype)

def retention_scan(q, k, v, log_gamma, s0):
    b, h, l, d = q.shape
    n = l // RET_CHUNK
    qc = q.reshape(b, h, n, RET_CHUNK, d)
    kc = k.reshape(b, h, n, RET_CHUNK, d)
    vc = v.reshape(b, h, n, RET_CHUNK, d)
    pos = jnp.arange(RET_CHUNK, dtype=jnp.float32)
    diff = pos[:, None] - pos[None, :]
    dmat = jnp.where(diff >= 0, jnp.exp(log_gamma[:, None, None] * jnp.maximum(diff, 0.0)), 0.0)
    inner = jnp.einsum('bhncd,bhnmd->bhncm', qc, kc) * dmat[None, :, None]
    o_inner = jnp.einsum('bhncm,bhnme->bhnce', inner, vc)
    zeta = jnp.exp(log_gamma[:, None] * (RET_CHUNK - 1 - pos))
    xi = jnp.exp(log_gamma[:, None] * (pos + 1.0))
    g_chunk = jnp.exp(log_gamma * RET_CHUNK)[None, :, None, None]
    kv = jnp.einsum('bhncd,bhnce->bhnde', kc * zeta[None, :, None, :, None], vc)

    def step(s, kv_i):
        return g_chunk * s + kv_i, s

    s_fin, s_prev = lax.scan(step, s0, jnp.moveaxis(kv, 2, 0))
    s_prev = jnp.moveaxis(s_prev, 0, 2)
    o_cross = jnp.einsum('bhncd,bhnde->bhnce', qc * xi[None, :, None, :, None], s_prev)
    return (o_inner + o_cross).reshape(b, h, l, d), s_fin

def retention_bidir(q, k, v, lg_f, lg_b, s0_f, s0_b):
    o_f, s_f = retention_scan(q, k, v, lg_f, s0_f)
    o_b, s_b = retention_scan(q[:, :, ::-1], k[:, :, ::-1], v[:, :, ::-1], lg_b, s0_b)
    return o_f + o_b[:, :, ::-1], s_f, s_b

def retention_readout(o, gate, gn_g, gn_b):
    mu = jnp.mean(o, -1, keepdims=True)
    var = jnp.mean(jnp.square(o - mu), -1, keepdims=True)
    on = merge_heads((o - mu) * lax.rsqrt(var + GN_EPS)) * gn_g + gn_b
    return (on * jax.nn.silu(gate.astype(jnp.float32))).astype(gate.dtype)

def dense_attn(q, k, v, sink):
    b, h, lq, d = q.shape
    n_kv = k.shape[1]
    g = h // n_kv
    qg = q.reshape(b, n_kv, g, lq, d)
    s = jnp.einsum('bkgqd,bksd->bkgqs', qg, k).astype(jnp.float32) * ATTN_SCALE
    if sink is not None:
        col = jnp.broadcast_to(sink.astype(jnp.float32).reshape(1, n_kv, g, 1, 1), (b, n_kv, g, lq, 1))
        p = jax.nn.softmax(jnp.concatenate([s, col], -1), axis=-1)[..., :-1]
    else:
        p = jax.nn.softmax(s, axis=-1)
    o = jnp.einsum('bkgqs,bksd->bkgqd', p.astype(v.dtype), v)
    return o.reshape(b, h, lq, d)

def banded_window_attn(q, k, v, k_ctx, v_ctx, sink):
    b, h, l, d = q.shape
    n_kv = k.shape[1]
    g = h // n_kv
    nb = l // BAND_BLOCK
    pad = ((0, 0), (0, 0), (BAND_BLOCK, BAND_BLOCK), (0, 0))

    def band(t):
        tp = jnp.pad(t, pad).reshape(b, n_kv, nb + 2, BAND_BLOCK, d)
        return jnp.concatenate([tp[:, :, 0:nb], tp[:, :, 1:nb + 1], tp[:, :, 2:nb + 2]], axis=3)

    kb, vb = band(k), band(v)
    qb = q.reshape(b, n_kv, g, nb, BAND_BLOCK, d)
    s_loc = jnp.einsum('bkgnqd,bknsd->bkgnqs', qb, kb).astype(jnp.float32) * ATTN_SCALE
    blk = jnp.arange(nb)[:, None, None] * BAND_BLOCK
    key_pos = blk - BAND_BLOCK + jnp.arange(3 * BAND_BLOCK)[None, None, :]
    q_pos = blk + jnp.arange(BAND_BLOCK)[None, :, None]
    valid = (jnp.abs(key_pos - q_pos) <= WINDOW) & (key_pos >= 0) & (key_pos < l)
    s_loc = jnp.where(valid, s_loc, NEG_INF)
    s_ctx = jnp.einsum('bkgnqd,bksd->bkgnqs', qb, k_ctx).astype(jnp.float32) * ATTN_SCALE
    col = jnp.broadcast_to(sink.astype(jnp.float32).reshape(1, n_kv, g, 1, 1, 1),
                           (b, n_kv, g, nb, BAND_BLOCK, 1))
    p = jax.nn.softmax(jnp.concatenate([s_loc, s_ctx, col], -1), axis=-1)
    n_loc = 3 * BAND_BLOCK
    lc = k_ctx.shape[2]
    o = (jnp.einsum('bkgnqs,bknsd->bkgnqd', p[..., :n_loc].astype(v.dtype), vb)
         + jnp.einsum('bkgnqs,bksd->bkgnqd', p[..., n_loc:n_loc + lc].astype(v.dtype), v_ctx))
    return o.reshape(b, h, l, d)

def neighbourhood_attn(q, k, v, k_ctx, v_ctx, rpb):
    b, h, l, d = q.shape
    rows = l // GRID_W
    kh = min(NA_ROWS, rows)
    ncb = GRID_W // NA_QBLK
    r = jnp.arange(rows)
    r0 = jnp.clip(r - kh // 2, 0, rows - kh)
    key_rows = r0[:, None] + jnp.arange(kh)[None, :]
    cstart = jnp.clip(jnp.arange(ncb) * NA_QBLK - (NA_KCOLS - NA_QBLK) // 2, 0, GRID_W - NA_KCOLS)
    key_cols = cstart[:, None] + jnp.arange(NA_KCOLS)[None, :]
    idx = (key_rows[:, None, :, None] * GRID_W + key_cols[None, :, None, :]).reshape(rows, ncb, kh * NA_KCOLS)
    kg = jnp.take(k, idx, axis=2)
    vg = jnp.take(v, idx, axis=2)
    qb = q.reshape(b, h, rows, ncb, NA_QBLK, d)
    s_loc = jnp.einsum('bhrjqd,bhrjsd->bhrjqs', qb, kg).astype(jnp.float32) * ATTN_SCALE
    q_cols = jnp.arange(ncb)[:, None] * NA_QBLK + jnp.arange(NA_QBLK)[None, :]
    c0 = jnp.clip(q_cols - NA_COLS // 2, 0, GRID_W - NA_COLS)
    kc_b = key_cols[:, None, :]
    in_win = (kc_b >= c0[:, :, None]) & (kc_b < c0[:, :, None] + NA_COLS)
    ri = (key_rows - r[:, None] + NA_ROWS - 1)[:, None, None, :, None]
    ci = jnp.clip(kc_b - q_cols[:, :, None] + NA_COLS - 1, 0, 2 * NA_COLS - 2)[None, :, :, None, :]
    bias = rpb[:, ri, ci].reshape(h, rows, ncb, NA_QBLK, kh * NA_KCOLS).astype(jnp.float32)
    mask = jnp.broadcast_to(in_win[:, :, None, :], (ncb, NA_QBLK, kh, NA_KCOLS)).reshape(ncb, NA_QBLK, kh * NA_KCOLS)
    s_loc = jnp.where(mask[None, None, None], s_loc + bias[None], NEG_INF)
    s_ctx = jnp.einsum('bhrjqd,bhsd->bhrjqs', qb, k_ctx).astype(jnp.float32) * ATTN_SCALE
    p = jax.nn.softmax(jnp.concatenate([s_loc, s_ctx], -1), axis=-1)
    n_loc = kh * NA_KCOLS
    o = (jnp.einsum('bhrjqs,bhrjsd->bhrjqd', p[..., :n_loc].astype(v.dtype), vg)
         + jnp.einsum('bhrjqs,bhsd->bhrjqd', p[..., n_loc:].astype(v.dtype), v_ctx))
    return o.reshape(b, h, l, d)

def mixer_context(h, w_in, w_out, dec_f, dec_b, gn_g, gn_b, sink):
    b, l, _ = h.shape
    qa, ka, va, ga, qb, kb, vb, qc, kc, vc = jnp.split(h @ w_in, SPLIT_POINTS, axis=-1)
    s0 = jnp.zeros((b, H_A, HEAD_DIM, HEAD_DIM), jnp.float32)
    oa, st_f, st_b = retention_bidir(heads(qa, H_A).astype(jnp.float32),
                                     heads(ka, H_A).astype(jnp.float32) * ATTN_SCALE,
                                     heads(va, H_A).astype(jnp.float32),
                                     jax.nn.log_sigmoid(dec_f.astype(jnp.float32)),
                                     jax.nn.log_sigmoid(dec_b.astype(jnp.float32)), s0, s0)
    ya = retention_readout(oa, ga, gn_g, gn_b)
    kb_h, vb_h = heads(kb, KV_B), heads(vb, KV_B)
    yb = merge_heads(dense_attn(heads(qb, H_B), kb_h, vb_h, sink))
    kc_h, vc_h = heads(kc, H_C), heads(vc, H_C)
    yc = merge_heads(dense_attn(heads(qc, H_C), kc_h, vc_h, None))
    y = jnp.concatenate([ya, yb, yc], -1) @ w_out
    return y, st_f.astype(h.dtype), st_b.astype(h.dtype), kb_h, vb_h, kc_h, vc_h

def mixer_latent(h, st_f, st_b, kb_ctx, vb_ctx, kc_ctx, vc_ctx, w_in, w_out, dec_f, dec_b, gn_g, gn_b, sink, rpb):
    b, l, _ = h.shape
    qa, ka, va, ga, qb, kb, vb, qc, kc, vc = jnp.split(h @ w_in, SPLIT_POINTS, axis=-1)
    oa, _, _ = retention_bidir(heads(qa, H_A).astype(jnp.float32),
                               heads(ka, H_A).astype(jnp.float32) * ATTN_SCALE,
                               heads(va, H_A).astype(jnp.float32),
                               jax.nn.log_sigmoid(dec_f.astype(jnp.float32)),
                               jax.nn.log_sigmoid(dec_b.astype(jnp.float32)),
                               st_f.astype(jnp.float32), st_b.astype(jnp.float32))
    ya = retention_readout(oa, ga, gn_g, gn_b)
    cos, sin = axial_rope(l)
    yb = merge_heads(banded_window_attn(apply_rope(heads(qb, H_B), cos, sin),
                                        apply_rope(heads(kb, KV_B), cos, sin),
                                        heads(vb, KV_B), kb_ctx, vb_ctx, sink))
    yc = merge_heads(neighbourhood_attn(heads(qc, H_C), heads(kc, H_C), heads(vc, H_C),
                                        kc_ctx, vc_ctx, rpb))
    return jnp.concatenate([ya, yb, yc], -1) @ w_out

def moe_ffn(h, w_router, b_router, w_gu, w_down, w_sgu, w_sdown):
    b, l, dm = h.shape
    t = b * l
    x = h.reshape(t, dm)
    scores = jax.nn.sigmoid((x @ w_router).astype(jnp.float32))
    sel = scores + b_router.astype(jnp.float32)
    grp_score = lax.top_k(sel.reshape(t, N_GROUPS, N_EXPERTS // N_GROUPS), 2)[0].sum(-1)
    _, gidx = lax.top_k(grp_score, TOPK_GROUPS)
    gmask = jax.nn.one_hot(gidx, N_GROUPS, dtype=jnp.float32).sum(1) > 0
    emask = jnp.repeat(gmask, N_EXPERTS // N_GROUPS, axis=1)
    _, eidx = lax.top_k(jnp.where(emask, sel, NEG_INF), TOP_K)
    wsel = jnp.take_along_axis(scores, eidx, axis=1)
    wsel = wsel / jnp.sum(wsel, -1, keepdims=True) * ROUTE_SCALE
    n_assign = t * TOP_K
    e_flat = eidx.reshape(n_assign).astype(jnp.int32)
    tok_flat = jnp.repeat(jnp.arange(t, dtype=jnp.int32), TOP_K)
    w_flat = wsel.reshape(n_assign)
    order = jnp.argsort(e_flat)
    e_s = e_flat[order]
    counts = jnp.bincount(e_flat, length=N_EXPERTS)
    start = jnp.cumsum(counts) - counts
    pcounts = (counts + MOE_BLOCK - 1) // MOE_BLOCK * MOE_BLOCK
    pend = jnp.cumsum(pcounts)
    pstart = pend - pcounts
    dest = pstart[e_s] + jnp.arange(n_assign) - start[e_s]
    n_blocks = (n_assign + N_EXPERTS * (MOE_BLOCK - 1) + MOE_BLOCK - 1) // MOE_BLOCK
    n_slots = n_blocks * MOE_BLOCK
    buf_tok = jnp.zeros((n_slots,), jnp.int32).at[dest].set(tok_flat[order])
    buf_w = jnp.zeros((n_slots,), jnp.float32).at[dest].set(w_flat[order])
    blk_e = jnp.minimum(jnp.searchsorted(pend, jnp.arange(n_blocks) * MOE_BLOCK, side='right'), N_EXPERTS - 1)

    def expert_block(args):
        tok, e = args
        gu = x[tok] @ w_gu[e]
        return (jax.nn.silu(gu[:, :D_EXPERT]) * gu[:, D_EXPERT:]) @ w_down[e]

    out = lax.map(expert_block, (buf_tok.reshape(n_blocks, MOE_BLOCK), blk_e))
    routed = jnp.zeros_like(x).at[buf_tok].add(out.reshape(n_slots, dm) * buf_w[:, None].astype(x.dtype))
    sgu = x @ w_sgu
    shared = (jax.nn.silu(sgu[:, :D_SHARED]) * sgu[:, D_SHARED:]) @ w_sdown
    return (routed + shared).reshape(b, l, dm)

def setup_inputs(seed: int = 0) -> dict:
    key = jax.random.key(seed)
    ks = jax.random.split(key, 30)
    f32 = jnp.float32

    def nrm(i, shape, scale):
        return jax.random.normal(ks[i], shape, f32) * scale

    decay_base = jnp.log(2.0 ** (5.0 + jnp.arange(H_A, dtype=f32)) - 1.0)
    return {
        "x_prompt": nrm(0, (BATCH, SEQ, D_MODEL), 1.0),
        "x_sample": nrm(1, (DEC_BATCH, DEC_SEQ, D_MODEL), 1.0),
        "state_ret_fwd": nrm(2, (DEC_BATCH, DEPTH, H_A, HEAD_DIM, HEAD_DIM), 0.5),
        "state_ret_bwd": nrm(3, (DEC_BATCH, DEPTH, H_A, HEAD_DIM, HEAD_DIM), 0.5),
        "cache_win_k": nrm(4, (DEC_BATCH, DEPTH, KV_B, PAST_LEN, HEAD_DIM), 1.0),
        "cache_win_v": nrm(5, (DEC_BATCH, DEPTH, KV_B, PAST_LEN, HEAD_DIM), 1.0),
        "cache_na_k": nrm(6, (DEC_BATCH, DEPTH, H_C, PAST_LEN, HEAD_DIM), 1.0),
        "cache_na_v": nrm(7, (DEC_BATCH, DEPTH, H_C, PAST_LEN, HEAD_DIM), 1.0),
        "c": nrm(8, (DEC_BATCH, D_MODEL), 1.0),
        "c_ctx": nrm(9, (D_MODEL,), 1.0),
        "w_in": nrm(10, (DEPTH, D_MODEL, IN_WIDTH), D_MODEL ** -0.5),
        "w_out": nrm(11, (DEPTH, MIX_WIDTH, D_MODEL), MIX_WIDTH ** -0.5 * BETA),
        "ret_decay_fwd": decay_base + nrm(12, (DEPTH, H_A), 0.1),
        "ret_decay_bwd": decay_base + nrm(13, (DEPTH, H_A), 0.1),
        "ret_gn_g": 1.0 + nrm(14, (DEPTH, W_A), 0.02),
        "ret_gn_b": nrm(15, (DEPTH, W_A), 0.02),
        "win_sink": nrm(16, (DEPTH, H_B), 0.5),
        "na_rpb": nrm(17, (DEPTH, H_C, 2 * NA_ROWS - 1, 2 * NA_COLS - 1), 0.1),
        "w_mod": nrm(18, (DEPTH, D_MODEL, 6 * D_MODEL), 0.5 * D_MODEL ** -0.5),
        "b_mod": nrm(19, (DEPTH, 6 * D_MODEL), 0.02),
        "ln1_g": 1.0 + nrm(20, (DEPTH, D_MODEL), 0.02),
        "ln1_b": nrm(21, (DEPTH, D_MODEL), 0.02),
        "ln2_g": 1.0 + nrm(22, (DEPTH, D_MODEL), 0.02),
        "ln2_b": nrm(23, (DEPTH, D_MODEL), 0.02),
        "w_router": nrm(24, (DEPTH, D_MODEL, N_EXPERTS), D_MODEL ** -0.5),
        "b_router": nrm(25, (DEPTH, N_EXPERTS), 0.01),
        "w_expert_gu": nrm(26, (DEPTH, N_EXPERTS, D_MODEL, 2 * D_EXPERT), D_MODEL ** -0.5),
        "w_expert_down": nrm(27, (DEPTH, N_EXPERTS, D_EXPERT, D_MODEL), D_EXPERT ** -0.5 * BETA),
        "w_shared_gu": nrm(28, (DEPTH, D_MODEL, 2 * D_SHARED), D_MODEL ** -0.5),
        "w_shared_down": nrm(29, (DEPTH, D_SHARED, D_MODEL), D_SHARED ** -0.5 * BETA),
    }

def reference(x_prompt, x_sample, state_ret_fwd, state_ret_bwd, cache_win_k, cache_win_v,
              cache_na_k, cache_na_v, c, c_ctx, w_in, w_out, ret_decay_fwd, ret_decay_bwd,
              ret_gn_g, ret_gn_b, win_sink, na_rpb, w_mod, b_mod, ln1_g, ln1_b, ln2_g, ln2_b,
              w_router, b_router, w_expert_gu, w_expert_down, w_shared_gu, w_shared_down):
    xp = x_prompt
    sf_l, sb_l, kb_l, vb_l, kc_l, vc_l = [], [], [], [], [], []
    for l in range(DEPTH):
        sh1, sc1, g1, sh2, sc2, g2 = ada_params(c_ctx[None, :], w_mod[l], b_mod[l])
        y, st_f, st_b, kb_h, vb_h, kc_h, vc_h = mixer_context(
            xp * (1.0 + sc1) + sh1, w_in[l], w_out[l], ret_decay_fwd[l], ret_decay_bwd[l],
            ret_gn_g[l], ret_gn_b[l], win_sink[l])
        xp = layer_norm(ALPHA * xp + g1 * y, ln1_g[l], ln1_b[l])
        f = moe_ffn(xp * (1.0 + sc2) + sh2, w_router[l], b_router[l], w_expert_gu[l],
                    w_expert_down[l], w_shared_gu[l], w_shared_down[l])
        xp = layer_norm(ALPHA * xp + g2 * f, ln2_g[l], ln2_b[l])
        sf_l.append(st_f); sb_l.append(st_b)
        kb_l.append(kb_h); vb_l.append(vb_h); kc_l.append(kc_h); vc_l.append(vc_h)
    new_state_ret_fwd = jnp.stack(sf_l, axis=1)
    new_state_ret_bwd = jnp.stack(sb_l, axis=1)
    new_cache_win_k = jnp.stack(kb_l, axis=1)
    new_cache_win_v = jnp.stack(vb_l, axis=1)
    new_cache_na_k = jnp.stack(kc_l, axis=1)
    new_cache_na_v = jnp.stack(vc_l, axis=1)

    xs = x_sample
    for l in range(DEPTH):
        sh1, sc1, g1, sh2, sc2, g2 = ada_params(c, w_mod[l], b_mod[l])
        y = mixer_latent(xs * (1.0 + sc1) + sh1, state_ret_fwd[:, l], state_ret_bwd[:, l],
                         cache_win_k[:, l], cache_win_v[:, l], cache_na_k[:, l], cache_na_v[:, l],
                         w_in[l], w_out[l], ret_decay_fwd[l], ret_decay_bwd[l],
                         ret_gn_g[l], ret_gn_b[l], win_sink[l], na_rpb[l])
        xs = layer_norm(ALPHA * xs + g1 * y, ln1_g[l], ln1_b[l])
        f = moe_ffn(xs * (1.0 + sc2) + sh2, w_router[l], b_router[l], w_expert_gu[l],
                    w_expert_down[l], w_shared_gu[l], w_shared_down[l])
        xs = layer_norm(ALPHA * xs + g2 * f, ln2_g[l], ln2_b[l])

    return (xp, xs, new_state_ret_fwd, new_state_ret_bwd, new_cache_win_k, new_cache_win_v,
            new_cache_na_k, new_cache_na_v)


_drawn_inputs = setup_inputs


def setup_inputs(seed=0):
    import zlib

    import numpy as np

    out = dict(_drawn_inputs(seed))
    spreads = {}
    factors = {'state_ret_fwd': 5.096,
     'state_ret_bwd': 5.39,
     'cache_win_k': 6.72,
     'cache_win_v': 5.478,
     'cache_na_k': 4.463,
     'cache_na_v': 3.993,
     'ret_gn_g': 32.471,
     'ret_gn_b': 36.366,
     'win_sink': 57.746,
     'na_rpb': 64.0}
    for name, (base, spread) in spreads.items():
        noise = np.random.default_rng([zlib.crc32(name.encode()), seed]).standard_normal(out[name].shape)
        drawn = base * np.exp(spread * noise) if base else spread * noise
        out[name] = __import__('jax').numpy.asarray(drawn.astype(out[name].dtype))
    for name, factor in factors.items():
        out[name] = (out[name] * factor).astype(out[name].dtype)
    return out
```

```python
import numpy as np
import concourse.bass as bass
from concourse import mybir
from contextlib import ExitStack

F32 = mybir.dt.float32
I32 = mybir.dt.int32
ALU = mybir.AluOpType
ACT = mybir.ActivationFunctionType
AX = mybir.AxisListType

P = 128
DM = 1024
KD = DM // P
DEPTH = 2
TILES = 3
TOK = TILES * P
HD = 64
CH = 512
W_IN = 2816
QA, KA, VA, GA, QB, KB, VB, QC, KC, VC = 0, 256, 512, 768, 1024, 1408, 1536, 1664, 2048, 2432
H_A, H_B, H_C = 4, 6, 6
SCALE = HD ** -0.5
ALPHA = float((2 * DEPTH) ** 0.25)
EPS = 1e-5
NEG = -1e30
BIG = 3.0e38
MARK = -3.0e38
E = 64
TOPK = 6
F = 256
ROUTE_SCALE = 2.5
FAR = 4096
NG = 4
ND = 2
UN = 4
MODC = 6 * DM // CH
INC = (W_IN + CH - 1) // CH
OUTC = DM // CH
CHUNKS = MODC + INC + OUTC + 1
NROW = 17
LN_ROW, SMALL_ROW = 12, 16
SINK, DEC = 64, 70

CONSTS = {}


def constants():
    p = np.arange(P)[:, None]
    j = np.arange(P)[None, :]
    parts = []

    def put(name, a):
        a = np.broadcast_to(a, (P, a.shape[1])).astype(np.float32)
        CONSTS[name] = (sum(x.shape[1] for x in parts), a.shape[1])
        parts.append(a)

    put("ident", (p == j) * 1.0)
    put("flip", (p + j == P - 1) * 1.0)
    put("before", (p < j) * 1.0)
    put("ones", np.ones((P, P)))
    put("slot", j * 1.0)
    put("band_next", np.where(j <= p, 0.0, NEG))
    put("band_prev", np.where(j >= p, 0.0, NEG))
    qc = 63 - np.arange(P)[:, None] % 64
    kc = np.arange(256)[None, :] % 64
    c0 = np.clip(qc - 8, 0, 48)
    put("na_mask", np.where((kc >= c0) & (kc < c0 + 16), 0.0, NEG))
    put("absdiff", np.abs(np.arange(3 * P)[None, :] - P - p) * 1.0)
    i = np.arange(2 * P)[None, :]
    put("from_start", i + 1.0)
    put("from_end", 2 * P - i * 1.0)
    inv = (10000.0 ** (-np.arange(16, dtype=np.float32) / 16)).astype(np.float32)
    tables = []
    for t in range(2):
        pos = np.arange(P) + P * t
        ang = np.concatenate([(pos // 64)[:, None] * inv, (pos % 64)[:, None] * inv], 1).astype(np.float32)
        tables.append((np.cos(ang), np.sin(ang)))
    put("cos", np.concatenate([tables[0][0], tables[1][0]], 1))
    put("sin", np.concatenate([tables[0][1], tables[1][1]], 1))
    put("down", P - 1.0 - p)
    put("up", p * 1.0)
    tok = p + P * np.arange(TILES)[None, :]
    put("tok", tok - 1.0 * FAR)
    put("row", tok * 6.0 - 1 - FAR)
    return np.ascontiguousarray(np.concatenate(parts, 1))


NCONST = constants().shape[1]


def psum_groups():
    names = [("mod", n) for n in range(MODC)] + [("small",), ("gn",)]
    names += [("m", 0, c, f, w) for c in range(2) for f in range(2) for w in range(2)]
    names += [("xT", 0, t, g) for t in range(TILES) for g in range(2)]
    names += [("h", n, t) for n in range(INC) for t in range(TILES)]
    names += [("qkT", b) for b in range(15)] + [("kctxT", 0), ("kctxT", 1)]
    for h in range(H_A):
        names += [("sA", h, 0), ("sA", h, 1)]
    names += [("oA", h) for h in range(H_A)] + [("state",)]
    for g in range(12 + 1):
        if g < 12:
            names += [("s", g, i) for i in range(3)]
        if g:
            names += [("pT", g - 1, i) for i in range(3)] + [("pv", g - 1)]
    names += [("yT", b) for b in range(8)]
    names += [("b", 0, r, f) for r in range(4) for f in range(2)]
    names += [("y", n, t) for n in range(OUTC) for t in range(TILES)]
    names += [("m", 1, c, f, w) for c in range(2) for f in range(2) for w in range(2)]
    names += [("b", 1, r, f) for r in range(4) for f in range(2)]
    names += [("xT", 1, t, g) for t in range(TILES) for g in range(2)]
    names += [("logit",), ("pos",)]
    names += [("sgu", t) for t in range(TILES)]
    for t in range(TILES):
        names += [("shT", t), ("sy", t, 0), ("sy", t, 1)]
    uses = [0] * 8
    out = {}
    for n, name in enumerate(names):
        out[name] = (n % 8, uses[n % 8])
        uses[n % 8] += 1
    return out, names, uses


def build(nc, a, o):
    groups, order, bank_uses = psum_groups()
    soft = [(m, t, h) for t in range(TILES) for m in "BC" for h in (0, 3)]

    with ExitStack() as ctx:
        def sb(name, cols, dt=F32, rows=P):
            return ctx.enter_context(nc.sbuf_tensor(name, [rows, cols], dt))

        scratch_x = nc.dram_tensor("scratch_x", (TOK, DM), F32, kind="Internal").ap()
        scratch_y = nc.dram_tensor("scratch_y", (TOK * TOPK, DM), F32, kind="Internal").ap()

        ring = [sb(f"ring{i}", KD * CH) for i in range(NG)]
        x = sb("x", TILES * DM)[:].rearrange("p (t d) -> p t d", t=TILES)
        cst = sb("cst", NCONST)
        xmT = sb("xmT", KD * TOK)[:].rearrange("p (k t) -> p k t", k=KD)
        rows = sb("rows", DM)
        condT = sb("condT", KD * 2)[:].rearrange("p (k c) -> p k c", c=2)
        cmisc = sb("cmisc", 512)
        A = sb("arena_a", TILES * W_IN + 15 * TOK)
        B = sb("arena_b", 12200)
        psum = [ctx.enter_context(nc.psum_tensor(f"bank{i}", [P, 512], F32)) for i in range(8)]

        def const(name):
            at, n = CONSTS[name]
            return cst[:, at:at + n]

        class Carve:
            def __init__(self, base, at=0):
                self.base, self.at = base, at

            def __call__(self, n):
                self.at += n
                assert self.at <= self.base.shape[1], self.at
                return self.base[:, self.at - n:self.at]

        c = Carve(A)
        xm = c(TILES * DM).rearrange("p (t d) -> p t d", t=TILES)
        raw, bmod, stage0, stage1 = c(DM), c(DM), c(CH), c(CH)
        stage = [stage0, stage1]
        cond = c(P)
        c = Carve(A)
        h = c(TILES * W_IN).rearrange("p (t d) -> p t d", t=TILES)
        qkT = c(15 * TOK).rearrange("p (b t) -> p b t", b=15)
        c = Carve(A, TILES * DM)
        xg = [c(DM), c(DM)]
        xgT = c(DM).rearrange("p (k t) -> p k t", k=KD)
        ys = [c(DM), c(DM)]
        hid, sgate = c(F), c(F)
        hT = c(F).rearrange("p (k t) -> p k t", k=2)
        pick = c(2 * TILES * P).rearrange("p (i t s) -> p i t s", i=2, t=TILES)
        shT = c(2 * P).rearrange("p (k t) -> p k t", k=2)
        vals = c(TILES * E * 3).rearrange("p (t e v) -> p t e v", t=TILES, e=E)
        wr = c(KD * E).rearrange("p (k e) -> p k e", k=KD)
        sg_s, hid_s = [c(F) for _ in range(TILES)], [c(F) for _ in range(2)]
        c = Carve(B)
        nab = c(H_C * 256).rearrange("p (h k) -> p h k", h=H_C)
        prob = c(3 * TOK).rearrange("p (i k) -> p i k", i=3)
        probT = c(3 * TOK).rearrange("p (i k) -> p i k", i=3)
        kctx = c(10 * HD)
        kctxT = c(5 * P).rearrange("p (b k) -> p b k", b=5)
        vctx = c(8 * HD).rearrange("p (h d) -> p h d", h=8)
        s0 = c(4 * HD).rearrange("p (r g d) -> p r g d", r=2, g=2)
        gn = c(2 * 256)
        decay_f, decay_b = c(TOK), c(TOK)
        decay = c(TOK)
        pa = c(5 * P)
        qx = c(4 * 256).rearrange("p (r g t) -> p r g t", r=2, g=2)
        kz = c(2 * 256).rearrange("p (r h d) -> p r h d", r=2, h=H_A)
        oA = c(TILES * 256).rearrange("p (t h d) -> p t h d", t=TILES, h=H_A)
        tmp = c(TILES * 256)
        ksw = c(TILES * P).rearrange("p (t d) -> p t d", t=TILES)
        stout = c(512)
        c = Carve(B)
        down = [c(2 * DM).rearrange("p (k n) -> p k n", k=2) for _ in range(ND)]
        gateb = c(2 * DM).rearrange("p (c d) -> p c d", c=2)
        lnb = c(2 * DM).rearrange("p (r d) -> p r d", r=2)
        score = c(TILES * E).rearrange("p (t e) -> p t e", t=TILES)
        sel = c(TILES * 66).rearrange("p (t e) -> p t e", t=TILES)
        sel2 = c(TILES * 66).rearrange("p (t e) -> p t e", t=TILES)
        grp = c(TILES * 12).rearrange("p (t e) -> p t e", t=TILES)
        grp2 = c(TILES * 12).rearrange("p (t e) -> p t e", t=TILES)
        top = c(24 * 8).rearrange("p (g e) -> p g e", g=24)
        top8 = c(TILES * 8).rearrange("p (t e) -> p t e", t=TILES)
        mask = c(TILES * E).rearrange("p (t e) -> p t e", t=TILES)
        posm = c(TILES * E).rearrange("p (t e) -> p t e", t=TILES)
        rank = c(TILES * E).rearrange("p (t e) -> p t e", t=TILES)
        wsum = c(8)
        counts = c(E)
        most = sb("most", 2, I32)
        slot_idx = sb("slot_idx", 2 * (E + 2), I32)[:].rearrange("p (v e) -> p v e", v=2)
        slot_w = sb("slot_w", E)
        now_idx = [sb(f"now_idx{i}", 1, I32) for i in range(4)]
        c = Carve(cmisc)
        lg, dneg, small, zeta = c(8), c(8), c(80), c(8)
        mx, neg, den, sinkx, sinke, recip = c(36), c(36), c(36), c(36), c(36), c(36)
        mean, var = c(12), c(12)
        bn, bnag, rstd = c(12), c(2), c(1)

        mod_row = {"sh1": 0, "sc1": 2, "g1": 4, "sh2": 6, "sc2": 8, "g2": 10}


        with ExitStack() as c0:
            cst_loaded, tokens_loaded, cond_loaded, cond_turned, cond_done, far_set = (
                c0.enter_context(nc.semaphore(n)) for n in
                ("cst_loaded", "tokens_loaded", "cond_loaded", "cond_turned", "cond_done", "far_set"))
            blk0 = c0.enter_context(nc.Block())

            @blk0.sync
            def _(sp):
                sp.dma_start(cst[:], a["consts"]).then_inc(cst_loaded, 16)
                sp.dma_start(x[:, 0, :], a["x_prompt"][0]).then_inc(tokens_loaded, 16)
                sp.dma_start(x[:, 1:3, :], a["x_sample"][0].rearrange("(t p) d -> p t d", p=P)).then_inc(tokens_loaded, 16)
                sp.dma_start(cond[0:KD, :], a["c_ctx"].rearrange("(k p) -> k p", p=P)).then_inc(cond_loaded, 16)
                sp.dma_start(cond[KD:2 * KD, :], a["c"][0].rearrange("(k p) -> k p", p=P)).then_inc(cond_loaded, 16)
                sp.wait_ge(cst_loaded, 16)
                sp.wait_ge(tokens_loaded, 32)

            @blk0.tensor
            def _(pe):
                pe.wait_ge(cst_loaded, 16)
                pe.wait_ge(cond_loaded, 32)
                pe.transpose(psum[0][:, 0:2 * KD], cond[0:2 * KD, :], const("ident")[0:2 * KD, 0:2 * KD]).then_inc(cond_turned, 1)

            @blk0.scalar
            def _(act):
                act.wait_ge(cond_turned, 1)
                act.activation(condT.rearrange("p k c -> p c k"), psum[0][:, 0:2 * KD].rearrange("p (c k) -> p c k", c=2),
                               ACT.Silu).then_inc(cond_done, 1)
                act.wait_ge(cond_done, 1)

            @blk0.gpsimd
            def _(pool):
                pool.memset(slot_idx[:, :, E:E + 2], FAR).then_inc(far_set, 1)
                pool.wait_ge(far_set, 1)

        with ExitStack() as lctx:
            l = lctx.enter_context(nc.Fori(0, DEPTH))

            def at_layer(name):
                return a[name][bass.ds(l, 1)]

            def of_layer(d, name):
                return d[name][0][bass.ds(l, 1)].rearrange("a h p d -> (a h) p d")

            layer_sems = []

            def sem(name):
                layer_sems.append(lctx.enter_context(nc.semaphore(name)))
                return layer_sems[-1]

            full = [sem(f"bank_full{i}") for i in range(8)]
            free = [sem(f"bank_free{i}") for i in range(8)]
            ring_ready = [sem(f"ring_ready{i}") for i in range(NG)]
            down_ready = [sem(f"down_ready{i}") for i in range(ND)]
            dve_step = sem("dve_step")
            stage_ready, stage_sent = sem("stage_ready"), [sem("stage_sent0"), sem("stage_sent1")]
            rows_loaded, bmod_loaded, rows_ready = sem("rows_loaded"), sem("bmod_loaded"), sem("rows_ready")
            xm_ready, xmT_ready = sem("xm_ready"), sem("xmT_ready")
            h_dve, h_act, rope_done, qkT_ready = sem("h_dve"), sem("h_act"), sem("rope_done"), sem("qkT_ready")
            ctx_loaded, kctxT_ready = sem("ctx_loaded"), sem("kctxT_ready")
            bias_loaded, bias_masked = sem("bias_loaded"), sem("bias_masked")
            small_ready, gn_ready = sem("small_ready"), sem("gn_ready")
            dneg_ready, softplus_ready, lg_ready = sem("dneg_ready"), sem("softplus_ready"), sem("lg_ready")
            act_step = sem("act_step")
            decay_raw, decay_cut, decay_ready = sem("decay_raw"), sem("decay_cut"), sem("decay_ready")
            pa_ready, zeta_ready, kz_ready = sem("pa_ready"), sem("zeta_ready"), sem("kz_ready")
            qx_raw, qx_ready, state_ready = sem("qx_raw"), sem("qx_ready"), sem("state_ready")
            var_ready, root_ready, gate_ready, ya_written = sem("var_ready"), sem("root_ready"), sem("gate_ready"), sem("ya_written")
            neg_ready, sinkx_ready, exp_done = sem("neg_ready"), sem("sinkx_ready"), sem("exp_done")
            probT_ready, y_written, yT_ready = sem("probT_ready"), sem("y_written"), sem("yT_ready")
            b_ready, x_ready, lvar_ready, lroot_ready = sem("b_ready"), sem("x_ready"), sem("lvar_ready"), sem("lroot_ready")
            wr_loaded, xm_saved, score_ready, mask_ready = sem("wr_loaded"), sem("xm_saved"), sem("score_ready"), sem("mask_ready")
            most_ready, vals_ready, xg_zeroed = sem("most_ready"), sem("vals_ready"), sem("xg_zeroed")
            ssilu_done, shid_ready, shT_ready = sem("ssilu_done"), sem("shid_ready"), sem("shT_ready")
            caches_stored, states_stored, experts_done = sem("caches_stored"), sem("states_stored"), sem("experts_done")
            back = [sem("rows_back0"), sem("rows_back1")]
            idx_seen = sem("idx_seen")

            def pass_sems(tag):
                return {n: sem(f"{n}_{tag}") for n in
                        ("pick_ready", "pick_used", "slots_ready", "gathered0", "gathered1", "xT_full", "xT_ready",
                         "gu_full", "silu_done", "hid_ready", "hT_full", "hT_ready", "y_full", "ys_ready",
                         "scattered0", "scattered1", "ring_in0", "ring_in1", "ring_in2", "ring_in3", "down_in0",
                         "down_in1", "idx_set", "ys_free", "pass_done")}

            MAIN, OVER = pass_sems("main"), pass_sems("over")
            for i in range(NG):
                MAIN[f"ring_in{i}"] = ring_ready[i]
            for i in range(ND):
                MAIN[f"down_in{i}"] = down_ready[i]
            bctx = ExitStack()
            blk = bctx.enter_context(nc.Block())

            def done(eng, name):
                b, n = groups[name]
                eng.wait_ge(full[b], n + 1)
                return psum[b]

            def give(ins, name):
                ins.then_inc(free[groups[name][0]], 1)

            HG = [(n, t) for n in range(INC) for t in range(TILES)]
            h_on_act = sum(i % 2 for i in range(len(HG)))
            h_on_dve = len(HG) - h_on_act
            soft_of = {g: s for g, s in enumerate(soft)}
            last_c1 = max(g for g, s in enumerate(soft) if s[:2] == ("C", 1))
            ring_base = [(CHUNKS - i + NG - 1) // NG for i in range(NG)]
            down_base = [1, 0]

            def ring_view(i):
                return ring[i][:].rearrange("p (k n) -> p k n", k=KD)

            @blk.sync
            def _(sp):
                last_use = ([("mod", i) for i in range(MODC)] + [("h", i, 2) for i in range(INC)] +
                            [("y", i, 2) for i in range(OUTC)] + [("sgu", 2)])

                def load_chunk(n, src, w=CH):
                    s = n % NG
                    if n >= NG:
                        done(sp, last_use[n - NG])
                    sp.dma_start(ring_view(s)[:, :, 0:w], src).then_inc(ring_ready[s], 16)

                def chunks(name):
                    return at_layer(name).rearrange("a (k p) n -> p (a k) n", p=P)

                for i in range(MODC):
                    load_chunk(i, chunks("w_mod")[:, :, CH * i:CH * i + CH])
                    if i == 1:
                        bm = at_layer("b_mod").rearrange("a (r d) -> (a r) d", r=6)
                        for c_ in range(2):
                            sp.dma_start(bmod[c_:12:2, :], bm).then_inc(bmod_loaded, 16)
                        for r, name in enumerate(("ln1_g", "ln1_b", "ln2_g", "ln2_b")):
                            sp.dma_start(rows[LN_ROW + r:LN_ROW + r + 1, :], at_layer(name)).then_inc(rows_loaded, 16)
                        at = 0
                        for name, w in (("ret_gn_g", 256), ("ret_gn_b", 256), ("b_router", E), ("win_sink", H_B),
                                        ("ret_decay_fwd", H_A), ("ret_decay_bwd", H_A)):
                            sp.dma_start(rows[SMALL_ROW:SMALL_ROW + 1, at:at + w], at_layer(name)).then_inc(rows_loaded, 16)
                            at += w
                    if i == 5:
                        kv = kctx.rearrange("p (h d) -> p h d", d=HD)
                        wk, nk = of_layer(a, "cache_win_k"), of_layer(a, "cache_na_k")
                        sp.dma_start(kv[:, 0:2, :], wk.rearrange("h p d -> p h d")).then_inc(ctx_loaded, 16)
                        sp.dma_start(kv[:, 2, :], wk[1]).then_inc(ctx_loaded, 16)
                        sp.dma_start(kv[:, 3, :], wk[0]).then_inc(ctx_loaded, 16)
                        sp.dma_start(kv[:, 4:10, :], nk.rearrange("h p d -> p h d")).then_inc(ctx_loaded, 16)
                        sp.dma_start(vctx[:, 0:2, :], of_layer(a, "cache_win_v").rearrange("h p d -> p h d")).then_inc(ctx_loaded, 16)
                        sp.dma_start(vctx[:, 2:8, :], of_layer(a, "cache_na_v").rearrange("h p d -> p h d")).then_inc(ctx_loaded, 16)
                        for r, name in enumerate(("state_ret_fwd", "state_ret_bwd")):
                            st = of_layer(a, name)
                            for g in range(2):
                                sp.dma_start(s0[:, r, g, :], st[2 * g:2 * g + 2].rearrange("h d e -> (h d) e")).then_inc(ctx_loaded, 16)

                def load_bias(t):
                    rp = at_layer("na_rpb")
                    for rr in range(2):
                        r = 2 * t + 1 - rr
                        for hh in range(H_C):
                            src = bass.AP(rp.tensor, rp.offset + (hh * 15 * 31 + (7 - r) * 31 + 15 - 63), [[1, 64], [31, 4], [1, 64]])
                            sp.dma_start(nab[64 * rr:64 * rr + 64, hh, :].rearrange("p (r c) -> p r c", r=4), src).then_inc(bias_loaded, 16)

                load_bias(0)
                for i in range(INC):
                    w = min(CH, W_IN - CH * i)
                    load_chunk(MODC + i, chunks("w_in")[:, :, CH * i:CH * i + w], w)
                for i in range(OUTC):
                    load_chunk(MODC + INC + i, chunks("w_out")[:, :, CH * i:CH * i + CH])
                sp.wait_ge(h_dve, h_on_dve)
                sp.wait_ge(h_act, h_on_act)
                for name, col, nh in (("new_win_k", KB, 2), ("new_win_v", VB, 2), ("new_na_k", KC, 6), ("new_na_v", VC, 6)):
                    sp.dma_start(of_layer(o, name).rearrange("h p d -> p h d"),
                                 h[:, 0, col:col + nh * HD].rearrange("p (h d) -> p h d", d=HD)).then_inc(caches_stored, 16)
                sp.wait_ge(state_ready, 1)
                for r, name in enumerate(("new_fwd", "new_bwd")):
                    sp.dma_start(of_layer(o, name).rearrange("h d e -> d h e"),
                                 stout[0:64, 256 * r:256 * r + 256].rearrange("p (h e) -> p h e", h=H_A)).then_inc(states_stored, 16)
                done(sp, ("s", last_c1, 2))
                load_bias(1)
                load_chunk(CHUNKS - 1, chunks("w_shared_gu"))
                sp.wait_ge(yT_ready, 8)
                sp.wait_ge(caches_stored, 64)
                sp.wait_ge(states_stored, 32)
                sp.dma_start(down[0], at_layer("w_shared_down").rearrange("a (k p) n -> p (a k) n", p=P)).then_inc(down_ready[0], 16)
                sp.dma_start(wr, at_layer("w_router").rearrange("a (k p) e -> p (a k) e", p=P)).then_inc(wr_loaded, 16)

                def expert_loads(S, q):
                    gu_v, dn_v = at_layer("w_expert_gu"), at_layer("w_expert_down")
                    b = q * E

                    def gu(i, e):
                        sp.dma_start(ring_view(i), gu_v[:, bass.ds(e, 1)].rearrange("a b (k p) n -> p (a b k) n", p=P)
                                     ).then_inc(S[f"ring_in{i}"], 16)

                    def dn(i, e):
                        sp.dma_start(down[i], dn_v[:, bass.ds(e, 1)].rearrange("a b (k p) n -> p (a b k) n", p=P)
                                     ).then_inc(S[f"down_in{i}"], 16)

                    for e in (1, 2, 3, 0):
                        if S is MAIN:
                            done(sp, last_use[max(n for n in range(CHUNKS) if n % NG == e)])
                        gu(e, e)
                        if e < ND:
                            if S is MAIN and e == 0:
                                done(sp, ("sy", 2, 1))
                            dn(e, e)
                    with sp.Fori(1, E // UN) as it:
                        for i in range(UN):
                            sp.wait_ge(S["gu_full"], it * UN + (b + i - NG + 1))
                            gu(i, it * UN + i)
                            sp.wait_ge(S["y_full"], it * UN + (b + i - NG + 1))
                            dn(i % ND, it * UN + (i - 2))
                    for e in (E - 2, E - 1):
                        sp.wait_ge(S["y_full"], b + e - 1)
                        dn(e % ND, e)

                sp.wait_ge(xm_ready, 2)
                sp.dma_start(scratch_x.rearrange("(t p) d -> p t d", p=P), xm).then_inc(xm_saved, 16)
                expert_loads(MAIN, 0)
                sp.wait_ge(most_ready, 1)
                with sp.If(sp.value_load(most[0:1, 0:1], min_val=0, max_val=TOK) > P):
                    sp.wait_ge(MAIN["pass_done"], 1)
                    expert_loads(OVER, 0)
                    sp.wait_ge(OVER["pass_done"], 1)
                    expert_loads(OVER, 1)
                    sp.nop()
                sp.wait_ge(experts_done, 1)
                for t in range(TILES):
                    if t == 2:
                        sp.wait_ge(x_ready, 4)
                    src = scratch_y.rearrange("(t p k) d -> t p k d", p=P, k=TOPK)[t]
                    s = 2 * (t % 2)
                    sp.dma_start(ring[s][:].rearrange("p (k d) -> p k d", d=DM), src[:, 0:4, :]).then_inc(back[t % 2], 16)
                    sp.dma_start(ring[s + 1][:].rearrange("p (k d) -> p k d", d=DM)[:, 0:2, :], src[:, 4:6, :]).then_inc(back[t % 2], 16)
                for s in range(2):
                    sp.wait_ge(back[s], 64 - 32 * s)

            @blk.tensor
            def _(pe):
                turn = iter(order)
                ident, flip, ones, before = const("ident"), const("flip"), const("ones"), const("before")

                def begin(name):
                    assert next(turn) == name, name
                    b, n = groups[name]
                    if n > 0:
                        pe.wait_ge(free[b], n)
                    return psum[b]

                def end(ins, name):
                    ins.then_inc(full[groups[name][0]], 1)

                def chunk(n):
                    pe.wait_ge(ring_ready[n % NG], 16 * (n // NG + 1))
                    return ring_view(n % NG)

                def spread(name, row, c0, n, k=16):
                    bank = begin(name)
                    end(pe.matmul(bank[:, 0:n], ident[0:k, row:row + 1].to_broadcast([k, P]), rows[0:k, c0:c0 + n],
                                  start=True, stop=True), name)

                def spread_mod(which):
                    sc, sh = (mod_row["sc1"], mod_row["sh1"]) if which == 0 else (mod_row["sc2"], mod_row["sh2"])
                    for c_ in range(2):
                        for f in range(2):
                            spread(("m", which, c_, f, 0), sc + c_, CH * f, CH)
                            spread(("m", which, c_, f, 1), sh + c_, CH * f, CH)

                def spread_norm(which):
                    g = mod_row["g1"] if which == 0 else mod_row["g2"]
                    for r, row in enumerate((g, g + 1, LN_ROW + 2 * which, LN_ROW + 2 * which + 1)):
                        for f in range(2):
                            spread(("b", which, r, f), row, CH * f, CH)

                def turn_x(which):
                    for t in range(TILES):
                        for g in range(2):
                            name = ("xT", which, t, g)
                            bank = begin(name)
                            for k in range(4):
                                ins = pe.transpose(bank[:, P * k:P * k + P], xm[:, t, P * (4 * g + k):P * (4 * g + k + 1)], ident)
                            end(ins, name)

                for n in range(MODC):
                    w = chunk(n)
                    bank = begin(("mod", n))
                    for k in range(KD):
                        ins = pe.matmul(bank[0:2, :], condT[:, k, :], w[:, k, :], start=(k == 0), stop=(k == KD - 1))
                    end(ins, ("mod", n))
                pe.wait_ge(rows_ready, 1)
                pe.wait_ge(rows_loaded, 160)
                spread(("small",), SMALL_ROW, 512, E + 14, 17)
                spread(("gn",), SMALL_ROW, 0, 512, 17)
                spread_mod(0)
                pe.wait_ge(xm_ready, 1)
                turn_x(0)
                pe.wait_ge(xmT_ready, 6)
                for n, t in HG:
                    w = chunk(MODC + n)
                    cols = min(CH, W_IN - CH * n)
                    bank = begin(("h", n, t))
                    for k in range(KD):
                        ins = pe.matmul(bank[:, 0:cols], xmT[:, k, P * t:P * t + P], w[:, k, 0:cols],
                                        start=(k == 0), stop=(k == KD - 1))
                    end(ins, ("h", n, t))
                pe.wait_ge(rope_done, 1)
                pe.wait_ge(h_act, h_on_act)
                qk_cols = [QA, QA + P, KA, KA + P, QB, QB + P, QB + 2 * P, KB, None, QC, QC + P, QC + 2 * P, KC, KC + P, KC + 2 * P]
                for b, col in enumerate(qk_cols):
                    bank = begin(("qkT", b))
                    for t in range(TILES):
                        src = ksw[:, t, :] if col is None else h[:, t, col:col + P]
                        ins = pe.transpose(bank[:, P * t:P * t + P], src, ident)
                    end(ins, ("qkT", b))
                pe.wait_ge(ctx_loaded, 160)
                for g, blocks in enumerate((range(4), range(4, 5))):
                    bank = begin(("kctxT", g))
                    for i, b in enumerate(blocks):
                        ins = pe.transpose(bank[:, P * i:P * i + P], kctx[:, P * b:P * b + P], ident)
                    end(ins, ("kctxT", g))
                pe.wait_ge(qkT_ready, 15)
                pe.wait_ge(kctxT_ready, 2)
                for hh in range(H_A):
                    p0, g = 64 * (hh % 2), hh // 2
                    q, k = qkT[p0:p0 + 64, g, :], qkT[p0:p0 + 64, 2 + g, :]
                    bank = begin(("sA", hh, 0))
                    pe.matmul(bank[:, 0:P], k[:, 0:P], q[:, 0:P], start=True, stop=True)
                    end(pe.matmul(bank[:, P:3 * P], k[:, P:2 * P], q[:, P:3 * P], start=True, stop=True), ("sA", hh, 0))
                    bank = begin(("sA", hh, 1))
                    end(pe.matmul(bank[:, 0:2 * P], k[:, 2 * P:3 * P], q[:, P:3 * P], start=True, stop=True), ("sA", hh, 1))
                for hh in range(H_A):
                    p0, g = 64 * (hh % 2), hh // 2
                    va = [h[:, t, VA + HD * hh:VA + HD * hh + HD] for t in range(TILES)]
                    bank = begin(("oA", hh))
                    pe.wait_ge(pa_ready, hh + 1)
                    pe.matmul(bank[:, 0:HD], pa[:, 0:P], va[0], start=True, stop=True)
                    pe.wait_ge(qx_ready, 1)
                    for t in (1, 2):
                        out = bank[:, HD * t:HD * t + HD]
                        pe.matmul(out, pa[:, P * t:P * t + P], va[1], start=True, stop=False)
                        pe.matmul(out, pa[:, P * (t + 2):P * (t + 2) + P], va[2], start=False, stop=False)
                        for r in range(2):
                            ins = pe.matmul(out, qx[p0:p0 + 64, r, g, P * (t - 1):P * t], s0[p0:p0 + 64, r, g, :],
                                            start=False, stop=(r == 1))
                    end(ins, ("oA", hh))
                bank = begin(("state",))
                pe.wait_ge(kz_ready, 1)
                for r in range(2):
                    for hh in range(H_A):
                        ins = pe.matmul(bank[0:64, HD * (4 * r + hh):HD * (4 * r + hh + 1)], kz[:, r, hh, :],
                                        h[:, 0, VA + HD * hh:VA + HD * hh + HD], start=True, stop=True)
                end(ins, ("state",))

                def scores(g):
                    m, t, h0 = soft[g]
                    if m == "C" and t > 0:
                        pe.wait_ge(bias_masked, t)
                    for i in range(3):
                        hh = h0 + i
                        p0 = 64 * (hh % 2)
                        if m == "B":
                            same = hh // 3 == hh % 2
                            qb, kb, cb = 4 + hh // 2, 7 if same else 8, 0 if same else 1
                        else:
                            qb, kb, cb = 9 + hh // 2, 12 + hh // 2, 2 + hh // 2
                        q = qkT[p0:p0 + 64, qb, P * t:P * t + P]
                        k = qkT[p0:p0 + 64, kb, :]
                        bank = begin(("s", g, i))
                        if t == 0:
                            end(pe.matmul(bank[:, 0:P], q, k[:, 0:P], start=True, stop=True), ("s", g, i))
                            continue
                        if m == "B":
                            for j in (0, 1):
                                masked = j == (t == 1)
                                out = bank[:, P * j:P * j + P]
                                pe.matmul(out, q, k[:, P * (j + 1):P * (j + 2)], start=True, stop=not masked)
                                if masked:
                                    pe.matmul(out, ident, const("band_next" if t == 1 else "band_prev"), start=False, stop=True)
                        else:
                            pe.matmul(bank[:, 0:2 * P], q, k[:, P:3 * P], start=True, stop=False)
                            pe.matmul(bank[:, 0:2 * P], flip, nab[:, hh, :], start=False, stop=True)
                        end(pe.matmul(bank[:, 2 * P:3 * P], q, kctxT[p0:p0 + 64, cb, :], start=True, stop=True), ("s", g, i))

                def mix(g):
                    m, t, h0 = soft[g]
                    nb = 1 if t == 0 else 3
                    pe.wait_ge(exp_done, g + 1)
                    for i in range(3):
                        bank = begin(("pT", g, i))
                        for j in range(nb):
                            ins = pe.transpose(bank[:, P * j:P * j + P], prob[:, i, P * j:P * j + P], ident)
                        end(ins, ("pT", g, i))
                    bank = begin(("pv", g))
                    for i in range(3):
                        hh = h0 + i
                        pe.wait_ge(probT_ready, 3 * g + i + 1)
                        for j in range(nb):
                            if j == 2:
                                v = vctx[:, hh // 3 if m == "B" else 2 + hh, :]
                            else:
                                col = VB + HD * (hh // 3) if m == "B" else VC + HD * hh
                                v = h[:, t if t == 0 else j + 1, col:col + HD]
                            ins = pe.matmul(bank[:, HD * i:HD * i + HD], probT[:, i, P * j:P * j + P], v,
                                            start=(j == 0), stop=(j == nb - 1))
                    end(ins, ("pv", g))

                for g in range(len(soft) + 1):
                    if g < len(soft):
                        scores(g)
                    if g:
                        mix(g - 1)
                pe.wait_ge(y_written, len(soft))
                pe.wait_ge(ya_written, 1)
                y_cols = [QA, QA + P, QB, QB + P, QB + 2 * P, QC, QC + P, QC + 2 * P]
                for b, col in enumerate(y_cols):
                    bank = begin(("yT", b))
                    for t in range(TILES):
                        ins = pe.transpose(bank[:, P * t:P * t + P], h[:, t, col:col + P], ident)
                    end(ins, ("yT", b))
                spread_norm(0)
                pe.wait_ge(yT_ready, 8)
                for n in range(OUTC):
                    for t in range(TILES):
                        w = chunk(MODC + INC + n)
                        bank = begin(("y", n, t))
                        for k in range(KD):
                            ins = pe.matmul(bank[:, :], xmT[:, k, P * t:P * t + P], w[:, k, :], start=(k == 0), stop=(k == KD - 1))
                        end(ins, ("y", n, t))
                spread_mod(1)
                spread_norm(1)
                pe.wait_ge(xm_ready, 2)
                turn_x(1)
                pe.wait_ge(xmT_ready, 12)
                pe.wait_ge(wr_loaded, 16)
                bank = begin(("logit",))
                for t in range(TILES):
                    for k in range(KD):
                        ins = pe.matmul(bank[:, E * t:E * t + E], xmT[:, k, P * t:P * t + P], wr[:, k, :],
                                        start=(k == 0), stop=(k == KD - 1))
                end(ins, ("logit",))
                pe.wait_ge(mask_ready, 1)
                bank = begin(("pos",))
                for t in range(TILES):
                    for s in range(t + 1):
                        ins = pe.matmul(bank[:, E * t:E * t + E], ones if s < t else before, mask[:, s, :],
                                        start=(s == 0), stop=(s == t))
                for s in range(TILES):
                    ins = pe.matmul(bank[:, E * TILES:E * TILES + E], ones, mask[:, s, :], start=(s == 0), stop=(s == TILES - 1))
                end(ins, ("pos",))
                w = chunk(CHUNKS - 1)
                for t in range(TILES):
                    bank = begin(("sgu", t))
                    for k in range(KD):
                        ins = pe.matmul(bank[:, :], xmT[:, k, P * t:P * t + P], w[:, k, :], start=(k == 0), stop=(k == KD - 1))
                    end(ins, ("sgu", t))
                pe.wait_ge(down_ready[0], 16)
                for t in range(TILES):
                    pe.wait_ge(shid_ready, t + 1)
                    bank = begin(("shT", t))
                    for k in range(2):
                        ins = pe.transpose(bank[:, P * k:P * k + P], hid_s[t % 2][:, P * k:P * k + P], ident)
                    end(ins, ("shT", t))
                    pe.wait_ge(shT_ready, t + 1)
                    for f in range(2):
                        bank = begin(("sy", t, f))
                        for k in range(2):
                            ins = pe.matmul(bank[:, :], shT[:, k, :], down[0][:, k, CH * f:CH * f + CH], start=(k == 0), stop=(k == 1))
                        end(ins, ("sy", t, f))
                assert next(turn, None) is None
                for b in range(8):
                    pe.wait_ge(free[b], bank_uses[b])

                def expert_pass(S, q):
                    b, bx = q * E, q * (E + 1)
                    if q:
                        pe.wait_ge(S["slots_ready"], q)
                    with pe.Fori(0, E // UN) as it:
                        for i in range(UN):
                            e = it * UN + i
                            pe.wait_ge(S["pick_ready"], e + (b + 1))
                            for t in range(TILES):
                                ins = pe.matmul(psum[7][:, bass.ds(e * 3, 3)], pick[:, i % 2, t, :],
                                                vals[:, t, bass.ds(e, 1), :], start=(t == 0), stop=(t == TILES - 1))
                            ins.then_inc(S["pick_used"], 1)

                    def turn_rows(m, half, i):
                        pe.wait_ge(S[f"gathered{i % 2}"], (half + (q * 33 + 1)) * 16)
                        pe.wait_ge(S["xT_ready"], m + (bx + 1))
                        for k in range(KD):
                            ins = pe.transpose(psum[2 + k // 4][:, P * (k % 4):P * (k % 4) + P], xg[i % 2][:, P * k:P * k + P], ident)
                        ins.then_inc(S["xT_full"], 1)

                    turn_rows(0, 0, 0)
                    with pe.Fori(0, E // UN) as it:
                        for i in range(UN):
                            e = it * UN + i
                            pe.wait_ge(S["xT_ready"], e + (bx + 2))
                            pe.wait_ge(S["hid_ready"], e + (b + 1))
                            pe.wait_ge(S[f"ring_in{i}"], (it + ((ring_base[i] if S is MAIN else 0) + q * (E // NG) + 1)) * 16)
                            for k in range(KD):
                                ins = pe.matmul(psum[i % 2][:, :], xgT[:, k, :], ring_view(i)[:, k, :], start=(k == 0), stop=(k == KD - 1))
                            ins.then_inc(S["gu_full"], 1)
                            turn_rows(e + 1, it * 2 + (i + 1) // 2, i + 1)
                            pe.wait_ge(S["hid_ready"], e + (b + 3))
                            pe.wait_ge(S["hT_ready"], e + (b + 1))
                            for k in range(2):
                                ins = pe.transpose(psum[4][:, P * k:P * k + P], hid[:, P * k:P * k + P], ident)
                            ins.then_inc(S["hT_full"], 1)
                            pe.wait_ge(S["hT_ready"], e + (b + 2))
                            pe.wait_ge(S["ys_ready"], e + (b + 1))
                            pe.wait_ge(S[f"down_in{i % ND}"], (it * 2 + (i // 2 + (down_base[i % ND] if S is MAIN else 0) + q * (E // ND) + 1)) * 16)
                            for f in range(2):
                                for k in range(2):
                                    ins = pe.matmul(psum[5 + f][:, :], hT[:, k, :], down[i % ND][:, k, CH * f:CH * f + CH],
                                                    start=(k == 0), stop=(k == 1))
                            ins.then_inc(S["y_full"], 1)

                expert_pass(MAIN, 0)
                pe.wait_ge(most_ready, 1)
                with pe.If(pe.value_load(most[0:1, 0:1], min_val=0, max_val=TOK) > P):
                    expert_pass(OVER, 0)
                    expert_pass(OVER, 1)
                    pe.nop()

            @blk.vector
            def _(dve):
                steps = [0]

                def link(ins):
                    steps[0] += 1
                    ins.then_inc(dve_step, 1)
                    dve.wait_ge(dve_step, steps[0])

                for n in range(MODC):
                    bank = done(dve, ("mod", n))
                    if n >= 2:
                        dve.wait_ge(stage_sent[n % 2], 16 * (n // 2))
                    dve.tensor_copy(stage[n % 2][0:2, :], bank[0:2, :]).then_inc(stage_ready, 1)
                    dve.wait_ge(stage_ready, n + 1)
                    dve.sem_inc(free[groups[("mod", n)][0]], 1)
                dve.wait_ge(bmod_loaded, 32)
                for s in range(2):
                    dve.wait_ge(stage_sent[s], 16 * MODC // 2)
                dve.tensor_tensor(rows[0:12, :], raw[0:12, :], bmod[0:12, :], ALU.add).then_inc(rows_ready, 1)
                bank = done(dve, ("small",))
                link(dve.tensor_copy(small[:, 0:E + 14], bank[:, 0:E + 14]))
                dve.sem_inc(free[groups[("small",)][0]], 1)
                dec = small[:, DEC:DEC + 8]
                link(dve.tensor_scalar(dneg, dec, -1.0, None, ALU.mult))
                dve.tensor_tensor(dneg, dneg, dec, ALU.min).then_inc(dneg_ready, 1)
                dve.wait_ge(softplus_ready, 1)
                link(dve.tensor_scalar(zeta, dec, 0.0, None, ALU.min))
                dve.tensor_tensor(lg, zeta, lg, ALU.subtract).then_inc(lg_ready, 1)

                def modulate(which):
                    for c_ in range(2):
                        for f in range(2):
                            bank = done(dve, ("m", which, c_, f, 0))
                            cols = slice(CH * f, CH * f + CH)
                            tiles = (0,) if c_ == 0 else (1, 2)
                            for t in tiles:
                                ins = dve.scalar_tensor_tensor(out=xm[:, t, cols], in0=bank[:, :], scalar=1.0, in1=x[:, t, cols],
                                                               op0=ALU.add, op1=ALU.mult)
                            give(ins, ("m", which, c_, f, 0))
                            bank = done(dve, ("m", which, c_, f, 1))
                            dve.wait_ge(free[groups[("m", which, c_, f, 0)][0]], groups[("m", which, c_, f, 0)][1] + 1)
                            for t in tiles:
                                ins = dve.tensor_tensor(xm[:, t, cols], xm[:, t, cols], bank[:, :], ALU.add)
                            give(ins, ("m", which, c_, f, 1))
                    name = ("m", which, 1, 1, 1)
                    dve.wait_ge(free[groups[name][0]], groups[name][1] + 1)
                    dve.sem_inc(xm_ready, 1)

                modulate(0)
                for i, (n, t) in enumerate(HG):
                    if i % 2 == 0:
                        cols = min(CH, W_IN - CH * n)
                        bank = done(dve, ("h", n, t))
                        give(dve.tensor_copy(h[:, t, CH * n:CH * n + cols], bank[:, 0:cols]), ("h", n, t))
                        dve.wait_ge(free[groups[("h", n, t)][0]], groups[("h", n, t)][1] + 1)
                        dve.sem_inc(h_dve, 1)
                dve.wait_ge(h_act, h_on_act)
                rt = prob.rearrange("p i k -> p (i k)")
                r1, r2, r3, r4 = (rt[:, 256 * i:256 * i + 256].rearrange("p (h d) -> p h d", h=8) for i in range(4))
                for t in (1, 2):
                    v = h[:, t, QB:QB + 512].rearrange("p (h s d) -> p h s d", h=8, s=2)
                    x1, x2 = v[:, :, 0, :], v[:, :, 1, :]
                    cos = const("cos")[:, 32 * (t - 1):32 * t].unsqueeze(1).to_broadcast([P, 8, 32])
                    sin = const("sin")[:, 32 * (t - 1):32 * t].unsqueeze(1).to_broadcast([P, 8, 32])
                    dve.tensor_tensor(r1, x1, cos, ALU.mult)
                    dve.tensor_tensor(r2, x2, sin, ALU.mult)
                    dve.tensor_tensor(r3, x1, sin, ALU.mult)
                    link(dve.tensor_tensor(r4, x2, cos, ALU.mult))
                    dve.tensor_tensor(x1, r1, r2, ALU.subtract)
                    link(dve.tensor_tensor(x2, r3, r4, ALU.add))
                link(dve.tensor_copy(ksw[:, :, 0:HD], h[:, :, KB + HD:KB + 2 * HD]))
                dve.tensor_copy(ksw[:, :, HD:2 * HD], h[:, :, KB:KB + HD]).then_inc(rope_done, 1)
                for b in range(15):
                    bank = done(dve, ("qkT", b))
                    s = SCALE if b in (4, 5, 6, 9, 10, 11) else 1.0
                    give(dve.tensor_scalar(qkT[:, b, :], bank[:, 0:TOK], s, None, ALU.mult), ("qkT", b))
                    dve.wait_ge(free[groups[("qkT", b)][0]], groups[("qkT", b)][1] + 1)
                    dve.sem_inc(qkT_ready, 1)
                dve.wait_ge(zeta_ready, 1)
                for r in range(2):
                    ins = dve.tensor_tensor(kz[:, r], h[:, 0, KA:KA + 256].rearrange("p (h d) -> p h d", h=H_A),
                                            zeta[:, 4 * r:4 * r + 4].unsqueeze(2).to_broadcast([P, H_A, HD]), ALU.mult)
                ins.then_inc(kz_ready, 1)
                dve.wait_ge(qx_raw, 1)
                for r in range(2):
                    ins = dve.tensor_tensor(qx[:, r], qx[:, r], qkT[:, 0:2, P:3 * P], ALU.mult)
                ins.then_inc(qx_ready, 1)
                for hh in range(H_A):
                    dve.wait_ge(decay_cut, hh + 1)
                    if hh:
                        done(dve, ("oA", hh - 1))
                    dve.tensor_tensor(decay, decay_f, decay_b, ALU.add).then_inc(decay_ready, 1)
                    dve.wait_ge(decay_ready, hh + 1)
                    bank = done(dve, ("sA", hh, 0))
                    link(dve.scalar_tensor_tensor(out=pa[:, 0:P], in0=bank[:, 0:P], scalar=SCALE, in1=decay[:, P:2 * P],
                                                  op0=ALU.mult, op1=ALU.mult))
                    give(dve.scalar_tensor_tensor(out=pa[:, P:3 * P], in0=bank[:, P:3 * P], scalar=SCALE, in1=decay[:, P:3 * P],
                                                  op0=ALU.mult, op1=ALU.mult), ("sA", hh, 0))
                    bank = done(dve, ("sA", hh, 1))
                    link(dve.scalar_tensor_tensor(out=pa[:, 3 * P:5 * P], in0=bank[:, 0:2 * P], scalar=SCALE, in1=decay[:, 0:2 * P],
                                                  op0=ALU.mult, op1=ALU.mult))
                    dve.sem_inc(free[groups[("sA", hh, 1)][0]], 1)
                    dve.sem_inc(pa_ready, 1)
                    bank = done(dve, ("oA", hh))
                    link(dve.tensor_copy(oA[:, :, hh, :], bank[:, 0:TILES * HD].rearrange("p (t d) -> p t d", t=TILES)))
                    dve.sem_inc(free[groups[("oA", hh)][0]], 1)
                bank = done(dve, ("state",))
                link(dve.tensor_scalar(stout[0:64, :], bank[0:64, :], SCALE, None, ALU.mult))
                dve.sem_inc(free[groups[("state",)][0]], 1)
                dve.sem_inc(state_ready, 1)
                ov = oA.rearrange("p t h d -> p (t h) d")
                tv = tmp.rearrange("p (g d) -> p g d", d=HD)
                link(dve.tensor_reduce(mean, ov, AX.X, ALU.add))
                link(dve.tensor_scalar(mean, mean, 1.0 / HD, None, ALU.mult))
                link(dve.tensor_tensor(ov, ov, mean.unsqueeze(2).to_broadcast([P, 12, HD]), ALU.subtract))
                link(dve.tensor_tensor(tv, ov, ov, ALU.mult))
                link(dve.tensor_reduce(var, tv, AX.X, ALU.add))
                dve.tensor_scalar(var, var, 1.0 / HD, EPS, ALU.mult, ALU.add).then_inc(var_ready, 1)
                dve.wait_ge(root_ready, 1)
                link(dve.reciprocal(var, var))
                link(dve.tensor_tensor(ov, ov, var.unsqueeze(2).to_broadcast([P, 12, HD]), ALU.mult))
                o2 = oA.rearrange("p t h d -> p t (h d)")
                dve.wait_ge(gn_ready, 1)
                link(dve.tensor_tensor(o2, o2, gn[:, 0:256].unsqueeze(1).to_broadcast([P, TILES, 256]), ALU.mult))
                link(dve.tensor_tensor(o2, o2, gn[:, 256:512].unsqueeze(1).to_broadcast([P, TILES, 256]), ALU.add))
                dve.wait_ge(gate_ready, 1)
                dve.tensor_tensor(h[:, :, QA:QA + 256], o2, h[:, :, GA:GA + 256], ALU.mult).then_inc(ya_written, 1)

                def peak(g):
                    m, t, h0 = soft[g]
                    nk = P if t == 0 else 3 * P
                    c3 = slice(3 * g, 3 * g + 3)
                    for i in range(3):
                        bank = done(dve, ("s", g, i))
                        ins = dve.tensor_reduce(mx[:, 3 * g + i:3 * g + i + 1], bank[:, 0:nk], AX.X, ALU.max)
                    link(ins)
                    if m == "B":
                        link(dve.tensor_tensor(mx[:, c3], mx[:, c3], small[:, SINK + h0:SINK + h0 + 3], ALU.max))
                    dve.tensor_scalar(neg[:, c3], mx[:, c3], -1.0, None, ALU.mult).then_inc(neg_ready, 1)
                    if m == "B":
                        dve.wait_ge(neg_ready, g + 1)
                        dve.tensor_tensor(sinkx[:, c3], neg[:, c3], small[:, SINK + h0:SINK + h0 + 3], ALU.add).then_inc(sinkx_ready, 1)

                def weigh(g):
                    m, t, h0 = soft[g]
                    c3 = slice(3 * g, 3 * g + 3)
                    dve.wait_ge(exp_done, g + 1)
                    if m == "B":
                        link(dve.tensor_tensor(den[:, c3], den[:, c3], sinke[:, c3], ALU.add))
                    link(dve.reciprocal(recip[:, c3], den[:, c3]))
                    bank = done(dve, ("pv", g))
                    col = (QB if m == "B" else QC) + HD * h0
                    link(dve.tensor_tensor(h[:, t, col:col + 3 * HD].rearrange("p (i d) -> p i d", i=3),
                                           bank[:, 0:3 * HD].rearrange("p (i d) -> p i d", i=3),
                                           recip[:, c3].unsqueeze(2).to_broadcast([P, 3, HD]), ALU.mult))
                    dve.sem_inc(free[groups[("pv", g)][0]], 1)
                    dve.sem_inc(y_written, 1)

                for g in range(len(soft) + 1):
                    if g < len(soft):
                        peak(g)
                    if g:
                        weigh(g - 1)

                def norm(which, t, source):
                    c_ = 0 if t == 0 else 1
                    z = xm[:, t, :]
                    source(z, gateb[:, c_, :])
                    link(dve.scalar_tensor_tensor(out=z, in0=x[:, t, :], scalar=ALPHA, in1=z, op0=ALU.mult, op1=ALU.add))
                    for f in range(2):
                        ins = dve.bn_stats(bn[:, 6 * f:6 * f + 6], z[:, CH * f:CH * f + CH])
                    link(ins)
                    link(dve.bn_aggr(bnag, bn))
                    dve.tensor_scalar(rstd, bnag[:, 1:2], EPS, None, ALU.add).then_inc(lvar_ready, 1)
                    dve.wait_ge(lroot_ready, TILES * which + t + 1)
                    link(dve.reciprocal(rstd, rstd))
                    link(dve.tensor_scalar(z, z, bnag[:, 0:1], rstd, ALU.subtract, ALU.mult))
                    link(dve.tensor_tensor(z, z, lnb[:, 0, :], ALU.mult))
                    dve.tensor_tensor(x[:, t, :], z, lnb[:, 1, :], ALU.add).then_inc(x_ready, 1)

                dve.wait_ge(caches_stored, 64)
                dve.wait_ge(b_ready, 8)
                for t in range(TILES):
                    def from_psum(z, g, t=t):
                        for n in range(OUTC):
                            bank = done(dve, ("y", n, t))
                            cols = slice(CH * n, CH * n + CH)
                            link(dve.tensor_tensor(z[:, cols], bank[:, :], g[:, cols], ALU.mult))
                            dve.sem_inc(free[groups[("y", n, t)][0]], 1)
                    norm(0, t, from_psum)
                dve.wait_ge(x_ready, TILES)
                modulate(1)
                link(dve.memset(sel[:, :, E:E + 2], BIG))
                link(dve.memset(grp[:, :, 8:12], BIG))
                dve.wait_ge(score_ready, 1)
                link(dve.tensor_tensor(sel[:, :, 0:E], score, small[:, 0:E].unsqueeze(1).to_broadcast([P, TILES, E]), ALU.add))
                for t in range(TILES):
                    for g in range(8):
                        ins = dve.max(top[:, 8 * t + g, :], sel[:, t, 8 * g:8 * g + 8])
                link(ins)
                topv = top.rearrange("p (t g) e -> p t g e", t=TILES)
                link(dve.tensor_tensor(grp[:, :, 0:8], topv[:, :, :, 0], topv[:, :, :, 1], ALU.add))
                for t in range(TILES):
                    link(dve.max(top8[:, t, :], grp[:, t, :]))
                    ins = dve.match_replace(grp2[:, t, :], top8[:, t, :], grp[:, t, :], MARK)
                link(ins)
                link(dve.tensor_scalar(grp2[:, :, 0:8], grp2[:, :, 0:8], MARK, None, ALU.is_equal))
                kept = grp2[:, :, 0:8].unsqueeze(3).to_broadcast([P, TILES, 8, 8])
                for t in range(TILES):
                    s8 = sel[:, t, 0:E].rearrange("p (g e) -> p g e", g=8)
                    link(dve.tensor_tensor(s8, s8, kept[:, t], ALU.mult))
                link(dve.tensor_scalar(grp[:, :, 0:8], grp2[:, :, 0:8], -NEG, NEG, ALU.mult, ALU.add))
                for t in range(TILES):
                    s8 = sel[:, t, 0:E].rearrange("p (g e) -> p g e", g=8)
                    link(dve.tensor_tensor(s8, s8, grp[:, t, 0:8].unsqueeze(2).to_broadcast([P, 8, 8]), ALU.add))
                for t in range(TILES):
                    link(dve.max(top8[:, t, :], sel[:, t, :]))
                    ins = dve.match_replace(sel2[:, t, :], top8[:, t, :], sel[:, t, :], MARK)
                link(ins)
                dve.tensor_scalar(mask, sel2[:, :, 0:E], MARK, None, ALU.is_equal).then_inc(mask_ready, 1)
                dve.wait_ge(mask_ready, 1)
                link(dve.tensor_tensor(score, score, mask, ALU.mult))
                link(dve.tensor_reduce(wsum[:, 0:TILES], score, AX.X, ALU.add))
                link(dve.reciprocal(wsum[:, 0:TILES], wsum[:, 0:TILES]))
                link(dve.tensor_tensor(score, score, wsum[:, 0:TILES].unsqueeze(2).to_broadcast([P, TILES, E]), ALU.mult))
                dve.tensor_scalar(vals[:, :, :, 2], score, ROUTE_SCALE, None, ALU.mult)
                for t in range(TILES):
                    link(dve.tensor_tensor_scan(rank[:, t, :], const("ones")[:, 0:E], mask[:, t, :], 0.0, ALU.mult, ALU.add))
                for t in range(TILES):
                    dve.tensor_scalar(vals[:, t, :, 1], rank[:, t, :], const("row")[:, t:t + 1], None, ALU.add)
                    link(dve.tensor_scalar(vals[:, t, :, 0], rank[:, t, :], 0.0, const("tok")[:, t:t + 1], ALU.mult, ALU.add))
                bank = done(dve, ("pos",))
                pos = bank[:, 0:TILES * E].rearrange("p (t e) -> p t e", t=TILES)
                link(dve.scalar_tensor_tensor(out=posm, in0=pos, scalar=1.0, in1=mask, op0=ALU.add, op1=ALU.mult))
                link(dve.tensor_scalar(posm, posm, -1.0, None, ALU.add))
                link(dve.tensor_reduce(wsum[:, 4:5], bank[:, TILES * E:TILES * E + E], AX.X, ALU.max))
                dve.sem_inc(free[groups[("pos",)][0]], 1)
                dve.tensor_copy(most[:, 0:1], wsum[:, 4:5]).then_inc(most_ready, 1)
                def shared_tail(t):
                    bank = done(dve, ("shT", t))
                    link(dve.tensor_copy(shT, bank[:, 0:2 * P].rearrange("p (k t) -> p k t", k=2)))
                    dve.sem_inc(free[groups[("shT", t)][0]], 1)
                    dve.sem_inc(shT_ready, 1)
                    dve.wait_ge(xm_saved, 16)
                    for f in range(2):
                        bank = done(dve, ("sy", t, f))
                        give(dve.tensor_copy(xm[:, t, CH * f:CH * f + CH], bank[:, :]), ("sy", t, f))

                for t in range(TILES):
                    bank = done(dve, ("sgu", t))
                    dve.wait_ge(ssilu_done, t + 1)
                    if t >= 2:
                        done(dve, ("shT", t - 2))
                    link(dve.tensor_tensor(hid_s[t % 2], sg_s[t], bank[:, F:2 * F], ALU.mult))
                    dve.sem_inc(free[groups[("sgu", t)][0]], 1)
                    dve.sem_inc(shid_ready, 1)
                    if t:
                        shared_tail(t - 1)
                shared_tail(TILES - 1)

                def expert_pass(S, q, p):
                    b = q * E
                    if p:
                        dve.wait_ge(MAIN["pass_done"], 1)
                    if q:
                        dve.wait_ge(S["pass_done"], q)
                    else:
                        dve.sem_inc(S["hid_ready"], 2)
                        dve.sem_inc(S["hT_ready"], 1)
                        dve.sem_inc(S["ys_ready"], 1)
                        dve.sem_inc(S["pick_used"], 2)
                    with dve.Fori(0, E // UN) as it:
                        for i in range(UN):
                            e = it * UN + i
                            dve.wait_ge(S["pick_used"], e + (b + 1))
                            for t in range(TILES):
                                ins = dve.tensor_scalar(pick[:, i % 2, t, :], const("slot"), 1.0 * P * p, posm[:, t, bass.ds(e, 1)],
                                                        ALU.add, ALU.is_equal)
                            ins.then_inc(S["pick_ready"], 1)
                    dve.wait_ge(S["pick_used"], b + E + 2)
                    sv = psum[7][:, 0:3 * E].rearrange("p (e v) -> p v e", v=3)
                    dve.tensor_scalar(slot_idx[:, :, 0:E], sv[:, 0:2, :], 1.0 * FAR, None, ALU.add)
                    dve.tensor_copy(slot_w[:], sv[:, 2, :]).then_inc(S["slots_ready"], 1)
                    dve.wait_ge(S["slots_ready"], q + 1)
                    with dve.Fori(0, E // UN) as it:
                        for i in range(UN):
                            e = it * UN + i
                            dve.wait_ge(S["silu_done"], e + (b + 1))
                            dve.scalar_tensor_tensor(out=hid, in0=sgate, scalar=slot_w[:, bass.ds(e, 1)], in1=psum[i % 2][:, F:2 * F],
                                                     op0=ALU.mult, op1=ALU.mult).then_inc(S["hid_ready"], 1)
                            dve.wait_ge(S["hT_full"], e + (b + 1))
                            dve.tensor_copy(hT, psum[4][:, 0:2 * P].rearrange("p (k t) -> p k t", k=2)).then_inc(S["hT_ready"], 1)
                            dve.wait_ge(S["y_full"], e + (b + 1))
                            dve.wait_ge(S["ys_free"], e + (b + 1))
                            dve.tensor_copy(ys[i % 2][:, 0:CH], psum[5][:, :])
                            dve.tensor_copy(ys[i % 2][:, CH:DM], psum[6][:, :]).then_inc(S["ys_ready"], 1)

                expert_pass(MAIN, 0, 0)
                dve.wait_ge(most_ready, 1)
                with dve.If(dve.value_load(most[0:1, 0:1], min_val=0, max_val=TOK) > P):
                    expert_pass(OVER, 0, 1)
                    expert_pass(OVER, 1, 2)
                    dve.nop()
                for t in range(TILES):
                    def from_rows(z, g, t=t):
                        s = 2 * (t % 2)
                        dve.wait_ge(back[t % 2], 32 * (t // 2 + 1))
                        r4 = ring[s][:].rearrange("p (k d) -> p k d", d=DM)
                        r2 = ring[s + 1][:].rearrange("p (k d) -> p k d", d=DM)
                        for k in range(4):
                            link(dve.tensor_tensor(z, z, r4[:, k, :], ALU.add))
                        for k in range(2):
                            link(dve.tensor_tensor(z, z, r2[:, k, :], ALU.add))
                        link(dve.tensor_tensor(z, z, g, ALU.mult))
                    norm(1, t, from_rows)
                dve.wait_ge(x_ready, 2 * TILES)

            @blk.scalar
            def _(act):
                for n in range(MODC):
                    act.wait_ge(stage_ready, n + 1)
                    r = 2 * (n // 2)
                    act.dma_start(raw[r:r + 2, CH * (n % 2):CH * (n % 2) + CH], stage[n % 2][0:2, :]).then_inc(stage_sent[n % 2], 16)
                act.wait_ge(dneg_ready, 1)
                act.activation(lg, dneg, ACT.Exp).then_inc(act_step, 1)
                act.wait_ge(act_step, 1)
                act.activation(lg, lg, ACT.Ln, bias=1.0).then_inc(softplus_ready, 1)
                bank = done(act, ("gn",))
                give(act.activation(gn, bank[:, :], ACT.Copy), ("gn",))
                act.wait_ge(free[groups[("gn",)][0]], groups[("gn",)][1] + 1)
                act.sem_inc(gn_ready, 1)

                def turned(which):
                    for t in range(TILES):
                        for g in range(2):
                            name = ("xT", which, t, g)
                            bank = done(act, name)
                            give(act.activation(xmT[:, 4 * g:4 * g + 4, P * t:P * t + P],
                                                bank[:, :].rearrange("p (k t) -> p k t", k=4), ACT.Copy), name)
                            act.wait_ge(free[groups[name][0]], groups[name][1] + 1)
                            act.sem_inc(xmT_ready, 1)

                turned(0)
                for i, (n, t) in enumerate(HG):
                    if i % 2 == 1:
                        cols = min(CH, W_IN - CH * n)
                        bank = done(act, ("h", n, t))
                        give(act.activation(h[:, t, CH * n:CH * n + cols], bank[:, 0:cols], ACT.Copy), ("h", n, t))
                        act.wait_ge(free[groups[("h", n, t)][0]], groups[("h", n, t)][1] + 1)
                        act.sem_inc(h_act, 1)
                act.wait_ge(lg_ready, 1)
                act.activation(zeta[:, 0:4], lg[:, 0:4], ACT.Exp, scale=const("down")).then_inc(act_step, 1)
                act.activation(zeta[:, 4:8], lg[:, 4:8], ACT.Exp, scale=const("up")).then_inc(act_step, 1)
                act.wait_ge(act_step, 3)
                act.sem_inc(zeta_ready, 1)
                for r, ramp in enumerate(("from_start", "from_end")):
                    for hh in range(H_A):
                        p0 = 64 * (hh % 2)
                        act.activation(qx[p0:p0 + 64, r, hh // 2, :], const(ramp)[p0:p0 + 64, :], ACT.Exp,
                                       scale=lg[p0:p0 + 64, 4 * r + hh:4 * r + hh + 1]).then_inc(act_step, 1)
                act.wait_ge(act_step, 11)
                act.sem_inc(qx_raw, 1)
                for hh in range(H_A):
                    if hh:
                        act.wait_ge(decay_ready, hh)
                    act.activation(decay_f, const("absdiff"), ACT.Exp, scale=lg[:, hh:hh + 1]).then_inc(decay_raw, 1)
                    act.activation(decay_b, const("absdiff"), ACT.Exp, scale=lg[:, 4 + hh:5 + hh]).then_inc(decay_raw, 1)
                    if hh == 0:
                        for g, n in ((0, 4), (1, 1)):
                            bank = done(act, ("kctxT", g))
                            give(act.activation(kctxT[:, 4 * g:4 * g + n, :], bank[:, 0:P * n].rearrange("p (b k) -> p b k", b=n),
                                                ACT.Copy), ("kctxT", g))
                            act.wait_ge(free[groups[("kctxT", g)][0]], groups[("kctxT", g)][1] + 1)
                            act.sem_inc(kctxT_ready, 1)
                act.wait_ge(h_dve, h_on_dve)
                act.activation(h[:, :, GA:GA + 256], h[:, :, GA:GA + 256], ACT.Silu).then_inc(gate_ready, 1)
                act.wait_ge(var_ready, 1)
                act.activation(var, var, ACT.Sqrt).then_inc(root_ready, 1)
                for g in range(len(soft) + 1):
                    if g:
                        m, t, h0 = soft[g - 1]
                        nk = P if t == 0 else 3 * P
                        for i in range(3):
                            bank = done(act, ("pT", g - 1, i))
                            give(act.activation(probT[:, i, 0:nk], bank[:, 0:nk], ACT.Copy), ("pT", g - 1, i))
                            act.wait_ge(free[groups[("pT", g - 1, i)][0]], groups[("pT", g - 1, i)][1] + 1)
                            act.sem_inc(probT_ready, 1)
                    if g < len(soft):
                        m, t, h0 = soft[g]
                        nk = P if t == 0 else 3 * P
                        act.wait_ge(neg_ready, g + 1)
                        for i in range(3):
                            c_ = 3 * g + i
                            bank = psum[groups[("s", g, i)][0]]
                            give(act.activation(prob[:, i, 0:nk], bank[:, 0:nk], ACT.Exp, bias=neg[:, c_:c_ + 1],
                                                accum_out=den[:, c_:c_ + 1]), ("s", g, i))
                        if m == "B":
                            act.wait_ge(sinkx_ready, sum(s[0] == "B" for s in soft[:g + 1]))
                            act.activation(sinke[:, 3 * g:3 * g + 3], sinkx[:, 3 * g:3 * g + 3], ACT.Exp).then_inc(act_step, 1)
                            act.wait_ge(act_step, 11 + sum(s[0] == "B" for s in soft[:g + 1]))
                        for i in range(3):
                            name = ("s", g, i)
                            act.wait_ge(free[groups[name][0]], groups[name][1] + 1)
                        act.sem_inc(exp_done, 1)
                for b in range(8):
                    bank = done(act, ("yT", b))
                    give(act.activation(xmT[:, b, :], bank[:, 0:TOK], ACT.Copy), ("yT", b))
                    act.wait_ge(free[groups[("yT", b)][0]], groups[("yT", b)][1] + 1)
                    act.sem_inc(yT_ready, 1)

                def norm_rows(which):
                    if which:
                        act.wait_ge(x_ready, TILES)
                    else:
                        act.wait_ge(states_stored, 32)
                    for r in range(4):
                        for f in range(2):
                            bank = done(act, ("b", which, r, f))
                            dst = (gateb[:, r, :] if r < 2 else lnb[:, r - 2, :])[:, CH * f:CH * f + CH]
                            give(act.activation(dst, bank[:, :], ACT.Copy), ("b", which, r, f))
                            act.wait_ge(free[groups[("b", which, r, f)][0]], groups[("b", which, r, f)][1] + 1)
                            act.sem_inc(b_ready, 1)

                norm_rows(0)
                for t in range(TILES):
                    act.wait_ge(lvar_ready, t + 1)
                    act.activation(rstd, rstd, ACT.Sqrt).then_inc(lroot_ready, 1)
                norm_rows(1)
                turned(1)
                bank = done(act, ("logit",))
                act.activation(score, bank[:, 0:TILES * E].rearrange("p (t e) -> p t e", t=TILES), ACT.Sigmoid).then_inc(score_ready, 1)
                act.wait_ge(score_ready, 1)
                act.sem_inc(free[groups[("logit",)][0]], 1)
                for t in range(TILES):
                    bank = done(act, ("sgu", t))
                    act.activation(sg_s[t], bank[:, 0:F], ACT.Silu).then_inc(ssilu_done, 1)

                def expert_pass(S, q):
                    b, bx = q * E, q * (E + 1)
                    if S is OVER and not q:
                        act.wait_ge(MAIN["xT_ready"], E + 2)
                    if not q:
                        act.sem_inc(S["xT_ready"], 1)

                    def turned_rows(m):
                        act.wait_ge(S["xT_full"], m + (bx + 1))
                        act.activation(xgT[:, 0:4, :], psum[2][:, :].rearrange("p (k t) -> p k t", k=4), ACT.Copy)
                        act.activation(xgT[:, 4:8, :], psum[3][:, :].rearrange("p (k t) -> p k t", k=4), ACT.Copy).then_inc(S["xT_ready"], 1)

                    turned_rows(0)
                    with act.Fori(0, E // UN) as it:
                        for i in range(UN):
                            e = it * UN + i
                            act.wait_ge(S["gu_full"], e + (b + 1))
                            act.wait_ge(S["hid_ready"], e + (b + 2))
                            act.activation(sgate, psum[i % 2][:, 0:F], ACT.Silu).then_inc(S["silu_done"], 1)
                            turned_rows(e + 1)

                expert_pass(MAIN, 0)
                act.wait_ge(most_ready, 1)
                with act.If(act.value_load(most[0:1, 0:1], min_val=0, max_val=TOK) > P):
                    expert_pass(OVER, 0)
                    expert_pass(OVER, 1)
                    act.nop()
                for t in range(TILES):
                    act.wait_ge(lvar_ready, TILES + t + 1)
                    act.activation(rstd, rstd, ACT.Sqrt).then_inc(lroot_ready, 1)

            @blk.gpsimd
            def _(pool):
                def mask_bias(t):
                    pool.wait_ge(bias_loaded, 32 * H_C * (t + 1))
                    nm = const("na_mask").unsqueeze(1).to_broadcast([P, H_C, 256])
                    pool.tensor_tensor(nab, nab, nm, ALU.add).then_inc(bias_masked, 1)

                mask_bias(0)
                for hh in range(H_A):
                    pool.wait_ge(decay_raw, 2 * hh + 2)
                    pool.affine_select(out=decay_f, in_=decay_f, compare_op=ALU.is_ge, fill=0.0, base=-P,
                                       pattern=[[1, TOK]], channel_multiplier=-1)
                    pool.affine_select(out=decay_b, in_=decay_b, compare_op=ALU.is_ge, fill=0.0, base=P,
                                       pattern=[[-1, TOK]], channel_multiplier=1).then_inc(decay_cut, 1)
                mask_bias(1)
                pool.wait_ge(yT_ready, 8)
                pool.wait_ge(caches_stored, 64)
                pool.memset(xg[0], 0.0).then_inc(xg_zeroed, 1)
                pool.memset(xg[1], 0.0).then_inc(xg_zeroed, 1)
                pool.wait_ge(xg_zeroed, 2)
                pool.wait_ge(xm_saved, 16)

                def expert_pass(S, q):
                    b, bx, bi = q * E, q * (E + 1), q * (2 * E + 2)
                    pool.wait_ge(S["slots_ready"], q + 1)
                    if not q:
                        pool.sem_inc(S["ys_free"], 2)

                    def gather(par, e, n):
                        pool.tensor_copy(now_idx[par][:], slot_idx[:, 0, e:e + 1] if isinstance(e, int) else slot_idx[:, 0, bass.ds(e, 1)]
                                         ).then_inc(S["idx_set"], 1)
                        pool.wait_ge(S["idx_set"], n)
                        pool.sem_inc(idx_seen, 1)
                        pool.indirect_dma_start(xg[par], None, scratch_x,
                                                bass.IndirectOffsetOnAxis(ap=now_idx[par][:], axis=0),
                                                bounds_check=TOK - 1, oob_is_err=False).then_inc(S[f"gathered{par}"], 16)

                    if q:
                        pool.wait_ge(S["xT_full"], bx)
                    gather(0, 0, bi + 1)
                    gather(1, 1, bi + 2)
                    with pool.Fori(0, E // UN) as it:
                        for i in range(UN):
                            e = it * UN + i
                            pool.wait_ge(S["xT_full"], e + (bx + 1))
                            gather(i % 2, e + 2, e * 2 + (bi + 3))
                            pool.wait_ge(S["ys_ready"], e + (b + 2))
                            pool.tensor_copy(now_idx[2 + i % 2][:], slot_idx[:, 1, bass.ds(e, 1)]).then_inc(S["idx_set"], 1)
                            pool.wait_ge(S["idx_set"], e * 2 + (bi + 4))
                            pool.sem_inc(idx_seen, 1)
                            pool.indirect_dma_start(scratch_y,
                                                    bass.IndirectOffsetOnAxis(ap=now_idx[2 + i % 2][:], axis=0),
                                                    ys[i % 2], None, bounds_check=TOK * TOPK - 1, oob_is_err=False
                                                    ).then_inc(S[f"scattered{i % 2}"], 16)
                            pool.wait_ge(S[f"scattered{i % 2}"], (it * 2 + (i // 2 + q * (E // 2) + 1)) * 16)
                            pool.sem_inc(S["ys_free"], 1)
                    for par in range(2):
                        pool.wait_ge(S[f"gathered{par}"], 16 * 33 * (q + 1))
                    pool.wait_ge(S["xT_full"], bx + E + 1)
                    pool.sem_inc(S["pass_done"], 1)

                expert_pass(MAIN, 0)
                pool.wait_ge(most_ready, 1)
                with pool.If(pool.value_load(most[0:1, 0:1], min_val=0, max_val=TOK) > P):
                    expert_pass(OVER, 0)
                    expert_pass(OVER, 1)
                    pool.nop()
                pool.sem_inc(experts_done, 1)

            bctx.close()
            numbers = sorted(x.num for x in layer_sems)
            assert numbers == list(range(numbers[0], numbers[-1] + 1))
            nc.gpsimd.dma_reset(range(numbers[0], numbers[-1] + 1))
            nc.gpsimd.sem_clear(range(numbers[0], numbers[-1] + 1))
            nc.all_engine_barrier()

        with ExitStack() as c1:
            tokens_stored = c1.enter_context(nc.semaphore("tokens_stored"))
            blk1 = c1.enter_context(nc.Block())

            @blk1.sync
            def _(sp):
                sp.dma_start(o["y_prompt"][0], x[:, 0, :]).then_inc(tokens_stored, 16)
                sp.dma_start(o["y_sample"][0].rearrange("(t p) d -> p t d", p=P), x[:, 1:3, :]).then_inc(tokens_stored, 16)
                sp.wait_ge(tokens_stored, 32)


INPUTS = ("x_prompt", "x_sample", "state_ret_fwd", "state_ret_bwd", "cache_win_k", "cache_win_v", "cache_na_k",
          "cache_na_v", "c", "c_ctx", "w_in", "w_out", "ret_decay_fwd", "ret_decay_bwd", "ret_gn_g", "ret_gn_b",
          "win_sink", "na_rpb", "w_mod", "b_mod", "ln1_g", "ln1_b", "ln2_g", "ln2_b", "w_router", "b_router",
          "w_expert_gu", "w_expert_down", "w_shared_gu", "w_shared_down")
OUTPUTS = (("y_prompt", (1, P, DM)), ("y_sample", (1, 2 * P, DM)),
           ("new_fwd", (1, DEPTH, H_A, HD, HD)), ("new_bwd", (1, DEPTH, H_A, HD, HD)),
           ("new_win_k", (1, DEPTH, 2, P, HD)), ("new_win_v", (1, DEPTH, 2, P, HD)),
           ("new_na_k", (1, DEPTH, H_C, P, HD)), ("new_na_v", (1, DEPTH, H_C, P, HD)))


def kernel(**inputs):
    import numpy as _np
    import concourse.bacc as _bacc
    from concourse import mybir as _mybir
    from concourse.bass_utils import run_bass_kernel_spmd as _run

    nc = _bacc.Bacc("TRN2", target_bir_lowering=False, num_devices=1)
    arrays, a, o = {}, {}, {}
    for name in INPUTS + ("consts",):
        v = constants() if name == "consts" else _np.ascontiguousarray(inputs[name])
        arrays[f"in_{name}"] = v
        a[name] = nc.dram_tensor(f"in_{name}", v.shape, _mybir.dt.from_np(v.dtype), kind="ExternalInput").ap()
    for name, shape in OUTPUTS:
        o[name] = nc.dram_tensor(f"out_{name}", shape, _mybir.dt.float32, kind="ExternalOutput").ap()
    build(nc, a, o)
    r = _run(nc, [arrays], core_ids=[0])
    return tuple(r.results[0][f"out_{name}"] for name, _ in OUTPUTS)
```

```python
import numpy as np
import concourse.bass as bass
from concourse import mybir
from contextlib import ExitStack

F32 = mybir.dt.float32
F32R = mybir.dt.float32r
I32 = mybir.dt.int32
ALU = mybir.AluOpType
ACT = mybir.ActivationFunctionType
AX = mybir.AxisListType

P = 128
DM = 1024
KD = DM // P
DEPTH = 2
TILES = 3
TOK = TILES * P
HD = 64
CH = 512
W_IN = 2816
QA, KA, VA, GA, QB, KB, VB, QC, KC, VC = 0, 256, 512, 768, 1024, 1408, 1536, 1664, 2048, 2432
H_A, H_B, H_C = 4, 6, 6
SCALE = HD ** -0.5
ALPHA = float((2 * DEPTH) ** 0.25)
EPS = 1e-5
NEG = -1e30
BIG = 3.0e38
MARK = -3.0e38
E = 64
TOPK = 6
F = 256
ROUTE_SCALE = 2.5
FAR = 4096
NG = 4
ND = 2
UN = 4
MODC = 6 * DM // CH
INC = (W_IN + CH - 1) // CH
OUTC = DM // CH
CHUNKS = MODC + INC + OUTC + 1
NROW = 17
LN_ROW, SMALL_ROW = 12, 16
SINK, DEC = 64, 70

CONSTS = {}


def constants():
    p = np.arange(P)[:, None]
    j = np.arange(P)[None, :]
    parts = []

    def put(name, a):
        a = np.broadcast_to(a, (P, a.shape[1])).astype(np.float32)
        CONSTS[name] = (sum(x.shape[1] for x in parts), a.shape[1])
        parts.append(a)

    put("ident", (p == j) * 1.0)
    put("flip", (p + j == P - 1) * 1.0)
    put("before", (p < j) * 1.0)
    put("ones", np.ones((P, P)))
    put("slot", j * 1.0)
    put("band_next", np.where(j <= p, 0.0, NEG))
    put("band_prev", np.where(j >= p, 0.0, NEG))
    qc = 63 - np.arange(P)[:, None] % 64
    kc = np.arange(256)[None, :] % 64
    c0 = np.clip(qc - 8, 0, 48)
    put("na_mask", np.where((kc >= c0) & (kc < c0 + 16), 0.0, NEG))
    put("absdiff", np.abs(np.arange(3 * P)[None, :] - P - p) * 1.0)
    i = np.arange(2 * P)[None, :]
    put("from_start", i + 1.0)
    put("from_end", 2 * P - i * 1.0)
    inv = (10000.0 ** (-np.arange(16, dtype=np.float32) / 16)).astype(np.float32)
    tables = []
    for t in range(2):
        pos = np.arange(P) + P * t
        ang = np.concatenate([(pos // 64)[:, None] * inv, (pos % 64)[:, None] * inv], 1).astype(np.float32)
        tables.append((np.cos(ang), np.sin(ang)))
    put("cos", np.concatenate([tables[0][0], tables[1][0]], 1))
    put("sin", np.concatenate([tables[0][1], tables[1][1]], 1))
    put("down", P - 1.0 - p)
    put("up", p * 1.0)
    tok = p + P * np.arange(TILES)[None, :]
    k = np.arange(TOPK)[None, None, :]
    t3 = tok[:, :, None] + 0 * k
    put("tok_row", np.stack([t3, t3 * TOPK + k, 0 * t3], -1).reshape(P, -1))
    put("empty", np.tile([1.0 * FAR, 1.0 * FAR, 0.0], E)[None, :])
    return np.ascontiguousarray(np.concatenate(parts, 1))


NCONST = constants().shape[1] - 3 * E


def psum_groups():
    names = [("mod", n) for n in range(MODC)] + [("small",), ("gn",)]
    names += [("m", 0, c, f, w) for c in range(2) for f in range(2) for w in range(2)]
    names += [("xT", 0, t, g) for t in range(TILES) for g in range(2)]
    names += [("h", n, t) for n in range(INC) for t in range(TILES)]
    names += [("qkT", b) for b in range(15)] + [("kctxT", 0), ("kctxT", 1)]
    for h in range(H_A):
        names += [("sA", h, 0), ("sA", h, 1)]
    names += [("oA", h) for h in range(H_A)] + [("state",)]
    for g in range(12 + 1):
        if g < 12:
            names += [("s", g, i) for i in range(3)]
        if g:
            names += [("pT", g - 1, i) for i in range(3)] + [("pv", g - 1)]
    names += [("yT", b) for b in range(8)]
    names += [("b", 0, r, f) for r in range(4) for f in range(2)]
    names += [("y", n, t) for n in range(OUTC) for t in range(TILES)]
    names += [("m", 1, c, f, w) for c in range(2) for f in range(2) for w in range(2)]
    names += [("b", 1, r, f) for r in range(4) for f in range(2)]
    names += [("xT", 1, t, g) for t in range(TILES) for g in range(2)]
    names += [("logit",), ("pos",)]
    names += [("sgu", t) for t in range(TILES)]
    for t in range(TILES):
        names += [("shT", t), ("sy", t, 0), ("sy", t, 1)]
    uses = [0] * 8
    out = {}
    for n, name in enumerate(names):
        out[name] = (n % 8, uses[n % 8])
        uses[n % 8] += 1
    return out, names, uses


def build(nc, a, o):
    groups, order, bank_uses = psum_groups()
    soft = [(m, t, h) for t in range(TILES) for m in "BC" for h in (0, 3)]

    with ExitStack() as ctx:
        begins = {}

        def sb(name, cols, dt=F32, rows=P):
            t = ctx.enter_context(nc.sbuf_tensor(name, [rows, cols], dt))
            begins[name] = nc.sbuf_base - 4 * cols
            return t

        def rounded(name, base, cols, at=0):
            return nc.alloc_sbuf_tensor_at(name, [P, cols], F32R, offset=begins[base] + 4 * at)[:]

        scratch_x = nc.dram_tensor("scratch_x", (TOK, DM), F32, kind="Internal").ap()
        scratch_y = nc.dram_tensor("scratch_y", (TOK * TOPK, DM), F32, kind="Internal").ap()
        slots = nc.dram_tensor("slots", (TOK * E, 3), F32, kind="Internal").ap()

        ring = [sb(f"ring{i}", KD * CH) for i in range(NG)]
        x = sb("x", TILES * DM)[:].rearrange("p (t d) -> p t d", t=TILES)
        cst = sb("cst", NCONST)
        xmT = sb("xmT", KD * TOK)[:].rearrange("p (k t) -> p k t", k=KD)
        rows = sb("rows", DM)
        condT = sb("condT", KD * 2)[:].rearrange("p (k c) -> p k c", c=2)
        cmisc = sb("cmisc", 512)
        A = sb("arena_a", TILES * W_IN + 15 * TOK)
        B = sb("arena_b", 12200)
        psum = [ctx.enter_context(nc.psum_tensor(f"bank{i}", [P, 512], F32)) for i in range(8)]

        def const(name):
            at, n = CONSTS[name]
            return cst[:, at:at + n]

        class Carve:
            def __init__(self, base, at=0):
                self.base, self.at = base, at

            def __call__(self, n):
                self.at += n
                assert self.at <= self.base.shape[1], self.at
                return self.base[:, self.at - n:self.at]

        c = Carve(A)
        xm = c(TILES * DM).rearrange("p (t d) -> p t d", t=TILES)
        raw, bmod, stage0, stage1 = c(DM), c(DM), c(CH), c(CH)
        stage = [stage0, stage1]
        cond = c(P)
        c = Carve(A)
        h = c(TILES * W_IN).rearrange("p (t d) -> p t d", t=TILES)
        qkT = c(15 * TOK).rearrange("p (b t) -> p b t", b=15)
        c = Carve(A, TILES * DM)
        xg = [c(DM), c(DM)]
        xgT_at = c.at
        c(DM)
        ys = [c(DM), c(DM)]
        hid, sgate = c(F), c(F)
        hT = [c(F).rearrange("p (k t) -> p k t", k=2) for _ in range(2)]
        table = c(TILES * E * 3).rearrange("p (t e v) -> p t e v", t=TILES, e=E)
        sg_s, hid_s = [c(F) for _ in range(TILES)], [c(F) for _ in range(2)]
        xgT_lo_at, high1_at = c.at, c.at + DM
        c(DM)
        high1 = c(KD * CH // 2)
        shT = high1[:, 0:2 * P].rearrange("p (k t) -> p k t", k=2)
        wr = high1[:, 2 * P:2 * P + KD * E].rearrange("p (k e) -> p k e", k=KD)
        c = Carve(B)
        nab = c(H_C * 256).rearrange("p (h k) -> p h k", h=H_C)
        prob = c(3 * TOK).rearrange("p (i k) -> p i k", i=3)
        probT = c(3 * TOK).rearrange("p (i k) -> p i k", i=3)
        kctx = c(10 * HD)
        kctxT = c(5 * P).rearrange("p (b k) -> p b k", b=5)
        vctx = c(8 * HD).rearrange("p (h d) -> p h d", h=8)
        s0 = c(4 * HD).rearrange("p (r g d) -> p r g d", r=2, g=2)
        gn = c(2 * 256)
        decay_f, decay_b = c(TOK), c(TOK)
        decay = c(TOK)
        pa = c(5 * P)
        qx = c(4 * 256).rearrange("p (r g t) -> p r g t", r=2, g=2)
        kz = c(2 * 256).rearrange("p (r h d) -> p r h d", r=2, h=H_A)
        oA = c(TILES * 256).rearrange("p (t h d) -> p t h d", t=TILES, h=H_A)
        tmp = c(TILES * 256)
        ksw = c(TILES * P).rearrange("p (t d) -> p t d", t=TILES)
        stout = c(512)
        c = Carve(B)
        down = [c(2 * DM).rearrange("p (k n) -> p k n", k=2) for _ in range(ND)]
        gateb = c(2 * DM).rearrange("p (c d) -> p c d", c=2)
        lnb = c(2 * DM).rearrange("p (r d) -> p r d", r=2)
        high0_at = c.at
        high0 = c(2 * TILES * TOPK * E)
        of_rank = high0[:, 0:TILES * TOPK * E].rearrange("p (t k e) -> p t k e", t=TILES, k=TOPK)
        picked = high0[:, TILES * TOPK * E:].rearrange("p (t k e) -> p t k e", t=TILES, k=TOPK)
        score = c(TILES * E).rearrange("p (t e) -> p t e", t=TILES)
        sel = c(TILES * 66).rearrange("p (t e) -> p t e", t=TILES)
        sel2 = c(TILES * 66).rearrange("p (t e) -> p t e", t=TILES)
        grp = c(TILES * 12).rearrange("p (t e) -> p t e", t=TILES)
        grp2 = c(TILES * 12).rearrange("p (t e) -> p t e", t=TILES)
        top = c(24 * 8).rearrange("p (g e) -> p g e", g=24)
        top8 = c(TILES * 8).rearrange("p (t e) -> p t e", t=TILES)
        mask = c(TILES * E).rearrange("p (t e) -> p t e", t=TILES)
        posm = c(TILES * E).rearrange("p (t e) -> p t e", t=TILES)
        rank = c(TILES * E).rearrange("p (t e) -> p t e", t=TILES)
        wsum = c(8)
        counts = c(E)
        entry = c(TILES * TOPK * 3).rearrange("p (j v) -> p j v", v=3)
        xT_hi = rounded("xT_hi", "arena_a", DM, xgT_at).rearrange("p (k t) -> p k t", k=KD)
        xT_lo = rounded("xT_lo", "arena_a", DM, xgT_lo_at).rearrange("p (k t) -> p k t", k=KD)
        w_hi = [rounded(f"w_hi{j}", n, KD * CH // 2, at).rearrange("p (k n) -> p k n", k=KD // 2)
                for j, (n, at) in enumerate((("arena_b", high0_at), ("arena_a", high1_at)))]
        w_lo = [rounded(f"w_lo{i}", f"ring{i}", KD * CH).rearrange("p (k n) -> p k n", k=KD) for i in range(NG)]
        place = c(TILES * TOPK)
        place_i = sb("place_i", TILES * TOPK, I32)
        most = sb("most", 2, I32)
        slot_idx = sb("slot_idx", 2 * (E + 2), I32)[:].rearrange("p (v e) -> p v e", v=2)
        slot_w = sb("slot_w", E)
        now_idx = [sb(f"now_idx{i}", 1, I32) for i in range(4)]
        c = Carve(cmisc)
        lg, dneg, small, zeta = c(8), c(8), c(80), c(8)
        mx, neg, den, sinkx, sinke, recip = c(36), c(36), c(36), c(36), c(36), c(36)
        mean, var = c(12), c(12)
        bn, bnag, rstd = c(12), c(2), c(1)

        mod_row = {"sh1": 0, "sc1": 2, "g1": 4, "sh2": 6, "sc2": 8, "g2": 10}


        with ExitStack() as c0:
            cst_loaded, tokens_loaded, cond_loaded, cond_turned, cond_done, far_set = (
                c0.enter_context(nc.semaphore(n)) for n in
                ("cst_loaded", "tokens_loaded", "cond_loaded", "cond_turned", "cond_done", "far_set"))
            blk0 = c0.enter_context(nc.Block())

            @blk0.sync
            def _(sp):
                sp.dma_start(cst[:], a["consts"][:, 0:NCONST]).then_inc(cst_loaded, 16)
                sp.dma_start(x[:, 0, :], a["x_prompt"][0]).then_inc(tokens_loaded, 16)
                sp.dma_start(x[:, 1:3, :], a["x_sample"][0].rearrange("(t p) d -> p t d", p=P)).then_inc(tokens_loaded, 16)
                sp.dma_start(cond[0:KD, :], a["c_ctx"].rearrange("(k p) -> k p", p=P)).then_inc(cond_loaded, 16)
                sp.dma_start(cond[KD:2 * KD, :], a["c"][0].rearrange("(k p) -> k p", p=P)).then_inc(cond_loaded, 16)
                sp.wait_ge(cst_loaded, 16)
                sp.wait_ge(tokens_loaded, 32)

            @blk0.tensor
            def _(pe):
                pe.wait_ge(cst_loaded, 16)
                pe.wait_ge(cond_loaded, 32)
                pe.transpose(psum[0][:, 0:2 * KD], cond[0:2 * KD, :], const("ident")[0:2 * KD, 0:2 * KD]).then_inc(cond_turned, 1)

            @blk0.scalar
            def _(act):
                act.wait_ge(cond_turned, 1)
                act.activation(condT.rearrange("p k c -> p c k"), psum[0][:, 0:2 * KD].rearrange("p (c k) -> p c k", c=2),
                               ACT.Silu).then_inc(cond_done, 1)
                act.wait_ge(cond_done, 1)

            @blk0.gpsimd
            def _(pool):
                pool.memset(slot_idx[:, :, E:E + 2], FAR).then_inc(far_set, 1)
                pool.wait_ge(far_set, 1)

        with ExitStack() as lctx:
            l = lctx.enter_context(nc.Fori(0, DEPTH))

            def at_layer(name):
                return a[name][bass.ds(l, 1)]

            def of_layer(d, name):
                return d[name][0][bass.ds(l, 1)].rearrange("a h p d -> (a h) p d")

            layer_sems = []

            def sem(name):
                layer_sems.append(lctx.enter_context(nc.semaphore(name)))
                return layer_sems[-1]

            full = [sem(f"bank_full{i}") for i in range(8)]
            free = [sem(f"bank_free{i}") for i in range(8)]
            ring_ready = [sem(f"ring_ready{i}") for i in range(NG)]
            down_ready = [sem(f"down_ready{i}") for i in range(ND)]
            dve_step = sem("dve_step")
            stage_ready, stage_sent = sem("stage_ready"), [sem("stage_sent0"), sem("stage_sent1")]
            rows_loaded, bmod_loaded, rows_ready = sem("rows_loaded"), sem("bmod_loaded"), sem("rows_ready")
            xm_ready, xmT_ready = sem("xm_ready"), sem("xmT_ready")
            h_dve, h_act, rope_done, qkT_ready = sem("h_dve"), sem("h_act"), sem("rope_done"), sem("qkT_ready")
            ctx_loaded, kctxT_ready = sem("ctx_loaded"), sem("kctxT_ready")
            bias_loaded, bias_masked = sem("bias_loaded"), sem("bias_masked")
            small_ready, gn_ready = sem("small_ready"), sem("gn_ready")
            dneg_ready, softplus_ready, lg_ready = sem("dneg_ready"), sem("softplus_ready"), sem("lg_ready")
            act_step = sem("act_step")
            decay_raw, decay_cut, decay_ready = sem("decay_raw"), sem("decay_cut"), sem("decay_ready")
            pa_ready, zeta_ready, kz_ready = sem("pa_ready"), sem("zeta_ready"), sem("kz_ready")
            qx_raw, qx_ready, state_ready = sem("qx_raw"), sem("qx_ready"), sem("state_ready")
            var_ready, root_ready, gate_ready, ya_written = sem("var_ready"), sem("root_ready"), sem("gate_ready"), sem("ya_written")
            neg_ready, sinkx_ready, exp_done = sem("neg_ready"), sem("sinkx_ready"), sem("exp_done")
            probT_ready, y_written, yT_ready = sem("probT_ready"), sem("y_written"), sem("yT_ready")
            b_ready, x_ready, lvar_ready, lroot_ready = sem("b_ready"), sem("x_ready"), sem("lvar_ready"), sem("lroot_ready")
            wr_loaded, xm_saved, score_ready, mask_ready = sem("wr_loaded"), sem("xm_saved"), sem("score_ready"), sem("mask_ready")
            most_ready, xg_zeroed = sem("most_ready"), sem("xg_zeroed")
            table_empty, entries_ready, entries_sent, table_loaded = (
                sem("table_empty"), sem("entries_ready"), sem("entries_sent"), sem("table_loaded"))
            ssilu_done, shid_ready, shT_ready = sem("ssilu_done"), sem("shid_ready"), sem("shT_ready")
            caches_stored, states_stored, experts_done = sem("caches_stored"), sem("states_stored"), sem("experts_done")
            back = [sem("rows_back0"), sem("rows_back1")]
            idx_seen = sem("idx_seen")

            def pass_sems(tag):
                return {n: sem(f"{n}_{tag}") for n in
                        ("slots_ready", "gathered0", "gathered1", "xT_full", "xT_ready",
                         "wh_ready", "wl_ready", "half_used", "xh_ready", "silu_done", "hid_ready", "hT_full", "hT_ready", "y_full", "ys_ready",
                         "scattered0", "scattered1", "ring_in0", "ring_in1", "ring_in2", "ring_in3", "down_in0",
                         "down_in1", "idx_set", "pass_done")}

            MAIN, OVER = pass_sems("main"), pass_sems("over")
            for i in range(NG):
                MAIN[f"ring_in{i}"] = ring_ready[i]
            for i in range(ND):
                MAIN[f"down_in{i}"] = down_ready[i]
            bctx = ExitStack()
            blk = bctx.enter_context(nc.Block())

            def done(eng, name):
                b, n = groups[name]
                eng.wait_ge(full[b], n + 1)
                return psum[b]

            def give(ins, name):
                ins.then_inc(free[groups[name][0]], 1)

            HG = [(n, t) for n in range(INC) for t in range(TILES)]
            h_on_act = sum(i % 2 for i in range(len(HG)))
            h_on_dve = len(HG) - h_on_act
            soft_of = {g: s for g, s in enumerate(soft)}
            last_c1 = max(g for g, s in enumerate(soft) if s[:2] == ("C", 1))
            ring_base = [(CHUNKS - i + NG - 1) // NG for i in range(NG)]
            down_base = [1, 0]

            def ring_view(i):
                return ring[i][:].rearrange("p (k n) -> p k n", k=KD)

            @blk.sync
            def _(sp):
                last_use = ([("mod", i) for i in range(MODC)] + [("h", i, 2) for i in range(INC)] +
                            [("y", i, 2) for i in range(OUTC)] + [("sgu", 2)])

                def load_chunk(n, src, w=CH):
                    s = n % NG
                    if n >= NG:
                        done(sp, last_use[n - NG])
                    sp.dma_start(ring_view(s)[:, :, 0:w], src).then_inc(ring_ready[s], 16)

                def chunks(name):
                    return at_layer(name).rearrange("a (k p) n -> p (a k) n", p=P)

                for i in range(MODC):
                    load_chunk(i, chunks("w_mod")[:, :, CH * i:CH * i + CH])
                    if i == 1:
                        bm = at_layer("b_mod").rearrange("a (r d) -> (a r) d", r=6)
                        for c_ in range(2):
                            sp.dma_start(bmod[c_:12:2, :], bm).then_inc(bmod_loaded, 16)
                        for r, name in enumerate(("ln1_g", "ln1_b", "ln2_g", "ln2_b")):
                            sp.dma_start(rows[LN_ROW + r:LN_ROW + r + 1, :], at_layer(name)).then_inc(rows_loaded, 16)
                        at = 0
                        for name, w in (("ret_gn_g", 256), ("ret_gn_b", 256), ("b_router", E), ("win_sink", H_B),
                                        ("ret_decay_fwd", H_A), ("ret_decay_bwd", H_A)):
                            sp.dma_start(rows[SMALL_ROW:SMALL_ROW + 1, at:at + w], at_layer(name)).then_inc(rows_loaded, 16)
                            at += w
                    if i == 5:
                        at, n = CONSTS["empty"]
                        for t in range(TILES):
                            sp.dma_start(slots.rearrange("(t p e) v -> t p (e v)", p=P, e=E)[t], a["consts"][:, at:at + n]).then_inc(table_empty, 16)
                        kv = kctx.rearrange("p (h d) -> p h d", d=HD)
                        wk, nk = of_layer(a, "cache_win_k"), of_layer(a, "cache_na_k")
                        sp.dma_start(kv[:, 0:2, :], wk.rearrange("h p d -> p h d")).then_inc(ctx_loaded, 16)
                        sp.dma_start(kv[:, 2, :], wk[1]).then_inc(ctx_loaded, 16)
                        sp.dma_start(kv[:, 3, :], wk[0]).then_inc(ctx_loaded, 16)
                        sp.dma_start(kv[:, 4:10, :], nk.rearrange("h p d -> p h d")).then_inc(ctx_loaded, 16)
                        sp.dma_start(vctx[:, 0:2, :], of_layer(a, "cache_win_v").rearrange("h p d -> p h d")).then_inc(ctx_loaded, 16)
                        sp.dma_start(vctx[:, 2:8, :], of_layer(a, "cache_na_v").rearrange("h p d -> p h d")).then_inc(ctx_loaded, 16)
                        for r, name in enumerate(("state_ret_fwd", "state_ret_bwd")):
                            st = of_layer(a, name)
                            for g in range(2):
                                sp.dma_start(s0[:, r, g, :], st[2 * g:2 * g + 2].rearrange("h d e -> (h d) e")).then_inc(ctx_loaded, 16)

                def load_bias(t):
                    rp = at_layer("na_rpb")
                    for rr in range(2):
                        r = 2 * t + 1 - rr
                        for hh in range(H_C):
                            src = bass.AP(rp.tensor, rp.offset + (hh * 15 * 31 + (7 - r) * 31 + 15 - 63), [[1, 64], [31, 4], [1, 64]])
                            sp.dma_start(nab[64 * rr:64 * rr + 64, hh, :].rearrange("p (r c) -> p r c", r=4), src).then_inc(bias_loaded, 16)

                load_bias(0)
                for i in range(INC):
                    w = min(CH, W_IN - CH * i)
                    load_chunk(MODC + i, chunks("w_in")[:, :, CH * i:CH * i + w], w)
                for i in range(OUTC):
                    load_chunk(MODC + INC + i, chunks("w_out")[:, :, CH * i:CH * i + CH])
                sp.wait_ge(h_dve, h_on_dve)
                sp.wait_ge(h_act, h_on_act)
                for name, col, nh in (("new_win_k", KB, 2), ("new_win_v", VB, 2), ("new_na_k", KC, 6), ("new_na_v", VC, 6)):
                    sp.dma_start(of_layer(o, name).rearrange("h p d -> p h d"),
                                 h[:, 0, col:col + nh * HD].rearrange("p (h d) -> p h d", d=HD)).then_inc(caches_stored, 16)
                sp.wait_ge(state_ready, 1)
                for r, name in enumerate(("new_fwd", "new_bwd")):
                    sp.dma_start(of_layer(o, name).rearrange("h d e -> d h e"),
                                 stout[0:64, 256 * r:256 * r + 256].rearrange("p (h e) -> p h e", h=H_A)).then_inc(states_stored, 16)
                done(sp, ("s", last_c1, 2))
                load_bias(1)
                load_chunk(CHUNKS - 1, chunks("w_shared_gu"))
                sp.wait_ge(yT_ready, 8)
                sp.wait_ge(caches_stored, 64)
                sp.wait_ge(states_stored, 32)
                sp.dma_start(down[0], at_layer("w_shared_down").rearrange("a (k p) n -> p (a k) n", p=P)).then_inc(down_ready[0], 16)
                sp.dma_start(wr, at_layer("w_router").rearrange("a (k p) e -> p (a k) e", p=P)).then_inc(wr_loaded, 16)

                def expert_loads(S, q):
                    gu_v, dn_v = at_layer("w_expert_gu"), at_layer("w_expert_down")
                    b = q * E

                    def gu(i, e):
                        sp.dma_start(ring_view(i), gu_v[:, bass.ds(e, 1)].rearrange("a b (k p) n -> p (a b k) n", p=P)
                                     ).then_inc(S[f"ring_in{i}"], 16)

                    def dn(i, e):
                        sp.dma_start(down[i], dn_v[:, bass.ds(e, 1)].rearrange("a b (k p) n -> p (a b k) n", p=P)
                                     ).then_inc(S[f"down_in{i}"], 16)

                    for e in (1, 2, 3, 0):
                        if S is MAIN:
                            done(sp, last_use[max(n for n in range(CHUNKS) if n % NG == e)])
                        gu(e, e)
                        if e < ND:
                            if S is MAIN and e == 0:
                                done(sp, ("sy", 2, 1))
                            dn(e, e)

                    def turn_of_loads(it):
                        for i in range(UN):
                            sp.wait_ge(S["half_used"], it * (2 * UN) + 2 * (b + i - NG + 1))
                            gu(i, it * UN + i)
                            if isinstance(it, int) and i == 0:
                                continue
                            sp.wait_ge(S["y_full"], it * UN + (b + i - 4))
                            dn((i + 1) % ND, it * UN + (i - 3))

                    turn_of_loads(1)
                    with sp.Fori(2, E // UN) as it:
                        turn_of_loads(it)
                    for e in (E - 3, E - 2, E - 1):
                        sp.wait_ge(S["y_full"], b + e - 1)
                        dn(e % ND, e)

                sp.wait_ge(xm_ready, 2)
                sp.dma_start(scratch_x.rearrange("(t p) d -> p t d", p=P), xm).then_inc(xm_saved, 16)
                expert_loads(MAIN, 0)
                sp.wait_ge(most_ready, 1)
                with sp.If(sp.value_load(most[0:1, 0:1], min_val=0, max_val=TOK) > P):
                    sp.wait_ge(MAIN["pass_done"], 1)
                    expert_loads(OVER, 0)
                    sp.wait_ge(OVER["pass_done"], 1)
                    expert_loads(OVER, 1)
                    sp.nop()
                sp.wait_ge(experts_done, 1)
                for t in range(TILES):
                    if t == 2:
                        sp.wait_ge(x_ready, 4)
                    src = scratch_y.rearrange("(t p k) d -> t p k d", p=P, k=TOPK)[t]
                    s = 2 * (t % 2)
                    sp.dma_start(ring[s][:].rearrange("p (k d) -> p k d", d=DM), src[:, 0:4, :]).then_inc(back[t % 2], 16)
                    sp.dma_start(ring[s + 1][:].rearrange("p (k d) -> p k d", d=DM)[:, 0:2, :], src[:, 4:6, :]).then_inc(back[t % 2], 16)
                for s in range(2):
                    sp.wait_ge(back[s], 64 - 32 * s)

            @blk.tensor
            def _(pe):
                turn = iter(order)
                ident, flip, ones, before = const("ident"), const("flip"), const("ones"), const("before")

                def begin(name):
                    assert next(turn) == name, name
                    b, n = groups[name]
                    if n > 0:
                        pe.wait_ge(free[b], n)
                    return psum[b]

                def end(ins, name):
                    ins.then_inc(full[groups[name][0]], 1)

                def chunk(n):
                    pe.wait_ge(ring_ready[n % NG], 16 * (n // NG + 1))
                    return ring_view(n % NG)

                def spread(name, row, c0, n, k=16):
                    bank = begin(name)
                    end(pe.matmul(bank[:, 0:n], ident[0:k, row:row + 1].to_broadcast([k, P]), rows[0:k, c0:c0 + n],
                                  start=True, stop=True), name)

                def spread_mod(which):
                    sc, sh = (mod_row["sc1"], mod_row["sh1"]) if which == 0 else (mod_row["sc2"], mod_row["sh2"])
                    for c_ in range(2):
                        for f in range(2):
                            spread(("m", which, c_, f, 0), sc + c_, CH * f, CH)
                            spread(("m", which, c_, f, 1), sh + c_, CH * f, CH)

                def spread_norm(which):
                    g = mod_row["g1"] if which == 0 else mod_row["g2"]
                    for r, row in enumerate((g, g + 1, LN_ROW + 2 * which, LN_ROW + 2 * which + 1)):
                        for f in range(2):
                            spread(("b", which, r, f), row, CH * f, CH)

                def turn_x(which):
                    for t in range(TILES):
                        for g in range(2):
                            name = ("xT", which, t, g)
                            bank = begin(name)
                            for k in range(4):
                                ins = pe.transpose(bank[:, P * k:P * k + P], xm[:, t, P * (4 * g + k):P * (4 * g + k + 1)], ident)
                            end(ins, name)

                for n in range(MODC):
                    w = chunk(n)
                    bank = begin(("mod", n))
                    for k in range(KD):
                        ins = pe.matmul(bank[0:2, :], condT[:, k, :], w[:, k, :], start=(k == 0), stop=(k == KD - 1))
                    end(ins, ("mod", n))
                pe.wait_ge(rows_ready, 1)
                pe.wait_ge(rows_loaded, 160)
                spread(("small",), SMALL_ROW, 512, E + 14, 17)
                spread(("gn",), SMALL_ROW, 0, 512, 17)
                spread_mod(0)
                pe.wait_ge(xm_ready, 1)
                turn_x(0)
                pe.wait_ge(xmT_ready, 6)
                for n, t in HG:
                    w = chunk(MODC + n)
                    cols = min(CH, W_IN - CH * n)
                    bank = begin(("h", n, t))
                    for k in range(KD):
                        ins = pe.matmul(bank[:, 0:cols], xmT[:, k, P * t:P * t + P], w[:, k, 0:cols],
                                        start=(k == 0), stop=(k == KD - 1))
                    end(ins, ("h", n, t))
                pe.wait_ge(rope_done, 1)
                pe.wait_ge(h_act, h_on_act)
                qk_cols = [QA, QA + P, KA, KA + P, QB, QB + P, QB + 2 * P, KB, None, QC, QC + P, QC + 2 * P, KC, KC + P, KC + 2 * P]
                for b, col in enumerate(qk_cols):
                    bank = begin(("qkT", b))
                    for t in range(TILES):
                        src = ksw[:, t, :] if col is None else h[:, t, col:col + P]
                        ins = pe.transpose(bank[:, P * t:P * t + P], src, ident)
                    end(ins, ("qkT", b))
                pe.wait_ge(ctx_loaded, 160)
                for g, blocks in enumerate((range(4), range(4, 5))):
                    bank = begin(("kctxT", g))
                    for i, b in enumerate(blocks):
                        ins = pe.transpose(bank[:, P * i:P * i + P], kctx[:, P * b:P * b + P], ident)
                    end(ins, ("kctxT", g))
                pe.wait_ge(qkT_ready, 15)
                pe.wait_ge(kctxT_ready, 2)
                for hh in range(H_A):
                    p0, g = 64 * (hh % 2), hh // 2
                    q, k = qkT[p0:p0 + 64, g, :], qkT[p0:p0 + 64, 2 + g, :]
                    bank = begin(("sA", hh, 0))
                    pe.matmul(bank[:, 0:P], k[:, 0:P], q[:, 0:P], start=True, stop=True)
                    end(pe.matmul(bank[:, P:3 * P], k[:, P:2 * P], q[:, P:3 * P], start=True, stop=True), ("sA", hh, 0))
                    bank = begin(("sA", hh, 1))
                    end(pe.matmul(bank[:, 0:2 * P], k[:, 2 * P:3 * P], q[:, P:3 * P], start=True, stop=True), ("sA", hh, 1))
                for hh in range(H_A):
                    p0, g = 64 * (hh % 2), hh // 2
                    va = [h[:, t, VA + HD * hh:VA + HD * hh + HD] for t in range(TILES)]
                    bank = begin(("oA", hh))
                    pe.wait_ge(pa_ready, hh + 1)
                    pe.matmul(bank[:, 0:HD], pa[:, 0:P], va[0], start=True, stop=True)
                    pe.wait_ge(qx_ready, 1)
                    for t in (1, 2):
                        out = bank[:, HD * t:HD * t + HD]
                        pe.matmul(out, pa[:, P * t:P * t + P], va[1], start=True, stop=False)
                        pe.matmul(out, pa[:, P * (t + 2):P * (t + 2) + P], va[2], start=False, stop=False)
                        for r in range(2):
                            ins = pe.matmul(out, qx[p0:p0 + 64, r, g, P * (t - 1):P * t], s0[p0:p0 + 64, r, g, :],
                                            start=False, stop=(r == 1))
                    end(ins, ("oA", hh))
                bank = begin(("state",))
                pe.wait_ge(kz_ready, 1)
                for r in range(2):
                    for hh in range(H_A):
                        ins = pe.matmul(bank[0:64, HD * (4 * r + hh):HD * (4 * r + hh + 1)], kz[:, r, hh, :],
                                        h[:, 0, VA + HD * hh:VA + HD * hh + HD], start=True, stop=True)
                end(ins, ("state",))

                def scores(g):
                    m, t, h0 = soft[g]
                    if m == "C" and t > 0:
                        pe.wait_ge(bias_masked, t)
                    for i in range(3):
                        hh = h0 + i
                        p0 = 64 * (hh % 2)
                        if m == "B":
                            same = hh // 3 == hh % 2
                            qb, kb, cb = 4 + hh // 2, 7 if same else 8, 0 if same else 1
                        else:
                            qb, kb, cb = 9 + hh // 2, 12 + hh // 2, 2 + hh // 2
                        q = qkT[p0:p0 + 64, qb, P * t:P * t + P]
                        k = qkT[p0:p0 + 64, kb, :]
                        bank = begin(("s", g, i))
                        if t == 0:
                            end(pe.matmul(bank[:, 0:P], q, k[:, 0:P], start=True, stop=True), ("s", g, i))
                            continue
                        if m == "B":
                            for j in (0, 1):
                                masked = j == (t == 1)
                                out = bank[:, P * j:P * j + P]
                                pe.matmul(out, q, k[:, P * (j + 1):P * (j + 2)], start=True, stop=not masked)
                                if masked:
                                    pe.matmul(out, ident, const("band_next" if t == 1 else "band_prev"), start=False, stop=True)
                        else:
                            pe.matmul(bank[:, 0:2 * P], q, k[:, P:3 * P], start=True, stop=False)
                            pe.matmul(bank[:, 0:2 * P], flip, nab[:, hh, :], start=False, stop=True)
                        end(pe.matmul(bank[:, 2 * P:3 * P], q, kctxT[p0:p0 + 64, cb, :], start=True, stop=True), ("s", g, i))

                def mix(g):
                    m, t, h0 = soft[g]
                    nb = 1 if t == 0 else 3
                    pe.wait_ge(exp_done, g + 1)
                    for i in range(3):
                        bank = begin(("pT", g, i))
                        for j in range(nb):
                            ins = pe.transpose(bank[:, P * j:P * j + P], prob[:, i, P * j:P * j + P], ident)
                        end(ins, ("pT", g, i))
                    bank = begin(("pv", g))
                    for i in range(3):
                        hh = h0 + i
                        pe.wait_ge(probT_ready, 3 * g + i + 1)
                        for j in range(nb):
                            if j == 2:
                                v = vctx[:, hh // 3 if m == "B" else 2 + hh, :]
                            else:
                                col = VB + HD * (hh // 3) if m == "B" else VC + HD * hh
                                v = h[:, t if t == 0 else j + 1, col:col + HD]
                            ins = pe.matmul(bank[:, HD * i:HD * i + HD], probT[:, i, P * j:P * j + P], v,
                                            start=(j == 0), stop=(j == nb - 1))
                    end(ins, ("pv", g))

                for g in range(len(soft) + 1):
                    if g < len(soft):
                        scores(g)
                    if g:
                        mix(g - 1)
                pe.wait_ge(y_written, len(soft))
                pe.wait_ge(ya_written, 1)
                y_cols = [QA, QA + P, QB, QB + P, QB + 2 * P, QC, QC + P, QC + 2 * P]
                for b, col in enumerate(y_cols):
                    bank = begin(("yT", b))
                    for t in range(TILES):
                        ins = pe.transpose(bank[:, P * t:P * t + P], h[:, t, col:col + P], ident)
                    end(ins, ("yT", b))
                spread_norm(0)
                pe.wait_ge(yT_ready, 8)
                for n in range(OUTC):
                    for t in range(TILES):
                        w = chunk(MODC + INC + n)
                        bank = begin(("y", n, t))
                        for k in range(KD):
                            ins = pe.matmul(bank[:, :], xmT[:, k, P * t:P * t + P], w[:, k, :], start=(k == 0), stop=(k == KD - 1))
                        end(ins, ("y", n, t))
                spread_mod(1)
                spread_norm(1)
                pe.wait_ge(xm_ready, 2)
                turn_x(1)
                pe.wait_ge(xmT_ready, 12)
                pe.wait_ge(wr_loaded, 16)
                bank = begin(("logit",))
                for t in range(TILES):
                    for k in range(KD):
                        ins = pe.matmul(bank[:, E * t:E * t + E], xmT[:, k, P * t:P * t + P], wr[:, k, :],
                                        start=(k == 0), stop=(k == KD - 1))
                end(ins, ("logit",))
                pe.wait_ge(mask_ready, 1)
                bank = begin(("pos",))
                for t in range(TILES):
                    for s in range(t + 1):
                        ins = pe.matmul(bank[:, E * t:E * t + E], ones if s < t else before, mask[:, s, :],
                                        start=(s == 0), stop=(s == t))
                for s in range(TILES):
                    ins = pe.matmul(bank[:, E * TILES:E * TILES + E], ones, mask[:, s, :], start=(s == 0), stop=(s == TILES - 1))
                end(ins, ("pos",))
                w = chunk(CHUNKS - 1)
                for t in range(TILES):
                    bank = begin(("sgu", t))
                    for k in range(KD):
                        ins = pe.matmul(bank[:, :], xmT[:, k, P * t:P * t + P], w[:, k, :], start=(k == 0), stop=(k == KD - 1))
                    end(ins, ("sgu", t))
                pe.wait_ge(down_ready[0], 16)
                for t in range(TILES):
                    pe.wait_ge(shid_ready, t + 1)
                    bank = begin(("shT", t))
                    for k in range(2):
                        ins = pe.transpose(bank[:, P * k:P * k + P], hid_s[t % 2][:, P * k:P * k + P], ident)
                    end(ins, ("shT", t))
                    pe.wait_ge(shT_ready, t + 1)
                    for f in range(2):
                        bank = begin(("sy", t, f))
                        for k in range(2):
                            ins = pe.matmul(bank[:, :], shT[:, k, :], down[0][:, k, CH * f:CH * f + CH], start=(k == 0), stop=(k == 1))
                        end(ins, ("sy", t, f))
                assert next(turn, None) is None
                for b in range(8):
                    pe.wait_ge(free[b], bank_uses[b])

                def expert_pass(S, q):
                    b, bx = q * E, q * (E + 1)

                    def turn_rows(m, half, i):
                        pe.wait_ge(S[f"gathered{i % 2}"], (half + (q * 33 + 1)) * 16)
                        pe.wait_ge(S["xT_ready"], m + (bx + 1))
                        for k in range(KD):
                            ins = pe.transpose(psum[2 + k // 4][:, P * (k % 4):P * (k % 4) + P], xg[i % 2][:, P * k:P * k + P], ident)
                        ins.then_inc(S["xT_full"], 1)

                    def down_rows(it, i):
                        e, s = it * UN + i, i % 2
                        pe.wait_ge(S["hT_ready"], e + (b + 2))
                        pe.wait_ge(S["ys_ready"], e + (b + 1))
                        pe.wait_ge(S[f"down_in{s}"], (it * 2 + (i // 2 + (down_base[s] if S is MAIN else 0) + q * (E // ND) + 1)) * 16)
                        for f in range(2):
                            for k in range(2):
                                ins = pe.matmul(psum[5 + f][:, :], hT[s][:, k, :], down[s][:, k, CH * f:CH * f + CH],
                                                start=(k == 0), stop=(k == 1))
                        ins.then_inc(S["y_full"], 1)

                    def turn_of_experts(it):
                        for i in range(UN):
                            e = it * UN + i
                            pe.wait_ge(S["xT_ready"], e + (bx + 2))
                            pe.wait_ge(S["hid_ready"], e + (b + 1))
                            for j in range(2):
                                pe.wait_ge(S["wl_ready"], e * 2 + (2 * b + j + 1))
                                for k in range(4 * j, 4 * j + 4):
                                    wh, wl = w_hi[j][:, k - 4 * j, :], w_lo[i][:, k, :]
                                    pe.matmul(psum[i % 2][:, :], xT_hi[:, k, :], wh, start=(k == 0), stop=False)
                                    pe.matmul(psum[i % 2][:, :], xT_lo[:, k, :], wh, start=False, stop=False)
                                    ins = pe.matmul(psum[i % 2][:, :], xT_hi[:, k, :], wl, start=False, stop=(k == KD - 1))
                                ins.then_inc(S["half_used"], 1)
                            turn_rows(e + 1, it * 2 + (i + 1) // 2, i + 1)
                            pe.wait_ge(S["hid_ready"], e + (b + 3))
                            pe.wait_ge(S["hT_ready"], e + (b + 1))
                            for k in range(2):
                                ins = pe.transpose(psum[4][:, P * k:P * k + P], hid[:, P * k:P * k + P], ident)
                            ins.then_inc(S["hT_full"], 1)
                            if not (isinstance(it, int) and e == 0):
                                down_rows(it, i - 1)

                    turn_rows(0, 0, 0)
                    turn_of_experts(0)
                    with pe.Fori(1, E // UN) as it:
                        turn_of_experts(it)
                    down_rows(E // UN, -1)

                expert_pass(MAIN, 0)
                pe.wait_ge(most_ready, 1)
                with pe.If(pe.value_load(most[0:1, 0:1], min_val=0, max_val=TOK) > P):
                    expert_pass(OVER, 0)
                    expert_pass(OVER, 1)
                    pe.nop()

            @blk.vector
            def _(dve):
                steps = [0]

                def link(ins):
                    steps[0] += 1
                    ins.then_inc(dve_step, 1)
                    dve.wait_ge(dve_step, steps[0])

                for n in range(MODC):
                    bank = done(dve, ("mod", n))
                    if n >= 2:
                        dve.wait_ge(stage_sent[n % 2], 16 * (n // 2))
                    dve.tensor_copy(stage[n % 2][0:2, :], bank[0:2, :]).then_inc(stage_ready, 1)
                    dve.wait_ge(stage_ready, n + 1)
                    dve.sem_inc(free[groups[("mod", n)][0]], 1)
                dve.wait_ge(bmod_loaded, 32)
                for s in range(2):
                    dve.wait_ge(stage_sent[s], 16 * MODC // 2)
                dve.tensor_tensor(rows[0:12, :], raw[0:12, :], bmod[0:12, :], ALU.add).then_inc(rows_ready, 1)
                bank = done(dve, ("small",))
                link(dve.tensor_copy(small[:, 0:E + 14], bank[:, 0:E + 14]))
                dve.sem_inc(free[groups[("small",)][0]], 1)
                dec = small[:, DEC:DEC + 8]
                link(dve.tensor_scalar(dneg, dec, -1.0, None, ALU.mult))
                dve.tensor_tensor(dneg, dneg, dec, ALU.min).then_inc(dneg_ready, 1)
                dve.wait_ge(softplus_ready, 1)
                link(dve.tensor_scalar(zeta, dec, 0.0, None, ALU.min))
                dve.tensor_tensor(lg, zeta, lg, ALU.subtract).then_inc(lg_ready, 1)

                def modulate(which):
                    for c_ in range(2):
                        for f in range(2):
                            bank = done(dve, ("m", which, c_, f, 0))
                            cols = slice(CH * f, CH * f + CH)
                            tiles = (0,) if c_ == 0 else (1, 2)
                            for t in tiles:
                                ins = dve.scalar_tensor_tensor(out=xm[:, t, cols], in0=bank[:, :], scalar=1.0, in1=x[:, t, cols],
                                                               op0=ALU.add, op1=ALU.mult)
                            give(ins, ("m", which, c_, f, 0))
                            bank = done(dve, ("m", which, c_, f, 1))
                            dve.wait_ge(free[groups[("m", which, c_, f, 0)][0]], groups[("m", which, c_, f, 0)][1] + 1)
                            for t in tiles:
                                ins = dve.tensor_tensor(xm[:, t, cols], xm[:, t, cols], bank[:, :], ALU.add)
                            give(ins, ("m", which, c_, f, 1))
                    name = ("m", which, 1, 1, 1)
                    dve.wait_ge(free[groups[name][0]], groups[name][1] + 1)
                    dve.sem_inc(xm_ready, 1)

                modulate(0)
                for i, (n, t) in enumerate(HG):
                    if i % 2 == 0:
                        cols = min(CH, W_IN - CH * n)
                        bank = done(dve, ("h", n, t))
                        give(dve.tensor_copy(h[:, t, CH * n:CH * n + cols], bank[:, 0:cols]), ("h", n, t))
                        dve.wait_ge(free[groups[("h", n, t)][0]], groups[("h", n, t)][1] + 1)
                        dve.sem_inc(h_dve, 1)
                dve.wait_ge(h_act, h_on_act)
                rt = prob.rearrange("p i k -> p (i k)")
                r1, r2, r3, r4 = (rt[:, 256 * i:256 * i + 256].rearrange("p (h d) -> p h d", h=8) for i in range(4))
                for t in (1, 2):
                    v = h[:, t, QB:QB + 512].rearrange("p (h s d) -> p h s d", h=8, s=2)
                    x1, x2 = v[:, :, 0, :], v[:, :, 1, :]
                    cos = const("cos")[:, 32 * (t - 1):32 * t].unsqueeze(1).to_broadcast([P, 8, 32])
                    sin = const("sin")[:, 32 * (t - 1):32 * t].unsqueeze(1).to_broadcast([P, 8, 32])
                    dve.tensor_tensor(r1, x1, cos, ALU.mult)
                    dve.tensor_tensor(r2, x2, sin, ALU.mult)
                    dve.tensor_tensor(r3, x1, sin, ALU.mult)
                    link(dve.tensor_tensor(r4, x2, cos, ALU.mult))
                    dve.tensor_tensor(x1, r1, r2, ALU.subtract)
                    link(dve.tensor_tensor(x2, r3, r4, ALU.add))
                link(dve.tensor_copy(ksw[:, :, 0:HD], h[:, :, KB + HD:KB + 2 * HD]))
                dve.tensor_copy(ksw[:, :, HD:2 * HD], h[:, :, KB:KB + HD]).then_inc(rope_done, 1)
                for b in range(15):
                    bank = done(dve, ("qkT", b))
                    s = SCALE if b in (4, 5, 6, 9, 10, 11) else 1.0
                    give(dve.tensor_scalar(qkT[:, b, :], bank[:, 0:TOK], s, None, ALU.mult), ("qkT", b))
                    dve.wait_ge(free[groups[("qkT", b)][0]], groups[("qkT", b)][1] + 1)
                    dve.sem_inc(qkT_ready, 1)
                dve.wait_ge(zeta_ready, 1)
                for r in range(2):
                    ins = dve.tensor_tensor(kz[:, r], h[:, 0, KA:KA + 256].rearrange("p (h d) -> p h d", h=H_A),
                                            zeta[:, 4 * r:4 * r + 4].unsqueeze(2).to_broadcast([P, H_A, HD]), ALU.mult)
                ins.then_inc(kz_ready, 1)
                dve.wait_ge(qx_raw, 1)
                for r in range(2):
                    ins = dve.tensor_tensor(qx[:, r], qx[:, r], qkT[:, 0:2, P:3 * P], ALU.mult)
                ins.then_inc(qx_ready, 1)
                for hh in range(H_A):
                    dve.wait_ge(decay_cut, hh + 1)
                    if hh:
                        done(dve, ("oA", hh - 1))
                    dve.tensor_tensor(decay, decay_f, decay_b, ALU.add).then_inc(decay_ready, 1)
                    dve.wait_ge(decay_ready, hh + 1)
                    bank = done(dve, ("sA", hh, 0))
                    link(dve.scalar_tensor_tensor(out=pa[:, 0:P], in0=bank[:, 0:P], scalar=SCALE, in1=decay[:, P:2 * P],
                                                  op0=ALU.mult, op1=ALU.mult))
                    give(dve.scalar_tensor_tensor(out=pa[:, P:3 * P], in0=bank[:, P:3 * P], scalar=SCALE, in1=decay[:, P:3 * P],
                                                  op0=ALU.mult, op1=ALU.mult), ("sA", hh, 0))
                    bank = done(dve, ("sA", hh, 1))
                    link(dve.scalar_tensor_tensor(out=pa[:, 3 * P:5 * P], in0=bank[:, 0:2 * P], scalar=SCALE, in1=decay[:, 0:2 * P],
                                                  op0=ALU.mult, op1=ALU.mult))
                    dve.sem_inc(free[groups[("sA", hh, 1)][0]], 1)
                    dve.sem_inc(pa_ready, 1)
                    bank = done(dve, ("oA", hh))
                    link(dve.tensor_copy(oA[:, :, hh, :], bank[:, 0:TILES * HD].rearrange("p (t d) -> p t d", t=TILES)))
                    dve.sem_inc(free[groups[("oA", hh)][0]], 1)
                bank = done(dve, ("state",))
                link(dve.tensor_scalar(stout[0:64, :], bank[0:64, :], SCALE, None, ALU.mult))
                dve.sem_inc(free[groups[("state",)][0]], 1)
                dve.sem_inc(state_ready, 1)
                ov = oA.rearrange("p t h d -> p (t h) d")
                tv = tmp.rearrange("p (g d) -> p g d", d=HD)
                link(dve.tensor_reduce(mean, ov, AX.X, ALU.add))
                link(dve.tensor_scalar(mean, mean, 1.0 / HD, None, ALU.mult))
                link(dve.tensor_tensor(ov, ov, mean.unsqueeze(2).to_broadcast([P, 12, HD]), ALU.subtract))
                link(dve.tensor_tensor(tv, ov, ov, ALU.mult))
                link(dve.tensor_reduce(var, tv, AX.X, ALU.add))
                dve.tensor_scalar(var, var, 1.0 / HD, EPS, ALU.mult, ALU.add).then_inc(var_ready, 1)
                dve.wait_ge(root_ready, 1)
                link(dve.reciprocal(var, var))
                link(dve.tensor_tensor(ov, ov, var.unsqueeze(2).to_broadcast([P, 12, HD]), ALU.mult))
                o2 = oA.rearrange("p t h d -> p t (h d)")
                dve.wait_ge(gn_ready, 1)
                link(dve.tensor_tensor(o2, o2, gn[:, 0:256].unsqueeze(1).to_broadcast([P, TILES, 256]), ALU.mult))
                link(dve.tensor_tensor(o2, o2, gn[:, 256:512].unsqueeze(1).to_broadcast([P, TILES, 256]), ALU.add))
                dve.wait_ge(gate_ready, 1)
                dve.tensor_tensor(h[:, :, QA:QA + 256], o2, h[:, :, GA:GA + 256], ALU.mult).then_inc(ya_written, 1)

                def peak(g):
                    m, t, h0 = soft[g]
                    nk = P if t == 0 else 3 * P
                    c3 = slice(3 * g, 3 * g + 3)
                    for i in range(3):
                        bank = done(dve, ("s", g, i))
                        ins = dve.tensor_reduce(mx[:, 3 * g + i:3 * g + i + 1], bank[:, 0:nk], AX.X, ALU.max)
                    link(ins)
                    if m == "B":
                        link(dve.tensor_tensor(mx[:, c3], mx[:, c3], small[:, SINK + h0:SINK + h0 + 3], ALU.max))
                    dve.tensor_scalar(neg[:, c3], mx[:, c3], -1.0, None, ALU.mult).then_inc(neg_ready, 1)
                    if m == "B":
                        dve.wait_ge(neg_ready, g + 1)
                        dve.tensor_tensor(sinkx[:, c3], neg[:, c3], small[:, SINK + h0:SINK + h0 + 3], ALU.add).then_inc(sinkx_ready, 1)

                def weigh(g):
                    m, t, h0 = soft[g]
                    c3 = slice(3 * g, 3 * g + 3)
                    dve.wait_ge(exp_done, g + 1)
                    if m == "B":
                        link(dve.tensor_tensor(den[:, c3], den[:, c3], sinke[:, c3], ALU.add))
                    link(dve.reciprocal(recip[:, c3], den[:, c3]))
                    bank = done(dve, ("pv", g))
                    col = (QB if m == "B" else QC) + HD * h0
                    link(dve.tensor_tensor(h[:, t, col:col + 3 * HD].rearrange("p (i d) -> p i d", i=3),
                                           bank[:, 0:3 * HD].rearrange("p (i d) -> p i d", i=3),
                                           recip[:, c3].unsqueeze(2).to_broadcast([P, 3, HD]), ALU.mult))
                    dve.sem_inc(free[groups[("pv", g)][0]], 1)
                    dve.sem_inc(y_written, 1)

                for g in range(len(soft) + 1):
                    if g < len(soft):
                        peak(g)
                    if g:
                        weigh(g - 1)

                def norm(which, t, source):
                    c_ = 0 if t == 0 else 1
                    z = xm[:, t, :]
                    source(z, gateb[:, c_, :])
                    link(dve.scalar_tensor_tensor(out=z, in0=x[:, t, :], scalar=ALPHA, in1=z, op0=ALU.mult, op1=ALU.add))
                    for f in range(2):
                        ins = dve.bn_stats(bn[:, 6 * f:6 * f + 6], z[:, CH * f:CH * f + CH])
                    link(ins)
                    link(dve.bn_aggr(bnag, bn))
                    dve.tensor_scalar(rstd, bnag[:, 1:2], EPS, None, ALU.add).then_inc(lvar_ready, 1)
                    dve.wait_ge(lroot_ready, TILES * which + t + 1)
                    link(dve.reciprocal(rstd, rstd))
                    link(dve.tensor_scalar(z, z, bnag[:, 0:1], rstd, ALU.subtract, ALU.mult))
                    link(dve.tensor_tensor(z, z, lnb[:, 0, :], ALU.mult))
                    dve.tensor_tensor(x[:, t, :], z, lnb[:, 1, :], ALU.add).then_inc(x_ready, 1)

                dve.wait_ge(caches_stored, 64)
                dve.wait_ge(b_ready, 8)
                for t in range(TILES):
                    def from_psum(z, g, t=t):
                        for n in range(OUTC):
                            bank = done(dve, ("y", n, t))
                            cols = slice(CH * n, CH * n + CH)
                            link(dve.tensor_tensor(z[:, cols], bank[:, :], g[:, cols], ALU.mult))
                            dve.sem_inc(free[groups[("y", n, t)][0]], 1)
                    norm(0, t, from_psum)
                dve.wait_ge(x_ready, TILES)
                modulate(1)
                link(dve.memset(sel[:, :, E:E + 2], BIG))
                link(dve.memset(grp[:, :, 8:12], BIG))
                dve.wait_ge(score_ready, 1)
                link(dve.tensor_tensor(sel[:, :, 0:E], score, small[:, 0:E].unsqueeze(1).to_broadcast([P, TILES, E]), ALU.add))
                for t in range(TILES):
                    for g in range(8):
                        ins = dve.max(top[:, 8 * t + g, :], sel[:, t, 8 * g:8 * g + 8])
                link(ins)
                topv = top.rearrange("p (t g) e -> p t g e", t=TILES)
                link(dve.tensor_tensor(grp[:, :, 0:8], topv[:, :, :, 0], topv[:, :, :, 1], ALU.add))
                for t in range(TILES):
                    link(dve.max(top8[:, t, :], grp[:, t, :]))
                    ins = dve.match_replace(grp2[:, t, :], top8[:, t, :], grp[:, t, :], MARK)
                link(ins)
                link(dve.tensor_scalar(grp2[:, :, 0:8], grp2[:, :, 0:8], MARK, None, ALU.is_equal))
                kept = grp2[:, :, 0:8].unsqueeze(3).to_broadcast([P, TILES, 8, 8])
                for t in range(TILES):
                    s8 = sel[:, t, 0:E].rearrange("p (g e) -> p g e", g=8)
                    link(dve.tensor_tensor(s8, s8, kept[:, t], ALU.mult))
                link(dve.tensor_scalar(grp[:, :, 0:8], grp2[:, :, 0:8], -NEG, NEG, ALU.mult, ALU.add))
                for t in range(TILES):
                    s8 = sel[:, t, 0:E].rearrange("p (g e) -> p g e", g=8)
                    link(dve.tensor_tensor(s8, s8, grp[:, t, 0:8].unsqueeze(2).to_broadcast([P, 8, 8]), ALU.add))
                for t in range(TILES):
                    link(dve.max(top8[:, t, :], sel[:, t, :]))
                    ins = dve.match_replace(sel2[:, t, :], top8[:, t, :], sel[:, t, :], MARK)
                link(ins)
                dve.tensor_scalar(mask, sel2[:, :, 0:E], MARK, None, ALU.is_equal).then_inc(mask_ready, 1)
                dve.wait_ge(mask_ready, 1)
                link(dve.tensor_tensor(score, score, mask, ALU.mult))
                link(dve.tensor_reduce(wsum[:, 0:TILES], score, AX.X, ALU.add))
                link(dve.reciprocal(wsum[:, 0:TILES], wsum[:, 0:TILES]))
                link(dve.tensor_tensor(score, score, wsum[:, 0:TILES].unsqueeze(2).to_broadcast([P, TILES, E]), ALU.mult))
                link(dve.tensor_scalar(score, score, ROUTE_SCALE, None, ALU.mult))
                for t in range(TILES):
                    link(dve.tensor_tensor_scan(rank[:, t, :], const("ones")[:, 0:E], mask[:, t, :], 0.0, ALU.mult, ALU.add))
                link(dve.tensor_tensor(rank, rank, mask, ALU.mult))
                full_shape = [P, TILES, TOPK, E]
                link(dve.tensor_tensor(of_rank, rank.unsqueeze(2).to_broadcast(full_shape),
                                       const("from_start")[:, 0:TOPK].unsqueeze(1).unsqueeze(3).to_broadcast(full_shape), ALU.is_equal))
                dve.tensor_tensor(picked, of_rank, score.unsqueeze(2).to_broadcast(full_shape), ALU.mult)
                link(dve.tensor_copy(entry, const("tok_row").rearrange("p (j v) -> p j v", v=3)))
                link(dve.tensor_reduce(entry[:, :, 2], picked.rearrange("p t k e -> p (t k) e"), AX.X, ALU.add))
                bank = done(dve, ("pos",))
                pos = bank[:, 0:TILES * E].rearrange("p (t e) -> p t e", t=TILES)
                link(dve.scalar_tensor_tensor(out=posm, in0=pos, scalar=1.0 * E, in1=const("slot")[:, 0:E].unsqueeze(1).to_broadcast([P, TILES, E]),
                                              op0=ALU.mult, op1=ALU.add))
                link(dve.tensor_tensor(picked, of_rank, posm.unsqueeze(2).to_broadcast(full_shape), ALU.mult))
                link(dve.tensor_reduce(place, picked.rearrange("p t k e -> p (t k) e"), AX.X, ALU.add))
                dve.tensor_copy(place_i[:], place).then_inc(entries_ready, 1)
                link(dve.tensor_reduce(wsum[:, 4:5], bank[:, TILES * E:TILES * E + E], AX.X, ALU.max))
                dve.sem_inc(free[groups[("pos",)][0]], 1)
                dve.tensor_copy(most[:, 0:1], wsum[:, 4:5]).then_inc(most_ready, 1)
                def shared_tail(t):
                    bank = done(dve, ("shT", t))
                    link(dve.tensor_copy(shT, bank[:, 0:2 * P].rearrange("p (k t) -> p k t", k=2)))
                    dve.sem_inc(free[groups[("shT", t)][0]], 1)
                    dve.sem_inc(shT_ready, 1)
                    dve.wait_ge(xm_saved, 16)
                    for f in range(2):
                        bank = done(dve, ("sy", t, f))
                        give(dve.tensor_copy(xm[:, t, CH * f:CH * f + CH], bank[:, :]), ("sy", t, f))

                for t in range(TILES):
                    bank = done(dve, ("sgu", t))
                    dve.wait_ge(ssilu_done, t + 1)
                    if t >= 2:
                        done(dve, ("shT", t - 2))
                    link(dve.tensor_tensor(hid_s[t % 2], sg_s[t], bank[:, F:2 * F], ALU.mult))
                    dve.sem_inc(free[groups[("sgu", t)][0]], 1)
                    dve.sem_inc(shid_ready, 1)
                    if t:
                        shared_tail(t - 1)
                shared_tail(TILES - 1)

                def expert_pass(S, q, p):
                    b, bx = q * E, q * (E + 1)
                    if p:
                        dve.wait_ge(MAIN["pass_done"], 1)
                    if q:
                        dve.wait_ge(S["pass_done"], q)
                    else:
                        dve.sem_inc(S["hid_ready"], 2)
                        dve.sem_inc(S["hT_ready"], 1)
                        dve.sem_inc(S["ys_ready"], 1)
                        dve.sem_inc(S["xT_ready"], 1)
                    dve.wait_ge(table_loaded, 16)
                    dve.tensor_copy(slot_idx[:, :, 0:E], table[:, p, :, 0:2].rearrange("p e v -> p v e"))
                    dve.tensor_copy(slot_w[:], table[:, p, :, 2]).then_inc(S["slots_ready"], 1)
                    dve.wait_ge(S["slots_ready"], q + 1)

                    def rows_out(it, i):
                        s = i % 2
                        dve.wait_ge(S["y_full"], it * UN + (b + i + 1))
                        if not (isinstance(it, int) and it * UN + i < 2):
                            dve.wait_ge(S[f"scattered{s}"], (it * 2 + (i // 2 + q * (E // 2))) * 16)
                        dve.tensor_copy(ys[s][:, 0:CH], psum[5][:, :])
                        dve.tensor_copy(ys[s][:, CH:DM], psum[6][:, :]).then_inc(S["ys_ready"], 1)

                    def low_weights(it, i, j):
                        dve.wait_ge(S["wh_ready"], it * (2 * UN) + (2 * (b + i) + j + 1))
                        half = slice(4 * j, 4 * j + 4)
                        dve.tensor_tensor(w_lo[i % UN][:, half, :], ring_view(i % UN)[:, half, :], w_hi[j].bitcast(F32), ALU.subtract).then_inc(S["wl_ready"], 1)

                    def low_rows(e):
                        dve.wait_ge(S["xh_ready"], e + (bx + 1))
                        for g in range(2):
                            ks = slice(4 * g, 4 * g + 4)
                            ins = dve.tensor_tensor(xT_lo[:, ks, :], psum[2 + g][:, :].rearrange("p (k t) -> p k t", k=4),
                                                    xT_hi[:, ks, :].bitcast(F32), ALU.subtract)
                        ins.then_inc(S["xT_ready"], 1)

                    def turn_of_experts(it):
                        for i in range(UN):
                            e = it * UN + i
                            last = isinstance(it, int) and e == E - 1
                            if not last:
                                low_weights(it, i + 1, 0)
                            dve.wait_ge(S["silu_done"], e + (b + 1))
                            dve.scalar_tensor_tensor(out=hid, in0=sgate, scalar=slot_w[:, e:e + 1] if isinstance(e, int) else slot_w[:, bass.ds(e, 1)],
                                                     in1=psum[i % 2][:, F:2 * F], op0=ALU.mult, op1=ALU.mult).then_inc(S["hid_ready"], 1)
                            dve.wait_ge(S["hT_full"], e + (b + 1))
                            dve.tensor_copy(hT[i % 2], psum[4][:, 0:2 * P].rearrange("p (k t) -> p k t", k=2)).then_inc(S["hT_ready"], 1)
                            low_rows(e + 1)
                            if not last:
                                low_weights(it, i + 1, 1)
                            if not (isinstance(it, int) and e == 0):
                                rows_out(it, i - 1)

                    low_weights(0, 0, 0)
                    low_weights(0, 0, 1)
                    low_rows(0)
                    turn_of_experts(0)
                    with dve.Fori(1, E // UN - 1) as it:
                        turn_of_experts(it)
                    turn_of_experts(E // UN - 1)
                    rows_out(E // UN, -1)

                expert_pass(MAIN, 0, 0)
                dve.wait_ge(most_ready, 1)
                with dve.If(dve.value_load(most[0:1, 0:1], min_val=0, max_val=TOK) > P):
                    expert_pass(OVER, 0, 1)
                    expert_pass(OVER, 1, 2)
                    dve.nop()
                for t in range(TILES):
                    def from_rows(z, g, t=t):
                        s = 2 * (t % 2)
                        dve.wait_ge(back[t % 2], 32 * (t // 2 + 1))
                        r4 = ring[s][:].rearrange("p (k d) -> p k d", d=DM)
                        r2 = ring[s + 1][:].rearrange("p (k d) -> p k d", d=DM)
                        for k in range(4):
                            link(dve.tensor_tensor(z, z, r4[:, k, :], ALU.add))
                        for k in range(2):
                            link(dve.tensor_tensor(z, z, r2[:, k, :], ALU.add))
                        link(dve.tensor_tensor(z, z, g, ALU.mult))
                    norm(1, t, from_rows)
                dve.wait_ge(x_ready, 2 * TILES)

            @blk.scalar
            def _(act):
                for n in range(MODC):
                    act.wait_ge(stage_ready, n + 1)
                    r = 2 * (n // 2)
                    act.dma_start(raw[r:r + 2, CH * (n % 2):CH * (n % 2) + CH], stage[n % 2][0:2, :]).then_inc(stage_sent[n % 2], 16)
                act.wait_ge(dneg_ready, 1)
                act.activation(lg, dneg, ACT.Exp).then_inc(act_step, 1)
                act.wait_ge(act_step, 1)
                act.activation(lg, lg, ACT.Ln, bias=1.0).then_inc(softplus_ready, 1)
                bank = done(act, ("gn",))
                give(act.activation(gn, bank[:, :], ACT.Copy), ("gn",))
                act.wait_ge(free[groups[("gn",)][0]], groups[("gn",)][1] + 1)
                act.sem_inc(gn_ready, 1)

                def turned(which):
                    for t in range(TILES):
                        for g in range(2):
                            name = ("xT", which, t, g)
                            bank = done(act, name)
                            give(act.activation(xmT[:, 4 * g:4 * g + 4, P * t:P * t + P],
                                                bank[:, :].rearrange("p (k t) -> p k t", k=4), ACT.Copy), name)
                            act.wait_ge(free[groups[name][0]], groups[name][1] + 1)
                            act.sem_inc(xmT_ready, 1)

                turned(0)
                for i, (n, t) in enumerate(HG):
                    if i % 2 == 1:
                        cols = min(CH, W_IN - CH * n)
                        bank = done(act, ("h", n, t))
                        give(act.activation(h[:, t, CH * n:CH * n + cols], bank[:, 0:cols], ACT.Copy), ("h", n, t))
                        act.wait_ge(free[groups[("h", n, t)][0]], groups[("h", n, t)][1] + 1)
                        act.sem_inc(h_act, 1)
                act.wait_ge(lg_ready, 1)
                act.activation(zeta[:, 0:4], lg[:, 0:4], ACT.Exp, scale=const("down")).then_inc(act_step, 1)
                act.activation(zeta[:, 4:8], lg[:, 4:8], ACT.Exp, scale=const("up")).then_inc(act_step, 1)
                act.wait_ge(act_step, 3)
                act.sem_inc(zeta_ready, 1)
                for r, ramp in enumerate(("from_start", "from_end")):
                    for hh in range(H_A):
                        p0 = 64 * (hh % 2)
                        act.activation(qx[p0:p0 + 64, r, hh // 2, :], const(ramp)[p0:p0 + 64, :], ACT.Exp,
                                       scale=lg[p0:p0 + 64, 4 * r + hh:4 * r + hh + 1]).then_inc(act_step, 1)
                act.wait_ge(act_step, 11)
                act.sem_inc(qx_raw, 1)
                for hh in range(H_A):
                    if hh:
                        act.wait_ge(decay_ready, hh)
                    act.activation(decay_f, const("absdiff"), ACT.Exp, scale=lg[:, hh:hh + 1]).then_inc(decay_raw, 1)
                    act.activation(decay_b, const("absdiff"), ACT.Exp, scale=lg[:, 4 + hh:5 + hh]).then_inc(decay_raw, 1)
                    if hh == 0:
                        for g, n in ((0, 4), (1, 1)):
                            bank = done(act, ("kctxT", g))
                            give(act.activation(kctxT[:, 4 * g:4 * g + n, :], bank[:, 0:P * n].rearrange("p (b k) -> p b k", b=n),
                                                ACT.Copy), ("kctxT", g))
                            act.wait_ge(free[groups[("kctxT", g)][0]], groups[("kctxT", g)][1] + 1)
                            act.sem_inc(kctxT_ready, 1)
                act.wait_ge(h_dve, h_on_dve)
                act.activation(h[:, :, GA:GA + 256], h[:, :, GA:GA + 256], ACT.Silu).then_inc(gate_ready, 1)
                act.wait_ge(var_ready, 1)
                act.activation(var, var, ACT.Sqrt).then_inc(root_ready, 1)
                for g in range(len(soft) + 1):
                    if g:
                        m, t, h0 = soft[g - 1]
                        nk = P if t == 0 else 3 * P
                        for i in range(3):
                            bank = done(act, ("pT", g - 1, i))
                            give(act.activation(probT[:, i, 0:nk], bank[:, 0:nk], ACT.Copy), ("pT", g - 1, i))
                            act.wait_ge(free[groups[("pT", g - 1, i)][0]], groups[("pT", g - 1, i)][1] + 1)
                            act.sem_inc(probT_ready, 1)
                    if g < len(soft):
                        m, t, h0 = soft[g]
                        nk = P if t == 0 else 3 * P
                        act.wait_ge(neg_ready, g + 1)
                        for i in range(3):
                            c_ = 3 * g + i
                            bank = psum[groups[("s", g, i)][0]]
                            give(act.activation(prob[:, i, 0:nk], bank[:, 0:nk], ACT.Exp, bias=neg[:, c_:c_ + 1],
                                                accum_out=den[:, c_:c_ + 1]), ("s", g, i))
                        if m == "B":
                            act.wait_ge(sinkx_ready, sum(s[0] == "B" for s in soft[:g + 1]))
                            act.activation(sinke[:, 3 * g:3 * g + 3], sinkx[:, 3 * g:3 * g + 3], ACT.Exp).then_inc(act_step, 1)
                            act.wait_ge(act_step, 11 + sum(s[0] == "B" for s in soft[:g + 1]))
                        for i in range(3):
                            name = ("s", g, i)
                            act.wait_ge(free[groups[name][0]], groups[name][1] + 1)
                        act.sem_inc(exp_done, 1)
                for b in range(8):
                    bank = done(act, ("yT", b))
                    give(act.activation(xmT[:, b, :], bank[:, 0:TOK], ACT.Copy), ("yT", b))
                    act.wait_ge(free[groups[("yT", b)][0]], groups[("yT", b)][1] + 1)
                    act.sem_inc(yT_ready, 1)

                def norm_rows(which):
                    if which:
                        act.wait_ge(x_ready, TILES)
                    else:
                        act.wait_ge(states_stored, 32)
                    for r in range(4):
                        for f in range(2):
                            bank = done(act, ("b", which, r, f))
                            dst = (gateb[:, r, :] if r < 2 else lnb[:, r - 2, :])[:, CH * f:CH * f + CH]
                            give(act.activation(dst, bank[:, :], ACT.Copy), ("b", which, r, f))
                            act.wait_ge(free[groups[("b", which, r, f)][0]], groups[("b", which, r, f)][1] + 1)
                            act.sem_inc(b_ready, 1)

                norm_rows(0)
                for t in range(TILES):
                    act.wait_ge(lvar_ready, t + 1)
                    act.activation(rstd, rstd, ACT.Sqrt).then_inc(lroot_ready, 1)
                norm_rows(1)
                turned(1)
                bank = done(act, ("logit",))
                act.activation(score, bank[:, 0:TILES * E].rearrange("p (t e) -> p t e", t=TILES), ACT.Sigmoid).then_inc(score_ready, 1)
                act.wait_ge(score_ready, 1)
                act.sem_inc(free[groups[("logit",)][0]], 1)
                for t in range(TILES):
                    bank = done(act, ("sgu", t))
                    act.activation(sg_s[t], bank[:, 0:F], ACT.Silu).then_inc(ssilu_done, 1)

                def expert_pass(S, q):
                    b, bx = q * E, q * (E + 1)
                    if S is OVER and not q:
                        act.wait_ge(MAIN["pass_done"], 1)

                    def high_rows(m):
                        act.wait_ge(S["xT_full"], m + (bx + 1))
                        act.activation(xT_hi[:, 0:4, :], psum[2][:, :].rearrange("p (k t) -> p k t", k=4), ACT.Copy)
                        act.activation(xT_hi[:, 4:8, :], psum[3][:, :].rearrange("p (k t) -> p k t", k=4), ACT.Copy
                                       ).then_inc(S["xh_ready"], 1)

                    def high_weights(it, i, j):
                        s = i % UN
                        if j == 0:
                            act.wait_ge(S[f"ring_in{s}"], (it + (i // UN + (ring_base[s] if S is MAIN else 0) + q * (E // NG) + 1)) * 16)
                        if not (isinstance(it, int) and b + it * UN + i == 0):
                            act.wait_ge(S["half_used"], it * (2 * UN) + (2 * (b + i) + j - 1))
                        act.activation(w_hi[j], ring_view(s)[:, 4 * j:4 * j + 4, :], ACT.Copy).then_inc(S["wh_ready"], 1)

                    def turn_of_experts(it):
                        for i in range(UN):
                            e = it * UN + i
                            last = isinstance(it, int) and e == E - 1
                            if not last:
                                high_weights(it, i + 1, 0)
                            act.wait_ge(S["half_used"], e * 2 + (2 * b + 2))
                            act.wait_ge(S["hid_ready"], e + (b + 2))
                            act.activation(sgate, psum[i % 2][:, 0:F], ACT.Silu).then_inc(S["silu_done"], 1)
                            high_rows(e + 1)
                            if not last:
                                high_weights(it, i + 1, 1)

                    if S is MAIN:
                        act.wait_ge(entries_ready, 1)
                    high_weights(0, 0, 0)
                    if S is MAIN:
                        done(act, ("sy", 2, 1))
                    high_weights(0, 0, 1)
                    high_rows(0)
                    with act.Fori(0, E // UN - 1) as it:
                        turn_of_experts(it)
                    turn_of_experts(E // UN - 1)

                expert_pass(MAIN, 0)
                act.wait_ge(most_ready, 1)
                with act.If(act.value_load(most[0:1, 0:1], min_val=0, max_val=TOK) > P):
                    expert_pass(OVER, 0)
                    expert_pass(OVER, 1)
                    act.nop()
                for t in range(TILES):
                    act.wait_ge(lvar_ready, TILES + t + 1)
                    act.activation(rstd, rstd, ACT.Sqrt).then_inc(lroot_ready, 1)

            @blk.gpsimd
            def _(pool):
                def mask_bias(t):
                    pool.wait_ge(bias_loaded, 32 * H_C * (t + 1))
                    nm = const("na_mask").unsqueeze(1).to_broadcast([P, H_C, 256])
                    pool.tensor_tensor(nab, nab, nm, ALU.add).then_inc(bias_masked, 1)

                mask_bias(0)
                for hh in range(H_A):
                    pool.wait_ge(decay_raw, 2 * hh + 2)
                    pool.affine_select(out=decay_f, in_=decay_f, compare_op=ALU.is_ge, fill=0.0, base=-P,
                                       pattern=[[1, TOK]], channel_multiplier=-1)
                    pool.affine_select(out=decay_b, in_=decay_b, compare_op=ALU.is_ge, fill=0.0, base=P,
                                       pattern=[[-1, TOK]], channel_multiplier=1).then_inc(decay_cut, 1)
                mask_bias(1)
                pool.wait_ge(table_empty, 16 * TILES)
                pool.wait_ge(entries_ready, 1)
                for j in range(TILES * TOPK):
                    pool.indirect_dma_start(slots, bass.IndirectOffsetOnAxis(ap=place_i[:, j:j + 1], axis=0),
                                            entry[:, j, :], None, bounds_check=TOK * E - 1, oob_is_err=False
                                            ).then_inc(entries_sent, 16)
                pool.wait_ge(entries_sent, 16 * TILES * TOPK)
                pool.dma_start(table.rearrange("p t e v -> p t (e v)"), slots.rearrange("(t p e) v -> p t (e v)", p=P, e=E)).then_inc(table_loaded, 16)
                pool.wait_ge(yT_ready, 8)
                pool.wait_ge(caches_stored, 64)
                pool.memset(xg[0], 0.0).then_inc(xg_zeroed, 1)
                pool.memset(xg[1], 0.0).then_inc(xg_zeroed, 1)
                pool.wait_ge(xg_zeroed, 2)
                pool.wait_ge(xm_saved, 16)

                def expert_pass(S, q):
                    b, bx, bi = q * E, q * (E + 1), q * (2 * E + 2)
                    pool.wait_ge(S["slots_ready"], q + 1)

                    def gather(par, e, n):
                        pool.tensor_copy(now_idx[par][:], slot_idx[:, 0, e:e + 1] if isinstance(e, int) else slot_idx[:, 0, bass.ds(e, 1)]
                                         ).then_inc(S["idx_set"], 1)
                        pool.wait_ge(S["idx_set"], n)
                        pool.sem_inc(idx_seen, 1)
                        pool.indirect_dma_start(xg[par], None, scratch_x,
                                                bass.IndirectOffsetOnAxis(ap=now_idx[par][:], axis=0),
                                                bounds_check=TOK - 1, oob_is_err=False).then_inc(S[f"gathered{par}"], 16)

                    if q:
                        pool.wait_ge(S["xT_full"], bx)
                    gather(0, 0, bi + 1)
                    gather(1, 1, bi + 2)

                    def scatter(par, e, n):
                        pool.wait_ge(S["ys_ready"], e + (b + 2))
                        pool.tensor_copy(now_idx[2 + par][:], slot_idx[:, 1, e:e + 1] if isinstance(e, int) else slot_idx[:, 1, bass.ds(e, 1)]
                                         ).then_inc(S["idx_set"], 1)
                        pool.wait_ge(S["idx_set"], n)
                        pool.sem_inc(idx_seen, 1)
                        pool.indirect_dma_start(scratch_y, bass.IndirectOffsetOnAxis(ap=now_idx[2 + par][:], axis=0),
                                                ys[par], None, bounds_check=TOK * TOPK - 1, oob_is_err=False
                                                ).then_inc(S[f"scattered{par}"], 16)

                    def turn_of_experts(it):
                        for i in range(UN):
                            e = it * UN + i
                            first = isinstance(it, int) and i == 0
                            pool.wait_ge(S["xT_full"], e + (bx + 1))
                            gather(i % 2, e + 2, e * 2 + (bi + (3 if first else 2)))
                            if not first:
                                scatter((i - 1) % 2, it * UN + (i - 1), e * 2 + (bi + 3))

                    turn_of_experts(0)
                    with pool.Fori(1, E // UN) as it:
                        turn_of_experts(it)
                    scatter(1, E - 1, bi + 2 * E + 2)
                    for par in range(2):
                        pool.wait_ge(S[f"scattered{par}"], 16 * (E // 2) * (q + 1))
                        pool.wait_ge(S[f"gathered{par}"], 16 * 33 * (q + 1))
                    pool.wait_ge(S["xT_full"], bx + E + 1)
                    pool.sem_inc(S["pass_done"], 1)

                expert_pass(MAIN, 0)
                pool.wait_ge(most_ready, 1)
                with pool.If(pool.value_load(most[0:1, 0:1], min_val=0, max_val=TOK) > P):
                    expert_pass(OVER, 0)
                    expert_pass(OVER, 1)
                    pool.nop()
                pool.sem_inc(experts_done, 1)

            bctx.close()
            numbers = sorted(x.num for x in layer_sems)
            assert numbers == list(range(numbers[0], numbers[-1] + 1))
            nc.gpsimd.dma_reset(range(numbers[0], numbers[-1] + 1))
            nc.gpsimd.sem_clear(range(numbers[0], numbers[-1] + 1))
            nc.all_engine_barrier()

        with ExitStack() as c1:
            tokens_stored = c1.enter_context(nc.semaphore("tokens_stored"))
            blk1 = c1.enter_context(nc.Block())

            @blk1.sync
            def _(sp):
                sp.dma_start(o["y_prompt"][0], x[:, 0, :]).then_inc(tokens_stored, 16)
                sp.dma_start(o["y_sample"][0].rearrange("(t p) d -> p t d", p=P), x[:, 1:3, :]).then_inc(tokens_stored, 16)
                sp.wait_ge(tokens_stored, 32)


INPUTS = ("x_prompt", "x_sample", "state_ret_fwd", "state_ret_bwd", "cache_win_k", "cache_win_v", "cache_na_k",
          "cache_na_v", "c", "c_ctx", "w_in", "w_out", "ret_decay_fwd", "ret_decay_bwd", "ret_gn_g", "ret_gn_b",
          "win_sink", "na_rpb", "w_mod", "b_mod", "ln1_g", "ln1_b", "ln2_g", "ln2_b", "w_router", "b_router",
          "w_expert_gu", "w_expert_down", "w_shared_gu", "w_shared_down")
OUTPUTS = (("y_prompt", (1, P, DM)), ("y_sample", (1, 2 * P, DM)),
           ("new_fwd", (1, DEPTH, H_A, HD, HD)), ("new_bwd", (1, DEPTH, H_A, HD, HD)),
           ("new_win_k", (1, DEPTH, 2, P, HD)), ("new_win_v", (1, DEPTH, 2, P, HD)),
           ("new_na_k", (1, DEPTH, H_C, P, HD)), ("new_na_v", (1, DEPTH, H_C, P, HD)))


def kernel(**inputs):
    import numpy as _np
    import concourse.bacc as _bacc
    from concourse import mybir as _mybir
    from concourse.bass_utils import run_bass_kernel_spmd as _run

    nc = _bacc.Bacc("TRN2", target_bir_lowering=False, num_devices=1)
    arrays, a, o = {}, {}, {}
    for name in INPUTS + ("consts",):
        v = constants() if name == "consts" else _np.ascontiguousarray(inputs[name])
        arrays[f"in_{name}"] = v
        a[name] = nc.dram_tensor(f"in_{name}", v.shape, _mybir.dt.from_np(v.dtype), kind="ExternalInput").ap()
    for name, shape in OUTPUTS:
        o[name] = nc.dram_tensor(f"out_{name}", shape, _mybir.dt.float32, kind="ExternalOutput").ap()
    build(nc, a, o)
    r = _run(nc, [arrays], core_ids=[0])
    return tuple(r.results[0][f"out_{name}"] for name, _ in OUTPUTS)
```

```python
import numpy as np
import concourse.bass as bass
from concourse import mybir
from contextlib import ExitStack

F32 = mybir.dt.float32
F32R = mybir.dt.float32r
I32 = mybir.dt.int32
ALU = mybir.AluOpType
ACT = mybir.ActivationFunctionType
AX = mybir.AxisListType

P = 128
DM = 1024
KD = DM // P
DEPTH = 2
TILES = 3
TOK = TILES * P
HD = 64
CH = 512
W_IN = 2816
QA, KA, VA, GA, QB, KB, VB, QC, KC, VC = 0, 256, 512, 768, 1024, 1408, 1536, 1664, 2048, 2432
H_A, H_B, H_C = 4, 6, 6
SCALE = HD ** -0.5
ALPHA = float((2 * DEPTH) ** 0.25)
EPS = 1e-5
NEG = -1e30
BIG = 3.0e38
MARK = -3.0e38
E = 64
TOPK = 6
F = 256
ROUTE_SCALE = 2.5
FAR = 4096
NG = 4
ND = 2
UN = 4
MODC = 6 * DM // CH
INC = (W_IN + CH - 1) // CH
OUTC = DM // CH
CHUNKS = MODC + INC + OUTC + 1
EARLY = 4
LATE = MODC - EARLY
LN_ROW, SMALL_ROW, BIAS_ROW, LATE_ROW, OUT_ROW = 0, 4, 32, 64, 96
SINK, DEC = 64, 70

CONSTS = {}


def constants():
    p = np.arange(P)[:, None]
    j = np.arange(P)[None, :]
    parts = []

    def put(name, a):
        a = np.broadcast_to(a, (P, a.shape[1])).astype(np.float32)
        CONSTS[name] = (sum(x.shape[1] for x in parts), a.shape[1])
        parts.append(a)

    put("ident", (p == j) * 1.0)
    put("flip", (p + j == P - 1) * 1.0)
    put("before", (p < j) * 1.0)
    put("ones", np.ones((P, P)))
    put("slot", j * 1.0)
    put("band_next", np.where(j <= p, 0.0, NEG))
    put("band_prev", np.where(j >= p, 0.0, NEG))
    qc = 63 - np.arange(P)[:, None] % 64
    kc = np.arange(256)[None, :] % 64
    c0 = np.clip(qc - 8, 0, 48)
    put("na_mask", np.where((kc >= c0) & (kc < c0 + 16), 0.0, NEG))
    put("absdiff", np.abs(np.arange(3 * P)[None, :] - P - p) * 1.0)
    i = np.arange(2 * P)[None, :]
    put("from_start", i + 1.0)
    put("from_end", 2 * P - i * 1.0)
    inv = (10000.0 ** (-np.arange(16, dtype=np.float32) / 16)).astype(np.float32)
    tables = []
    for t in range(2):
        pos = np.arange(P) + P * t
        ang = np.concatenate([(pos // 64)[:, None] * inv, (pos % 64)[:, None] * inv], 1).astype(np.float32)
        tables.append((np.cos(ang), np.sin(ang)))
    put("cos", np.concatenate([tables[0][0], tables[1][0]], 1))
    put("sin", np.concatenate([tables[0][1], tables[1][1]], 1))
    put("down", P - 1.0 - p)
    put("up", p * 1.0)
    tok = p + P * np.arange(TILES)[None, :]
    k = np.arange(TOPK)[None, None, :]
    t3 = tok[:, :, None] + 0 * k
    put("tok_row", np.stack([t3, t3 * TOPK + k, 0 * t3], -1).reshape(P, -1))
    put("empty", np.tile([1.0 * FAR, 1.0 * FAR, 0.0], E)[None, :])
    return np.ascontiguousarray(np.concatenate(parts, 1))


NCONST = constants().shape[1] - 3 * E


def psum_groups():
    names = [("mod", n) for n in range(EARLY)] + [("small",), ("gn",)]
    names += [("m", 0, c, f, w) for c in range(2) for f in range(2) for w in range(2)]
    names += [("xT", 0, t, g) for t in range(TILES) for g in range(2)]
    names += [("h", n, t) for n in range(INC) for t in range(TILES)]
    names += [("qkT", b) for b in range(15)] + [("kctxT", 0), ("kctxT", 1)]
    for h in range(H_A):
        names += [("sA", h, 0), ("sA", h, 1)]
    names += [("oA", h) for h in range(H_A)] + [("state",)]
    for g in range(12 + 1):
        if g < 12:
            names += [("s", g, i) for i in range(3)]
        if g:
            names += [("pT", g - 1, i) for i in range(3)] + [("pv", g - 1)]
    names += [("yT", b) for b in range(8)]
    names += [("b", 0, r, f) for r in range(4) for f in range(2)]
    names += [("y", n, t) for n in range(OUTC) for t in range(TILES)]
    names += [("m", 1, c, f, w) for c in range(2) for f in range(2) for w in range(2)]
    names += [("b", 1, r, f) for r in range(4) for f in range(2)]
    names += [("xT", 1, t, g) for t in range(TILES) for g in range(2)]
    names += [("logit",), ("pos",)]
    names += [("sgu", t) for t in range(TILES)]
    for t in range(TILES):
        names += [("shT", t), ("sy", t, 0), ("sy", t, 1)]
    uses = [0] * 8
    out = {}
    for n, name in enumerate(names):
        out[name] = (n % 7, uses[n % 7])
        uses[n % 7] += 1
    for n in range(EARLY, MODC):
        out[("mod", n)] = (7, uses[7])
        uses[7] += 1
    return out, names, uses


def build(nc, a, o):
    groups, order, bank_uses = psum_groups()
    soft = [(m, t, h) for t in range(TILES) for m in "BC" for h in (0, 3)]

    with ExitStack() as ctx:
        begins = {}

        def sb(name, cols, dt=F32, rows=P):
            t = ctx.enter_context(nc.sbuf_tensor(name, [rows, cols], dt))
            begins[name] = nc.sbuf_base - 4 * cols
            return t

        def rounded(name, base, cols, at=0):
            return nc.alloc_sbuf_tensor_at(name, [P, cols], F32R, offset=begins[base] + 4 * at)[:]

        scratch_x = nc.dram_tensor("scratch_x", (TOK, DM), F32, kind="Internal").ap()
        scratch_y = nc.dram_tensor("scratch_y", (TOK * TOPK, DM), F32, kind="Internal").ap()
        slots = nc.dram_tensor("slots", (TOK * E, 3), F32, kind="Internal").ap()

        ring = [sb(f"ring{i}", KD * CH) for i in range(NG)]
        x = sb("x", TILES * DM)[:].rearrange("p (t d) -> p t d", t=TILES)
        cst = sb("cst", NCONST)
        xmT = sb("xmT", KD * TOK)[:].rearrange("p (k t) -> p k t", k=KD)
        rows = sb("rows", DM)
        condT = sb("condT", KD * 2)[:].rearrange("p (k c) -> p k c", c=2)
        cmisc = sb("cmisc", 512)
        A = sb("arena_a", TILES * W_IN + 15 * TOK)
        B = sb("arena_b", 12200)
        psum = [ctx.enter_context(nc.psum_tensor(f"bank{i}", [P, 512], F32)) for i in range(8)]

        def const(name):
            at, n = CONSTS[name]
            return cst[:, at:at + n]

        class Carve:
            def __init__(self, base, at=0):
                self.base, self.at = base, at

            def __call__(self, n):
                self.at += n
                assert self.at <= self.base.shape[1], self.at
                return self.base[:, self.at - n:self.at]

        c = Carve(A)
        xm = c(TILES * DM).rearrange("p (t d) -> p t d", t=TILES)
        stage = [rows[OUT_ROW:OUT_ROW + 2, CH * i:CH * i + CH] for i in range(2)]
        cond = c(P)
        early = c(EARLY * CH)
        c = Carve(A)
        h = c(TILES * W_IN).rearrange("p (t d) -> p t d", t=TILES)
        qkT = c(15 * TOK).rearrange("p (b t) -> p b t", b=15)
        c = Carve(A, TILES * DM)
        xg = [c(DM), c(DM)]
        xgT_at = c.at
        c(DM)
        ys = [c(DM), c(DM)]
        hid, sgate = c(F), c(F)
        hT = [c(F).rearrange("p (k t) -> p k t", k=2) for _ in range(2)]
        table = c(TILES * E * 3).rearrange("p (t e v) -> p t e v", t=TILES, e=E)
        sg_s, hid_s = [c(F) for _ in range(TILES)], [c(F) for _ in range(2)]
        xgT_lo_at, high1_at = c.at, c.at + DM
        c(DM)
        high1 = c(KD * CH // 2)
        shT = high1[:, 0:2 * P].rearrange("p (k t) -> p k t", k=2)
        wr = high1[:, 2 * P:2 * P + KD * E].rearrange("p (k e) -> p k e", k=KD)
        c = Carve(B)
        nab = c(H_C * 256).rearrange("p (h k) -> p h k", h=H_C)
        kctx = c(10 * HD)
        kctxT = c(5 * P).rearrange("p (b k) -> p b k", b=5)
        vctx = c(8 * HD).rearrange("p (h d) -> p h d", h=8)
        s0 = c(4 * HD).rearrange("p (r g d) -> p r g d", r=2, g=2)
        gn = c(2 * 256)
        xmT_lo_at = c.at
        prob = c(3 * TOK).rearrange("p (i k) -> p i k", i=3)
        probT = c(3 * TOK).rearrange("p (i k) -> p i k", i=3)
        decay_f, decay_b = c(TOK), c(TOK)
        assert c.at - xmT_lo_at >= KD * TOK
        decay = c(TOK)
        pa = c(5 * P)
        qx = c(4 * 256).rearrange("p (r g t) -> p r g t", r=2, g=2)
        kz = c(2 * 256).rearrange("p (r h d) -> p r h d", r=2, h=H_A)
        oA = c(TILES * 256).rearrange("p (t h d) -> p t h d", t=TILES, h=H_A)
        tmp = c(TILES * 256)
        ksw = c(TILES * P).rearrange("p (t d) -> p t d", t=TILES)
        stout = c(512)
        c = Carve(B)
        down = [c(2 * DM).rearrange("p (k n) -> p k n", k=2) for _ in range(ND)]
        gateb = c(2 * DM).rearrange("p (c d) -> p c d", c=2)
        lnb = c(2 * DM).rearrange("p (r d) -> p r d", r=2)
        high0_at = c.at
        high0 = c(2 * TILES * TOPK * E)
        of_rank = high0[:, 0:TILES * TOPK * E].rearrange("p (t k e) -> p t k e", t=TILES, k=TOPK)
        picked = high0[:, TILES * TOPK * E:].rearrange("p (t k e) -> p t k e", t=TILES, k=TOPK)
        score = c(TILES * E).rearrange("p (t e) -> p t e", t=TILES)
        sel = c(TILES * 66).rearrange("p (t e) -> p t e", t=TILES)
        sel2 = c(TILES * 66).rearrange("p (t e) -> p t e", t=TILES)
        grp = c(TILES * 12).rearrange("p (t e) -> p t e", t=TILES)
        grp2 = c(TILES * 12).rearrange("p (t e) -> p t e", t=TILES)
        top = c(24 * 8).rearrange("p (g e) -> p g e", g=24)
        top8 = c(TILES * 8).rearrange("p (t e) -> p t e", t=TILES)
        mask = c(TILES * E).rearrange("p (t e) -> p t e", t=TILES)
        posm = c(TILES * E).rearrange("p (t e) -> p t e", t=TILES)
        rank = c(TILES * E).rearrange("p (t e) -> p t e", t=TILES)
        wsum = c(8)
        entry = c(TILES * TOPK * 3).rearrange("p (j v) -> p j v", v=3)
        xT_hi = rounded("xT_hi", "arena_a", DM, xgT_at).rearrange("p (k t) -> p k t", k=KD)
        xT_lo = rounded("xT_lo", "arena_a", DM, xgT_lo_at).rearrange("p (k t) -> p k t", k=KD)
        w_hi = [rounded(f"w_hi{j}", n, KD * CH // 2, at).rearrange("p (k n) -> p k n", k=KD // 2)
                for j, (n, at) in enumerate((("arena_b", high0_at), ("arena_a", high1_at)))]
        xmT_hi = rounded("xmT_hi", "xmT", KD * TOK).rearrange("p (k t) -> p k t", k=KD)
        xmT_lo = rounded("xmT_lo", "arena_b", KD * TOK, xmT_lo_at).rearrange("p (k t) -> p k t", k=KD)
        win_hi = rounded("win_hi", "arena_a", KD * CH, TILES * W_IN).rearrange("p (k n) -> p k n", k=KD)
        w_lo = [rounded(f"w_lo{i}", f"ring{i}", KD * CH).rearrange("p (k n) -> p k n", k=KD) for i in range(NG)]
        place = c(TILES * TOPK)
        place_i = sb("place_i", TILES * TOPK, I32)
        most = sb("most", 2, I32)
        slot_idx = sb("slot_idx", 2 * (E + 2), I32)[:].rearrange("p (v e) -> p v e", v=2)
        slot_w = sb("slot_w", E)
        now_idx = [sb(f"now_idx{i}", 1, I32) for i in range(4)]
        c = Carve(cmisc)
        lg, dneg, small, zeta = c(8), c(8), c(80), c(8)
        mx, neg, den, sinkx, sinke, recip = c(36), c(36), c(36), c(36), c(36), c(36)
        mean, var = c(12), c(12)
        bn, bnag, rstd, shift = c(12), c(2 * TILES), c(TILES), c(TILES)

        mod_row = {"g1": LATE_ROW, "sh2": LATE_ROW + 2, "sc2": LATE_ROW + 4, "g2": LATE_ROW + 6}

        def mod_dst(n):
            r = LATE_ROW + 2 * (n // 2) - EARLY
            return rows[r:r + 2, CH * (n % 2):CH * (n % 2) + CH]

        with ExitStack() as c0:
            cst_loaded, tokens_loaded, cond_loaded, cond_turned, cond_done, far_set = (
                c0.enter_context(nc.semaphore(n)) for n in
                ("cst_loaded", "tokens_loaded", "cond_loaded", "cond_turned", "cond_done", "far_set"))
            blk0 = c0.enter_context(nc.Block())

            @blk0.sync
            def _(sp):
                sp.dma_start(cst[:], a["consts"][:, 0:NCONST]).then_inc(cst_loaded, 16)
                sp.dma_start(x[:, 0, :], a["x_prompt"][0]).then_inc(tokens_loaded, 16)
                sp.dma_start(x[:, 1:3, :], a["x_sample"][0].rearrange("(t p) d -> p t d", p=P)).then_inc(tokens_loaded, 16)
                sp.dma_start(cond[0:KD, :], a["c_ctx"].rearrange("(k p) -> k p", p=P)).then_inc(cond_loaded, 16)
                sp.dma_start(cond[KD:2 * KD, :], a["c"][0].rearrange("(k p) -> k p", p=P)).then_inc(cond_loaded, 16)
                sp.wait_ge(cst_loaded, 16)
                sp.wait_ge(tokens_loaded, 32)

            @blk0.tensor
            def _(pe):
                pe.wait_ge(cst_loaded, 16)
                pe.wait_ge(cond_loaded, 32)
                pe.transpose(psum[0][:, 0:2 * KD], cond[0:2 * KD, :], const("ident")[0:2 * KD, 0:2 * KD]).then_inc(cond_turned, 1)

            @blk0.scalar
            def _(act):
                act.wait_ge(cond_turned, 1)
                act.activation(condT.rearrange("p k c -> p c k"), psum[0][:, 0:2 * KD].rearrange("p (c k) -> p c k", c=2),
                               ACT.Silu).then_inc(cond_done, 1)
                act.wait_ge(cond_done, 1)

            @blk0.gpsimd
            def _(pool):
                pool.memset(slot_idx[:, :, E:E + 2], FAR).then_inc(far_set, 1)
                pool.wait_ge(far_set, 1)

        with ExitStack() as lctx:
            l = lctx.enter_context(nc.Fori(0, DEPTH))

            def at_layer(name):
                return a[name][bass.ds(l, 1)]

            def of_layer(d, name):
                return d[name][0][bass.ds(l, 1)].rearrange("a h p d -> (a h) p d")

            layer_sems = []

            def sem(name):
                layer_sems.append(lctx.enter_context(nc.semaphore(name)))
                return layer_sems[-1]

            full = [sem(f"bank_full{i}") for i in range(8)]
            free = [sem(f"bank_free{i}") for i in range(8)]
            ring_ready = [sem(f"ring_ready{i}") for i in range(NG)]
            down_ready = [sem(f"down_ready{i}") for i in range(ND)]
            dve_step = sem("dve_step")
            stage_ready, stage_sent = sem("stage_ready"), [sem("stage_sent0"), sem("stage_sent1")]
            rows_loaded, bmod_loaded = sem("rows_loaded"), sem("bmod_loaded")
            xm_ready, xmT_ready = sem("xm_ready"), sem("xmT_ready")
            h_dve, h_act, rope_done, qkT_ready = sem("h_dve"), sem("h_act"), sem("rope_done"), sem("qkT_ready")
            ctx_loaded, kctxT_ready = sem("ctx_loaded"), sem("kctxT_ready")
            bias_loaded, bias_masked = sem("bias_loaded"), sem("bias_masked")
            gn_ready = sem("gn_ready")
            dneg_ready, softplus_ready, lg_ready = sem("dneg_ready"), sem("softplus_ready"), sem("lg_ready")
            act_step = sem("act_step")
            decay_raw, decay_cut, decay_ready = sem("decay_raw"), sem("decay_cut"), sem("decay_ready")
            pa_ready, zeta_ready, kz_ready = sem("pa_ready"), sem("zeta_ready"), sem("kz_ready")
            qx_raw, qx_ready, state_ready = sem("qx_raw"), sem("qx_ready"), sem("state_ready")
            var_ready, root_ready, gate_ready, ya_written = sem("var_ready"), sem("root_ready"), sem("gate_ready"), sem("ya_written")
            neg_ready, sinkx_ready, exp_done = sem("neg_ready"), sem("sinkx_ready"), sem("exp_done")
            probT_ready, y_written, yT_ready = sem("probT_ready"), sem("y_written"), sem("yT_ready")
            b_ready, x_ready, lvar_ready, lroot_ready = sem("b_ready"), sem("x_ready"), sem("lvar_ready"), sem("lroot_ready")
            wr_loaded, xm_saved, score_ready, mask_ready = sem("wr_loaded"), sem("xm_saved"), sem("score_ready"), sem("mask_ready")
            most_ready, xg_zeroed = sem("most_ready"), sem("xg_zeroed")
            table_empty, entries_ready, entries_sent, table_loaded = (
                sem("table_empty"), sem("entries_ready"), sem("entries_sent"), sem("table_loaded"))
            ssilu_done, shid_ready, shT_ready = sem("ssilu_done"), sem("shid_ready"), sem("shT_ready")
            caches_stored, states_stored, experts_done = sem("caches_stored"), sem("states_stored"), sem("experts_done")
            back = [sem(f"rows_back{t}") for t in range(TILES)]
            x_pool, rows_summed, shift_ready, normal_ready, scaled_ready = (
                sem("x_pool"), sem("rows_summed"), sem("shift_ready"), sem("normal_ready"), sem("scaled_ready"))
            idx_seen, early_ready = sem("idx_seen"), sem("early_ready")
            xmT_hi_ready, win_hi_ready, win_lo_ready, win_used = (
                sem("xmT_hi_ready"), sem("win_hi_ready"), sem("win_lo_ready"), sem("win_used"))

            def pass_sems(tag):
                return {n: sem(f"{n}_{tag}") for n in
                        ("slots_ready", "gathered0", "gathered1", "xT_full", "xT_ready",
                         "wh_ready", "wl_ready", "half_used", "xh_ready", "silu_done", "hid_ready", "hT_full", "hT_ready", "y_full", "ys_ready",
                         "scattered0", "scattered1", "ring_in0", "ring_in1", "ring_in2", "ring_in3", "down_in0",
                         "down_in1", "idx_set", "pass_done")}

            MAIN, OVER = pass_sems("main"), pass_sems("over")
            for i in range(NG):
                MAIN[f"ring_in{i}"] = ring_ready[i]
            for i in range(ND):
                MAIN[f"down_in{i}"] = down_ready[i]
            bctx = ExitStack()
            blk = bctx.enter_context(nc.Block())

            def done(eng, name):
                b, n = groups[name]
                eng.wait_ge(full[b], n + 1)
                return psum[b]

            def give(ins, name):
                ins.then_inc(free[groups[name][0]], 1)

            HG = [(n, t) for n in range(INC) for t in range(TILES)]
            h_on_act = sum(i % 2 for i in range(len(HG)))
            h_on_dve = len(HG) - h_on_act
            last_c1 = max(g for g, s in enumerate(soft) if s[:2] == ("C", 1))
            ring_base = [(CHUNKS - i + NG - 1) // NG for i in range(NG)]
            down_base = [1, 0]

            def win_half(n, j):
                return (EARLY + n) % NG, slice(4 * j, 4 * j + 4), slice(0, min(CH, W_IN - CH * n))

            def ring_view(i):
                return ring[i][:].rearrange("p (k n) -> p k n", k=KD)

            rr = [ring[i][:].rearrange("p (k d) -> p k d", d=DM) for i in range(NG)]
            back_in = [[(rr[0], 0, 4), (rr[1][:, 0:2, :], 4, 2)],
                       [(rr[2], 0, 4), (rr[3][:, 0:2, :], 4, 2)],
                       [(rr[1][:, 2:4, :], 0, 2), (rr[3][:, 2:4, :], 2, 2), (down[0], 4, 2)]]
            back_rows = [[dst[:, j, :] for dst, k0, n in back_in[t] for j in range(n)] for t in range(TILES)]

            @blk.sync
            def _(sp):
                last_use = ([("mod", i) for i in range(EARLY)] + [("h", i, 2) for i in range(INC)] +
                            [("mod", i) for i in range(EARLY, MODC)] + [("y", i, 2) for i in range(OUTC)] + [("sgu", 2)])

                def load_chunk(n, src, w=CH):
                    s = n % NG
                    if n >= NG:
                        done(sp, last_use[n - NG])
                    sp.dma_start(ring_view(s)[:, :, 0:w], src).then_inc(ring_ready[s], 16)

                def chunks(name):
                    return at_layer(name).rearrange("a (k p) n -> p (a k) n", p=P)

                for i in range(EARLY):
                    if i == 0:
                        sp.dma_start(rows[BIAS_ROW:BIAS_ROW + 6, :], at_layer("b_mod").rearrange("a (r d) -> (a r) d", r=6)
                                     ).then_inc(bmod_loaded, 16)
                        for r, name in enumerate(("ln1_g", "ln1_b", "ln2_g", "ln2_b")):
                            sp.dma_start(rows[LN_ROW + r:LN_ROW + r + 1, :], at_layer(name)).then_inc(rows_loaded, 16)
                        at = 0
                        for name, w in (("ret_gn_g", 256), ("ret_gn_b", 256), ("b_router", E), ("win_sink", H_B),
                                        ("ret_decay_fwd", H_A), ("ret_decay_bwd", H_A)):
                            sp.dma_start(rows[SMALL_ROW:SMALL_ROW + 1, at:at + w], at_layer(name)).then_inc(rows_loaded, 16)
                            at += w
                    load_chunk(i, chunks("w_mod")[:, :, CH * i:CH * i + CH])
                    if i == 3:
                        at, n = CONSTS["empty"]
                        for t in range(TILES):
                            sp.dma_start(slots.rearrange("(t p e) v -> t p (e v)", p=P, e=E)[t], a["consts"][:, at:at + n]).then_inc(table_empty, 16)
                        kv = kctx.rearrange("p (h d) -> p h d", d=HD)
                        wk, nk = of_layer(a, "cache_win_k"), of_layer(a, "cache_na_k")
                        sp.dma_start(kv[:, 0:2, :], wk.rearrange("h p d -> p h d")).then_inc(ctx_loaded, 16)
                        sp.dma_start(kv[:, 2, :], wk[1]).then_inc(ctx_loaded, 16)
                        sp.dma_start(kv[:, 3, :], wk[0]).then_inc(ctx_loaded, 16)
                        sp.dma_start(kv[:, 4:10, :], nk.rearrange("h p d -> p h d")).then_inc(ctx_loaded, 16)
                        sp.dma_start(vctx[:, 0:2, :], of_layer(a, "cache_win_v").rearrange("h p d -> p h d")).then_inc(ctx_loaded, 16)
                        sp.dma_start(vctx[:, 2:8, :], of_layer(a, "cache_na_v").rearrange("h p d -> p h d")).then_inc(ctx_loaded, 16)
                        for r, name in enumerate(("state_ret_fwd", "state_ret_bwd")):
                            st = of_layer(a, name)
                            for g in range(2):
                                sp.dma_start(s0[:, r, g, :], st[2 * g:2 * g + 2].rearrange("h d e -> (h d) e")).then_inc(ctx_loaded, 16)

                def load_bias(t):
                    rp = at_layer("na_rpb")
                    for rr in range(2):
                        r = 2 * t + 1 - rr
                        for hh in range(H_C):
                            src = bass.AP(rp.tensor, rp.offset + (hh * 15 * 31 + (7 - r) * 31 + 15 - 63), [[1, 64], [31, 4], [1, 64]])
                            sp.dma_start(nab[64 * rr:64 * rr + 64, hh, :].rearrange("p (r c) -> p r c", r=4), src).then_inc(bias_loaded, 16)

                def load_late(i):
                    n = EARLY + i
                    load_chunk(EARLY + INC + i, chunks("w_mod")[:, :, CH * n:CH * n + CH])

                for i in range(INC):
                    w = min(CH, W_IN - CH * i)
                    load_chunk(EARLY + i, chunks("w_in")[:, :, CH * i:CH * i + w], w)
                    if i == 3:
                        load_bias(0)
                for i in range(4):
                    load_late(i)
                sp.wait_ge(h_dve, h_on_dve)
                sp.wait_ge(h_act, h_on_act)
                for name, col, nh in (("new_win_k", KB, 2), ("new_win_v", VB, 2), ("new_na_k", KC, 6), ("new_na_v", VC, 6)):
                    sp.dma_start(of_layer(o, name).rearrange("h p d -> p h d"),
                                 h[:, 0, col:col + nh * HD].rearrange("p (h d) -> p h d", d=HD)).then_inc(caches_stored, 16)
                load_late(4)
                load_late(5)
                sp.wait_ge(state_ready, 1)
                for r, name in enumerate(("new_fwd", "new_bwd")):
                    sp.dma_start(of_layer(o, name).rearrange("h d e -> d h e"),
                                 stout[0:64, 256 * r:256 * r + 256].rearrange("p (h e) -> p h e", h=H_A)).then_inc(states_stored, 16)
                load_late(6)
                load_late(7)
                for i in range(OUTC):
                    load_chunk(MODC + INC + i, chunks("w_out")[:, :, CH * i:CH * i + CH])
                done(sp, ("s", last_c1, 2))
                load_bias(1)
                load_chunk(CHUNKS - 1, chunks("w_shared_gu"))
                sp.wait_ge(yT_ready, 8)
                sp.wait_ge(caches_stored, 64)
                sp.wait_ge(states_stored, 32)
                sp.dma_start(down[0], at_layer("w_shared_down").rearrange("a (k p) n -> p (a k) n", p=P)).then_inc(down_ready[0], 16)
                sp.dma_start(wr, at_layer("w_router").rearrange("a (k p) e -> p (a k) e", p=P)).then_inc(wr_loaded, 16)

                def expert_loads(S, q):
                    gu_v, dn_v = at_layer("w_expert_gu"), at_layer("w_expert_down")
                    b = q * E

                    def gu(i, e):
                        sp.dma_start(ring_view(i), gu_v[:, bass.ds(e, 1)].rearrange("a b (k p) n -> p (a b k) n", p=P)
                                     ).then_inc(S[f"ring_in{i}"], 16)

                    def dn(i, e):
                        sp.dma_start(down[i], dn_v[:, bass.ds(e, 1)].rearrange("a b (k p) n -> p (a b k) n", p=P)
                                     ).then_inc(S[f"down_in{i}"], 16)

                    for e in (1, 2, 3, 0):
                        if S is MAIN:
                            done(sp, last_use[max(n for n in range(CHUNKS) if n % NG == e)])
                        gu(e, e)
                        if e < ND:
                            if S is MAIN and e == 0:
                                done(sp, ("sy", 2, 1))
                            dn(e, e)

                    def turn_of_loads(it):
                        for i in range(UN):
                            sp.wait_ge(S["half_used"], it * (2 * UN) + 2 * (b + i - NG + 1))
                            gu(i, it * UN + i)
                            if isinstance(it, int) and i == 0:
                                continue
                            sp.wait_ge(S["y_full"], it * UN + (b + i - 4))
                            dn((i + 1) % ND, it * UN + (i - 3))

                    turn_of_loads(1)
                    with sp.Fori(2, E // UN) as it:
                        turn_of_loads(it)
                    for e in (E - 3, E - 2, E - 1):
                        sp.wait_ge(S["y_full"], b + e - 1)
                        dn(e % ND, e)

                sp.wait_ge(xm_ready, 2)
                sp.dma_start(scratch_x.rearrange("(t p) d -> p t d", p=P), xm).then_inc(xm_saved, 16)
                expert_loads(MAIN, 0)
                sp.wait_ge(most_ready, 1)
                with sp.If(sp.value_load(most[0:1, 0:1], min_val=0, max_val=TOK) > P):
                    sp.wait_ge(MAIN["pass_done"], 1)
                    expert_loads(OVER, 0)
                    sp.wait_ge(OVER["pass_done"], 1)
                    expert_loads(OVER, 1)
                    sp.nop()
                sp.wait_ge(experts_done, 1)
                for t in range(TILES):
                    src = scratch_y.rearrange("(t p k) d -> t p k d", p=P, k=TOPK)[t]
                    for dst, k0, n in back_in[t]:
                        sp.dma_start(dst, src[:, k0:k0 + n, :]).then_inc(back[t], 16)
                for t in range(TILES):
                    sp.wait_ge(back[t], 16 * len(back_in[t]))

            @blk.tensor
            def _(pe):
                turn = iter(order)
                ident, flip, ones, before = const("ident"), const("flip"), const("ones"), const("before")

                def begin(name):
                    assert next(turn) == name, name
                    b, n = groups[name]
                    if n > 0:
                        pe.wait_ge(free[b], n)
                    return psum[b]

                def end(ins, name):
                    ins.then_inc(full[groups[name][0]], 1)

                def chunk(n):
                    pe.wait_ge(ring_ready[n % NG], 16 * (n // NG + 1))
                    return ring_view(n % NG)

                def spread(name, row, c0, n, k=8):
                    bank = begin(name)
                    lo = LATE_ROW if row >= LATE_ROW else 0
                    end(pe.matmul(bank[:, 0:n], ident[lo:lo + k, row:row + 1].to_broadcast([k, P]), rows[lo:lo + k, c0:c0 + n],
                                  start=True, stop=True), name)

                def spread_early():
                    for c_ in range(2):
                        for f in range(2):
                            for w, at in enumerate((DM + CH * f, CH * f)):
                                bank = begin(("m", 0, c_, f, w))
                                end(pe.matmul(bank[:, :], ident[0:2, c_:c_ + 1].to_broadcast([2, P]), early[0:2, at:at + CH],
                                              start=True, stop=True), ("m", 0, c_, f, w))

                def spread_late():
                    sc, sh = mod_row["sc2"], mod_row["sh2"]
                    for c_ in range(2):
                        for f in range(2):
                            spread(("m", 1, c_, f, 0), sc + c_, CH * f, CH)
                            spread(("m", 1, c_, f, 1), sh + c_, CH * f, CH)

                def spread_norm(which):
                    g = mod_row["g1"] if which == 0 else mod_row["g2"]
                    for r, row in enumerate((g, g + 1, LN_ROW + 2 * which, LN_ROW + 2 * which + 1)):
                        for f in range(2):
                            spread(("b", which, r, f), row, CH * f, CH, 8 if r < 2 else SMALL_ROW)

                def turn_x(which):
                    for t in range(TILES):
                        for g in range(2):
                            name = ("xT", which, t, g)
                            bank = begin(name)
                            for k in range(4):
                                ins = pe.transpose(bank[:, P * k:P * k + P], xm[:, t, P * (4 * g + k):P * (4 * g + k + 1)], ident)
                            end(ins, name)

                def modulation(n, c_, k0, bank):
                    w = ring_view(c_ % NG)
                    for k in (k0, k0 + 1):
                        pe.matmul(bank[0:2, :], condT[:, k, :], w[:, k, :], start=(k == 0), stop=False)
                    if k0 + 2 == KD:
                        r = BIAS_ROW + n // 2
                        end(pe.matmul(bank[0:2, :], ident[BIAS_ROW:BIAS_ROW + 6, r:r + 1].to_broadcast([6, 2]),
                                      rows[BIAS_ROW:BIAS_ROW + 6, CH * (n % 2):CH * (n % 2) + CH], start=False, stop=True), ("mod", n))

                def late_step(i):
                    n, k0 = EARLY + i // 4, 2 * (i % 4)
                    if k0 == 0:
                        chunk(EARLY + INC + i // 4)
                        if i:
                            pe.wait_ge(free[7], i // 4)
                    modulation(n, EARLY + INC + i // 4, k0, psum[7])

                for n in range(EARLY):
                    chunk(n)
                    bank = begin(("mod", n))
                    if n == 0:
                        pe.wait_ge(bmod_loaded, 16)
                    for k0 in range(0, KD, 2):
                        modulation(n, n, k0, bank)
                pe.wait_ge(rows_loaded, 160)
                spread(("small",), SMALL_ROW, 512, E + 14, SMALL_ROW + 1)
                spread(("gn",), SMALL_ROW, 0, 512, SMALL_ROW + 1)
                pe.wait_ge(early_ready, EARLY)
                spread_early()
                pe.wait_ge(xm_ready, 1)
                turn_x(0)
                pe.wait_ge(xmT_ready, 6)
                for n in range(INC):
                    banks = [begin(("h", n, t)) for t in range(TILES)]
                    for j in range(2):
                        s, ks, cols = win_half(n, j)
                        pe.wait_ge(win_lo_ready, 2 * n + j + 1)
                        for t in range(TILES):
                            hi, lo = xmT_hi[:, :, P * t:P * t + P], xmT_lo[:, :, P * t:P * t + P]
                            out = banks[t][:, cols]
                            for k in range(4 * j, 4 * j + 4):
                                pe.matmul(out, hi[:, k, :], win_hi[:, k, cols], start=(k == 0), stop=False)
                                pe.matmul(out, lo[:, k, :], win_hi[:, k, cols], start=False, stop=False)
                                ins = pe.matmul(out, hi[:, k, :], w_lo[s][:, k, cols], start=False, stop=(k == KD - 1))
                            if j == 1:
                                end(ins, ("h", n, t))
                        if j == 0:
                            ins.then_inc(win_used, 1)
                pe.wait_ge(rope_done, 1)
                pe.wait_ge(h_act, h_on_act)
                qk_cols = [QA, QA + P, KA, KA + P, QB, QB + P, QB + 2 * P, KB, None, QC, QC + P, QC + 2 * P, KC, KC + P, KC + 2 * P]
                for b, col in enumerate(qk_cols):
                    bank = begin(("qkT", b))
                    for t in range(TILES):
                        src = ksw[:, t, :] if col is None else h[:, t, col:col + P]
                        ins = pe.transpose(bank[:, P * t:P * t + P], src, ident)
                    end(ins, ("qkT", b))
                pe.wait_ge(ctx_loaded, 160)
                for g, blocks in enumerate((range(4), range(4, 5))):
                    bank = begin(("kctxT", g))
                    for i, b in enumerate(blocks):
                        ins = pe.transpose(bank[:, P * i:P * i + P], kctx[:, P * b:P * b + P], ident)
                    end(ins, ("kctxT", g))
                pe.wait_ge(qkT_ready, 15)
                pe.wait_ge(kctxT_ready, 2)
                for hh in range(H_A):
                    p0, g = 64 * (hh % 2), hh // 2
                    q, k = qkT[p0:p0 + 64, g, :], qkT[p0:p0 + 64, 2 + g, :]
                    bank = begin(("sA", hh, 0))
                    pe.matmul(bank[:, 0:P], k[:, 0:P], q[:, 0:P], start=True, stop=True)
                    end(pe.matmul(bank[:, P:3 * P], k[:, P:2 * P], q[:, P:3 * P], start=True, stop=True), ("sA", hh, 0))
                    bank = begin(("sA", hh, 1))
                    end(pe.matmul(bank[:, 0:2 * P], k[:, 2 * P:3 * P], q[:, P:3 * P], start=True, stop=True), ("sA", hh, 1))
                for hh in range(H_A):
                    p0, g = 64 * (hh % 2), hh // 2
                    va = [h[:, t, VA + HD * hh:VA + HD * hh + HD] for t in range(TILES)]
                    bank = begin(("oA", hh))
                    pe.wait_ge(pa_ready, hh + 1)
                    pe.matmul(bank[:, 0:HD], pa[:, 0:P], va[0], start=True, stop=True)
                    pe.wait_ge(qx_ready, 1)
                    for t in (1, 2):
                        out = bank[:, HD * t:HD * t + HD]
                        pe.matmul(out, pa[:, P * t:P * t + P], va[1], start=True, stop=False)
                        pe.matmul(out, pa[:, P * (t + 2):P * (t + 2) + P], va[2], start=False, stop=False)
                        for r in range(2):
                            ins = pe.matmul(out, qx[p0:p0 + 64, r, g, P * (t - 1):P * t], s0[p0:p0 + 64, r, g, :],
                                            start=False, stop=(r == 1))
                    end(ins, ("oA", hh))
                    late_step(2 * hh)
                    late_step(2 * hh + 1)
                bank = begin(("state",))
                pe.wait_ge(kz_ready, 1)
                for r in range(2):
                    for hh in range(H_A):
                        ins = pe.matmul(bank[0:64, HD * (4 * r + hh):HD * (4 * r + hh + 1)], kz[:, r, hh, :],
                                        h[:, 0, VA + HD * hh:VA + HD * hh + HD], start=True, stop=True)
                end(ins, ("state",))

                def scores(g):
                    m, t, h0 = soft[g]
                    if m == "C" and t > 0:
                        pe.wait_ge(bias_masked, t)
                    for i in range(3):
                        hh = h0 + i
                        p0 = 64 * (hh % 2)
                        if m == "B":
                            same = hh // 3 == hh % 2
                            qb, kb, cb = 4 + hh // 2, 7 if same else 8, 0 if same else 1
                        else:
                            qb, kb, cb = 9 + hh // 2, 12 + hh // 2, 2 + hh // 2
                        q = qkT[p0:p0 + 64, qb, P * t:P * t + P]
                        k = qkT[p0:p0 + 64, kb, :]
                        bank = begin(("s", g, i))
                        if t == 0:
                            end(pe.matmul(bank[:, 0:P], q, k[:, 0:P], start=True, stop=True), ("s", g, i))
                            continue
                        if m == "B":
                            for j in (0, 1):
                                masked = j == (t == 1)
                                out = bank[:, P * j:P * j + P]
                                pe.matmul(out, q, k[:, P * (j + 1):P * (j + 2)], start=True, stop=not masked)
                                if masked:
                                    pe.matmul(out, ident, const("band_next" if t == 1 else "band_prev"), start=False, stop=True)
                        else:
                            pe.matmul(bank[:, 0:2 * P], q, k[:, P:3 * P], start=True, stop=False)
                            pe.matmul(bank[:, 0:2 * P], flip, nab[:, hh, :], start=False, stop=True)
                        end(pe.matmul(bank[:, 2 * P:3 * P], q, kctxT[p0:p0 + 64, cb, :], start=True, stop=True), ("s", g, i))

                def mix(g):
                    m, t, h0 = soft[g]
                    nb = 1 if t == 0 else 3
                    pe.wait_ge(exp_done, g + 1)
                    for i in range(3):
                        bank = begin(("pT", g, i))
                        for j in range(nb):
                            ins = pe.transpose(bank[:, P * j:P * j + P], prob[:, i, P * j:P * j + P], ident)
                        end(ins, ("pT", g, i))
                    if g < len(soft) - 1:
                        late_step(2 * H_A + 2 * g + 3)
                    bank = begin(("pv", g))
                    for i in range(3):
                        hh = h0 + i
                        pe.wait_ge(probT_ready, 3 * g + i + 1)
                        for j in range(nb):
                            if j == 2:
                                v = vctx[:, hh // 3 if m == "B" else 2 + hh, :]
                            else:
                                col = VB + HD * (hh // 3) if m == "B" else VC + HD * hh
                                v = h[:, t if t == 0 else j + 1, col:col + HD]
                            ins = pe.matmul(bank[:, HD * i:HD * i + HD], probT[:, i, P * j:P * j + P], v,
                                            start=(j == 0), stop=(j == nb - 1))
                    end(ins, ("pv", g))

                for g in range(len(soft) + 1):
                    if g < len(soft):
                        scores(g)
                        late_step(2 * H_A + 2 * g)
                    if g:
                        mix(g - 1)
                    else:
                        late_step(2 * H_A + 1)
                pe.wait_ge(y_written, len(soft))
                pe.wait_ge(ya_written, 1)
                y_cols = [QA, QA + P, QB, QB + P, QB + 2 * P, QC, QC + P, QC + 2 * P]
                for b, col in enumerate(y_cols):
                    bank = begin(("yT", b))
                    for t in range(TILES):
                        ins = pe.transpose(bank[:, P * t:P * t + P], h[:, t, col:col + P], ident)
                    end(ins, ("yT", b))
                for s in range(2):
                    pe.wait_ge(stage_sent[s], 16 * (LATE // 2))
                spread_norm(0)
                pe.wait_ge(yT_ready, 8)
                for n in range(OUTC):
                    for t in range(TILES):
                        w = chunk(MODC + INC + n)
                        bank = begin(("y", n, t))
                        for k in range(KD):
                            ins = pe.matmul(bank[:, :], xmT[:, k, P * t:P * t + P], w[:, k, :], start=(k == 0), stop=(k == KD - 1))
                        end(ins, ("y", n, t))
                spread_late()
                spread_norm(1)
                pe.wait_ge(xm_ready, 2)
                turn_x(1)
                pe.wait_ge(xmT_ready, 12)
                pe.wait_ge(wr_loaded, 16)
                bank = begin(("logit",))
                for t in range(TILES):
                    for k in range(KD):
                        ins = pe.matmul(bank[:, E * t:E * t + E], xmT[:, k, P * t:P * t + P], wr[:, k, :],
                                        start=(k == 0), stop=(k == KD - 1))
                end(ins, ("logit",))
                pe.wait_ge(mask_ready, 1)
                bank = begin(("pos",))
                for t in range(TILES):
                    for s in range(t + 1):
                        ins = pe.matmul(bank[:, E * t:E * t + E], ones if s < t else before, mask[:, s, :],
                                        start=(s == 0), stop=(s == t))
                for s in range(TILES):
                    ins = pe.matmul(bank[:, E * TILES:E * TILES + E], ones, mask[:, s, :], start=(s == 0), stop=(s == TILES - 1))
                end(ins, ("pos",))
                w = chunk(CHUNKS - 1)
                for t in range(TILES):
                    bank = begin(("sgu", t))
                    for k in range(KD):
                        ins = pe.matmul(bank[:, :], xmT[:, k, P * t:P * t + P], w[:, k, :], start=(k == 0), stop=(k == KD - 1))
                    end(ins, ("sgu", t))
                pe.wait_ge(down_ready[0], 16)
                for t in range(TILES):
                    pe.wait_ge(shid_ready, t + 1)
                    bank = begin(("shT", t))
                    for k in range(2):
                        ins = pe.transpose(bank[:, P * k:P * k + P], hid_s[t % 2][:, P * k:P * k + P], ident)
                    end(ins, ("shT", t))
                    pe.wait_ge(shT_ready, t + 1)
                    for f in range(2):
                        bank = begin(("sy", t, f))
                        for k in range(2):
                            ins = pe.matmul(bank[:, :], shT[:, k, :], down[0][:, k, CH * f:CH * f + CH], start=(k == 0), stop=(k == 1))
                        end(ins, ("sy", t, f))
                assert next(turn, None) is None
                for b in range(8):
                    pe.wait_ge(free[b], bank_uses[b])

                def expert_pass(S, q):
                    b, bx = q * E, q * (E + 1)

                    def turn_rows(m, half, i):
                        pe.wait_ge(S[f"gathered{i % 2}"], (half + (q * 33 + 1)) * 16)
                        pe.wait_ge(S["xT_ready"], m + (bx + 1))
                        for k in range(KD):
                            ins = pe.transpose(psum[2 + k // 4][:, P * (k % 4):P * (k % 4) + P], xg[i % 2][:, P * k:P * k + P], ident)
                        ins.then_inc(S["xT_full"], 1)

                    def down_rows(it, i):
                        e, s = it * UN + i, i % 2
                        pe.wait_ge(S["hT_ready"], e + (b + 2))
                        pe.wait_ge(S["ys_ready"], e + (b + 1))
                        pe.wait_ge(S[f"down_in{s}"], (it * 2 + (i // 2 + (down_base[s] if S is MAIN else 0) + q * (E // ND) + 1)) * 16)
                        for f in range(2):
                            for k in range(2):
                                ins = pe.matmul(psum[5 + f][:, :], hT[s][:, k, :], down[s][:, k, CH * f:CH * f + CH],
                                                start=(k == 0), stop=(k == 1))
                        ins.then_inc(S["y_full"], 1)

                    def turn_of_experts(it):
                        for i in range(UN):
                            e = it * UN + i
                            pe.wait_ge(S["xT_ready"], e + (bx + 2))
                            pe.wait_ge(S["hid_ready"], e + (b + 1))
                            for j in range(2):
                                pe.wait_ge(S["wl_ready"], e * 2 + (2 * b + j + 1))
                                for k in range(4 * j, 4 * j + 4):
                                    wh, wl = w_hi[j][:, k - 4 * j, :], w_lo[i][:, k, :]
                                    pe.matmul(psum[i % 2][:, :], xT_hi[:, k, :], wh, start=(k == 0), stop=False)
                                    pe.matmul(psum[i % 2][:, :], xT_lo[:, k, :], wh, start=False, stop=False)
                                    ins = pe.matmul(psum[i % 2][:, :], xT_hi[:, k, :], wl, start=False, stop=(k == KD - 1))
                                ins.then_inc(S["half_used"], 1)
                            turn_rows(e + 1, it * 2 + (i + 1) // 2, i + 1)
                            pe.wait_ge(S["hid_ready"], e + (b + 3))
                            pe.wait_ge(S["hT_ready"], e + (b + 1))
                            for k in range(2):
                                ins = pe.transpose(psum[4][:, P * k:P * k + P], hid[:, P * k:P * k + P], ident)
                            ins.then_inc(S["hT_full"], 1)
                            if not (isinstance(it, int) and e == 0):
                                down_rows(it, i - 1)

                    turn_rows(0, 0, 0)
                    turn_of_experts(0)
                    with pe.Fori(1, E // UN) as it:
                        turn_of_experts(it)
                    down_rows(E // UN, -1)

                expert_pass(MAIN, 0)
                pe.wait_ge(most_ready, 1)
                with pe.If(pe.value_load(most[0:1, 0:1], min_val=0, max_val=TOK) > P):
                    expert_pass(OVER, 0)
                    expert_pass(OVER, 1)
                    pe.nop()
                for t in range(TILES):
                    pe.wait_ge(back[t], 16 * len(back_in[t]))
                    for f in range(2):
                        for k in range(3):
                            ins = pe.matmul(psum[2 * t + f][:, :], ident, back_rows[t][k][:, CH * f:CH * f + CH], start=(k == 0), stop=(k == 2))
                    ins.then_inc(rows_summed, 1)

            @blk.vector
            def _(dve):
                steps = [0]

                def link(ins):
                    steps[0] += 1
                    ins.then_inc(dve_step, 1)
                    dve.wait_ge(dve_step, steps[0])

                for n in range(EARLY):
                    bank = done(dve, ("mod", n))
                    dve.tensor_copy(early[0:2, CH * n:CH * n + CH], bank[0:2, :]).then_inc(early_ready, 1)
                    dve.wait_ge(early_ready, n + 1)
                    dve.sem_inc(free[groups[("mod", n)][0]], 1)
                bank = done(dve, ("small",))
                link(dve.tensor_copy(small[:, 0:E + 14], bank[:, 0:E + 14]))
                dve.sem_inc(free[groups[("small",)][0]], 1)
                dec = small[:, DEC:DEC + 8]
                link(dve.tensor_scalar(dneg, dec, -1.0, None, ALU.mult))
                dve.tensor_tensor(dneg, dneg, dec, ALU.min).then_inc(dneg_ready, 1)
                dve.wait_ge(softplus_ready, 1)
                link(dve.tensor_scalar(zeta, dec, 0.0, None, ALU.min))
                dve.tensor_tensor(lg, zeta, lg, ALU.subtract).then_inc(lg_ready, 1)

                def modulate(which):
                    for c_ in range(2):
                        if which and c_ == 0:
                            dve.wait_ge(x_pool, 1)
                        if which and c_ == 1:
                            dve.wait_ge(x_ready, 2)
                        for f in range(2):
                            bank = done(dve, ("m", which, c_, f, 0))
                            cols = slice(CH * f, CH * f + CH)
                            tiles = (0,) if c_ == 0 else (1, 2)
                            for t in tiles:
                                ins = dve.scalar_tensor_tensor(out=xm[:, t, cols], in0=bank[:, :], scalar=1.0, in1=x[:, t, cols],
                                                               op0=ALU.add, op1=ALU.mult)
                            give(ins, ("m", which, c_, f, 0))
                            bank = done(dve, ("m", which, c_, f, 1))
                            dve.wait_ge(free[groups[("m", which, c_, f, 0)][0]], groups[("m", which, c_, f, 0)][1] + 1)
                            for t in tiles:
                                ins = dve.tensor_tensor(xm[:, t, cols], xm[:, t, cols], bank[:, :], ALU.add)
                            give(ins, ("m", which, c_, f, 1))
                    name = ("m", which, 1, 1, 1)
                    dve.wait_ge(free[groups[name][0]], groups[name][1] + 1)
                    dve.sem_inc(xm_ready, 1)

                modulate(0)

                def low_win(n, j):
                    s, ks, cols = win_half(n, j)
                    dve.wait_ge(win_hi_ready, 2 * n + j + 1)
                    dve.tensor_tensor(w_lo[s][:, ks, cols], ring_view(s)[:, ks, cols], win_hi[:, ks, cols].bitcast(F32), ALU.subtract
                                      ).then_inc(win_lo_ready, 1)

                low_win(0, 0)
                low_win(0, 1)
                for t in range(TILES):
                    for g in range(2):
                        name = ("xT", 0, t, g)
                        dve.wait_ge(xmT_hi_ready, 2 * t + g + 1)
                        bank = done(dve, name)
                        at = (slice(4 * g, 4 * g + 4), slice(P * t, P * t + P))
                        give(dve.tensor_tensor(xmT_lo[:, at[0], at[1]], bank[:, :].rearrange("p (k t) -> p k t", k=4),
                                               xmT_hi[:, at[0], at[1]].bitcast(F32), ALU.subtract), name)
                        dve.wait_ge(free[groups[name][0]], groups[name][1] + 1)
                        dve.sem_inc(xmT_ready, 1)
                for i, (n, t) in enumerate(HG):
                    if t == 0 and n + 1 < INC:
                        low_win(n + 1, 0)
                    if i % 2 == 0:
                        cols = min(CH, W_IN - CH * n)
                        bank = done(dve, ("h", n, t))
                        give(dve.tensor_copy(h[:, t, CH * n:CH * n + cols], bank[:, 0:cols]), ("h", n, t))
                        dve.wait_ge(free[groups[("h", n, t)][0]], groups[("h", n, t)][1] + 1)
                        dve.sem_inc(h_dve, 1)
                    if t == TILES - 1 and n + 1 < INC:
                        low_win(n + 1, 1)
                dve.wait_ge(h_act, h_on_act)
                rt = prob.rearrange("p i k -> p (i k)")
                r1, r2, r3, r4 = (rt[:, 256 * i:256 * i + 256].rearrange("p (h d) -> p h d", h=8) for i in range(4))
                for t in (1, 2):
                    v = h[:, t, QB:QB + 512].rearrange("p (h s d) -> p h s d", h=8, s=2)
                    x1, x2 = v[:, :, 0, :], v[:, :, 1, :]
                    cos = const("cos")[:, 32 * (t - 1):32 * t].unsqueeze(1).to_broadcast([P, 8, 32])
                    sin = const("sin")[:, 32 * (t - 1):32 * t].unsqueeze(1).to_broadcast([P, 8, 32])
                    dve.tensor_tensor(r1, x1, cos, ALU.mult)
                    dve.tensor_tensor(r2, x2, sin, ALU.mult)
                    dve.tensor_tensor(r3, x1, sin, ALU.mult)
                    link(dve.tensor_tensor(r4, x2, cos, ALU.mult))
                    dve.tensor_tensor(x1, r1, r2, ALU.subtract)
                    link(dve.tensor_tensor(x2, r3, r4, ALU.add))
                link(dve.tensor_copy(ksw[:, :, 0:HD], h[:, :, KB + HD:KB + 2 * HD]))
                dve.tensor_copy(ksw[:, :, HD:2 * HD], h[:, :, KB:KB + HD]).then_inc(rope_done, 1)
                for b in range(15):
                    bank = done(dve, ("qkT", b))
                    s = SCALE if b in (4, 5, 6, 9, 10, 11) else 1.0
                    give(dve.tensor_scalar(qkT[:, b, :], bank[:, 0:TOK], s, None, ALU.mult), ("qkT", b))
                    dve.wait_ge(free[groups[("qkT", b)][0]], groups[("qkT", b)][1] + 1)
                    dve.sem_inc(qkT_ready, 1)
                dve.wait_ge(zeta_ready, 1)
                for r in range(2):
                    ins = dve.tensor_tensor(kz[:, r], h[:, 0, KA:KA + 256].rearrange("p (h d) -> p h d", h=H_A),
                                            zeta[:, 4 * r:4 * r + 4].unsqueeze(2).to_broadcast([P, H_A, HD]), ALU.mult)
                ins.then_inc(kz_ready, 1)
                dve.wait_ge(qx_raw, 1)
                for r in range(2):
                    ins = dve.tensor_tensor(qx[:, r], qx[:, r], qkT[:, 0:2, P:3 * P], ALU.mult)
                ins.then_inc(qx_ready, 1)
                for hh in range(H_A):
                    dve.wait_ge(decay_cut, hh + 1)
                    if hh:
                        done(dve, ("oA", hh - 1))
                    dve.tensor_tensor(decay, decay_f, decay_b, ALU.add).then_inc(decay_ready, 1)
                    dve.wait_ge(decay_ready, hh + 1)
                    bank = done(dve, ("sA", hh, 0))
                    link(dve.scalar_tensor_tensor(out=pa[:, 0:P], in0=bank[:, 0:P], scalar=SCALE, in1=decay[:, P:2 * P],
                                                  op0=ALU.mult, op1=ALU.mult))
                    give(dve.scalar_tensor_tensor(out=pa[:, P:3 * P], in0=bank[:, P:3 * P], scalar=SCALE, in1=decay[:, P:3 * P],
                                                  op0=ALU.mult, op1=ALU.mult), ("sA", hh, 0))
                    bank = done(dve, ("sA", hh, 1))
                    link(dve.scalar_tensor_tensor(out=pa[:, 3 * P:5 * P], in0=bank[:, 0:2 * P], scalar=SCALE, in1=decay[:, 0:2 * P],
                                                  op0=ALU.mult, op1=ALU.mult))
                    dve.sem_inc(free[groups[("sA", hh, 1)][0]], 1)
                    dve.sem_inc(pa_ready, 1)
                    bank = done(dve, ("oA", hh))
                    link(dve.tensor_copy(oA[:, :, hh, :], bank[:, 0:TILES * HD].rearrange("p (t d) -> p t d", t=TILES)))
                    dve.sem_inc(free[groups[("oA", hh)][0]], 1)
                bank = done(dve, ("state",))
                link(dve.tensor_scalar(stout[0:64, :], bank[0:64, :], SCALE, None, ALU.mult))
                dve.sem_inc(free[groups[("state",)][0]], 1)
                dve.sem_inc(state_ready, 1)
                ov = oA.rearrange("p t h d -> p (t h) d")
                tv = tmp.rearrange("p (g d) -> p g d", d=HD)
                link(dve.tensor_reduce(mean, ov, AX.X, ALU.add))
                link(dve.tensor_scalar(mean, mean, 1.0 / HD, None, ALU.mult))
                link(dve.tensor_tensor(ov, ov, mean.unsqueeze(2).to_broadcast([P, 12, HD]), ALU.subtract))
                link(dve.tensor_tensor(tv, ov, ov, ALU.mult))
                link(dve.tensor_reduce(var, tv, AX.X, ALU.add))
                dve.tensor_scalar(var, var, 1.0 / HD, EPS, ALU.mult, ALU.add).then_inc(var_ready, 1)
                dve.wait_ge(root_ready, 1)
                link(dve.reciprocal(var, var))
                link(dve.tensor_tensor(ov, ov, var.unsqueeze(2).to_broadcast([P, 12, HD]), ALU.mult))
                o2 = oA.rearrange("p t h d -> p t (h d)")
                dve.wait_ge(gn_ready, 1)
                link(dve.tensor_tensor(o2, o2, gn[:, 0:256].unsqueeze(1).to_broadcast([P, TILES, 256]), ALU.mult))
                link(dve.tensor_tensor(o2, o2, gn[:, 256:512].unsqueeze(1).to_broadcast([P, TILES, 256]), ALU.add))
                dve.wait_ge(gate_ready, 1)
                dve.tensor_tensor(h[:, :, QA:QA + 256], o2, h[:, :, GA:GA + 256], ALU.mult).then_inc(ya_written, 1)

                def peak(g):
                    m, t, h0 = soft[g]
                    nk = P if t == 0 else 3 * P
                    c3 = slice(3 * g, 3 * g + 3)
                    for i in range(3):
                        bank = done(dve, ("s", g, i))
                        ins = dve.tensor_reduce(mx[:, 3 * g + i:3 * g + i + 1], bank[:, 0:nk], AX.X, ALU.max)
                    link(ins)
                    if m == "B":
                        link(dve.tensor_tensor(mx[:, c3], mx[:, c3], small[:, SINK + h0:SINK + h0 + 3], ALU.max))
                    dve.tensor_scalar(neg[:, c3], mx[:, c3], -1.0, None, ALU.mult).then_inc(neg_ready, 1)
                    if m == "B":
                        dve.wait_ge(neg_ready, g + 1)
                        dve.tensor_tensor(sinkx[:, c3], neg[:, c3], small[:, SINK + h0:SINK + h0 + 3], ALU.add).then_inc(sinkx_ready, 1)

                def weigh(g):
                    m, t, h0 = soft[g]
                    c3 = slice(3 * g, 3 * g + 3)
                    dve.wait_ge(exp_done, g + 1)
                    if m == "B":
                        link(dve.tensor_tensor(den[:, c3], den[:, c3], sinke[:, c3], ALU.add))
                    link(dve.reciprocal(recip[:, c3], den[:, c3]))
                    bank = done(dve, ("pv", g))
                    col = (QB if m == "B" else QC) + HD * h0
                    link(dve.tensor_tensor(h[:, t, col:col + 3 * HD].rearrange("p (i d) -> p i d", i=3),
                                           bank[:, 0:3 * HD].rearrange("p (i d) -> p i d", i=3),
                                           recip[:, c3].unsqueeze(2).to_broadcast([P, 3, HD]), ALU.mult))
                    dve.sem_inc(free[groups[("pv", g)][0]], 1)
                    dve.sem_inc(y_written, 1)

                for g in range(len(soft) + 1):
                    if g < len(soft):
                        peak(g)
                    if g:
                        weigh(g - 1)

                def statistics(t, source):
                    c_ = 0 if t == 0 else 1
                    z = xm[:, t, :]
                    source(t, z, gateb[:, c_, :])
                    link(dve.scalar_tensor_tensor(out=z, in0=x[:, t, :], scalar=ALPHA, in1=z, op0=ALU.mult, op1=ALU.add))
                    for f in range(2):
                        ins = dve.bn_stats(bn[:, 6 * f:6 * f + 6], z[:, CH * f:CH * f + CH])
                    link(ins)
                    link(dve.bn_aggr(bnag[:, 2 * t:2 * t + 2], bn))
                    dve.tensor_scalar(rstd[:, t:t + 1], bnag[:, 2 * t + 1:2 * t + 2], EPS, None, ALU.add).then_inc(lvar_ready, 1)

                def scale_shift(which, t):
                    dve.wait_ge(lroot_ready, TILES * which + t + 1)
                    link(dve.reciprocal(rstd[:, t:t + 1], rstd[:, t:t + 1]))
                    dve.tensor_scalar(shift[:, t:t + 1], bnag[:, 2 * t:2 * t + 1], rstd[:, t:t + 1], -1.0, ALU.mult, ALU.mult).then_inc(shift_ready, 1)

                def norm(which, source):
                    for t in range(TILES):
                        statistics(t, source)
                        if t:
                            scale_shift(which, t - 1)
                    scale_shift(which, TILES - 1)
                    for t in range(1, TILES):
                        dve.wait_ge(normal_ready, TILES * which + t + 1)
                        link(dve.tensor_tensor(xm[:, t, :], xm[:, t, :], lnb[:, 0, :], ALU.mult))
                        dve.tensor_tensor(x[:, t, :], xm[:, t, :], lnb[:, 1, :], ALU.add).then_inc(x_ready, 1)

                dve.wait_ge(caches_stored, 64)
                dve.wait_ge(b_ready, 8)

                def from_psum(t, z, g):
                    for n in range(OUTC):
                        bank = done(dve, ("y", n, t))
                        cols = slice(CH * n, CH * n + CH)
                        link(dve.tensor_tensor(z[:, cols], bank[:, :], g[:, cols], ALU.mult))
                        dve.sem_inc(free[groups[("y", n, t)][0]], 1)

                norm(0, from_psum)
                modulate(1)
                link(dve.memset(sel[:, :, E:E + 2], BIG))
                link(dve.memset(grp[:, :, 8:12], BIG))
                dve.wait_ge(score_ready, 1)
                link(dve.tensor_tensor(sel[:, :, 0:E], score, small[:, 0:E].unsqueeze(1).to_broadcast([P, TILES, E]), ALU.add))
                for t in range(TILES):
                    for g in range(8):
                        ins = dve.max(top[:, 8 * t + g, :], sel[:, t, 8 * g:8 * g + 8])
                link(ins)
                topv = top.rearrange("p (t g) e -> p t g e", t=TILES)
                link(dve.tensor_tensor(grp[:, :, 0:8], topv[:, :, :, 0], topv[:, :, :, 1], ALU.add))
                for t in range(TILES):
                    link(dve.max(top8[:, t, :], grp[:, t, :]))
                    ins = dve.match_replace(grp2[:, t, :], top8[:, t, :], grp[:, t, :], MARK)
                link(ins)
                link(dve.tensor_scalar(grp2[:, :, 0:8], grp2[:, :, 0:8], MARK, None, ALU.is_equal))
                kept = grp2[:, :, 0:8].unsqueeze(3).to_broadcast([P, TILES, 8, 8])
                for t in range(TILES):
                    s8 = sel[:, t, 0:E].rearrange("p (g e) -> p g e", g=8)
                    link(dve.tensor_tensor(s8, s8, kept[:, t], ALU.mult))
                link(dve.tensor_scalar(grp[:, :, 0:8], grp2[:, :, 0:8], -NEG, NEG, ALU.mult, ALU.add))
                for t in range(TILES):
                    s8 = sel[:, t, 0:E].rearrange("p (g e) -> p g e", g=8)
                    link(dve.tensor_tensor(s8, s8, grp[:, t, 0:8].unsqueeze(2).to_broadcast([P, 8, 8]), ALU.add))
                for t in range(TILES):
                    link(dve.max(top8[:, t, :], sel[:, t, :]))
                    ins = dve.match_replace(sel2[:, t, :], top8[:, t, :], sel[:, t, :], MARK)
                link(ins)
                dve.tensor_scalar(mask, sel2[:, :, 0:E], MARK, None, ALU.is_equal).then_inc(mask_ready, 1)
                dve.wait_ge(mask_ready, 1)
                link(dve.tensor_tensor(score, score, mask, ALU.mult))
                link(dve.tensor_reduce(wsum[:, 0:TILES], score, AX.X, ALU.add))
                link(dve.reciprocal(wsum[:, 0:TILES], wsum[:, 0:TILES]))
                link(dve.tensor_tensor(score, score, wsum[:, 0:TILES].unsqueeze(2).to_broadcast([P, TILES, E]), ALU.mult))
                link(dve.tensor_scalar(score, score, ROUTE_SCALE, None, ALU.mult))
                for t in range(TILES):
                    link(dve.tensor_tensor_scan(rank[:, t, :], const("ones")[:, 0:E], mask[:, t, :], 0.0, ALU.mult, ALU.add))
                link(dve.tensor_tensor(rank, rank, mask, ALU.mult))
                full_shape = [P, TILES, TOPK, E]
                link(dve.tensor_tensor(of_rank, rank.unsqueeze(2).to_broadcast(full_shape),
                                       const("from_start")[:, 0:TOPK].unsqueeze(1).unsqueeze(3).to_broadcast(full_shape), ALU.is_equal))
                dve.tensor_tensor(picked, of_rank, score.unsqueeze(2).to_broadcast(full_shape), ALU.mult)
                link(dve.tensor_copy(entry, const("tok_row").rearrange("p (j v) -> p j v", v=3)))
                link(dve.tensor_reduce(entry[:, :, 2], picked.rearrange("p t k e -> p (t k) e"), AX.X, ALU.add))
                bank = done(dve, ("pos",))
                pos = bank[:, 0:TILES * E].rearrange("p (t e) -> p t e", t=TILES)
                link(dve.scalar_tensor_tensor(out=posm, in0=pos, scalar=1.0 * E, in1=const("slot")[:, 0:E].unsqueeze(1).to_broadcast([P, TILES, E]),
                                              op0=ALU.mult, op1=ALU.add))
                link(dve.tensor_tensor(picked, of_rank, posm.unsqueeze(2).to_broadcast(full_shape), ALU.mult))
                link(dve.tensor_reduce(place, picked.rearrange("p t k e -> p (t k) e"), AX.X, ALU.add))
                dve.tensor_copy(place_i[:], place).then_inc(entries_ready, 1)
                link(dve.tensor_reduce(wsum[:, 4:5], bank[:, TILES * E:TILES * E + E], AX.X, ALU.max))
                dve.sem_inc(free[groups[("pos",)][0]], 1)
                dve.tensor_copy(most[:, 0:1], wsum[:, 4:5]).then_inc(most_ready, 1)
                def shared_tail(t):
                    bank = done(dve, ("shT", t))
                    link(dve.tensor_copy(shT, bank[:, 0:2 * P].rearrange("p (k t) -> p k t", k=2)))
                    dve.sem_inc(free[groups[("shT", t)][0]], 1)
                    dve.sem_inc(shT_ready, 1)
                    dve.wait_ge(xm_saved, 16)
                    for f in range(2):
                        bank = done(dve, ("sy", t, f))
                        give(dve.tensor_copy(xm[:, t, CH * f:CH * f + CH], bank[:, :]), ("sy", t, f))

                def take_slots(S, p):
                    dve.wait_ge(table_loaded, 16)
                    dve.tensor_copy(slot_idx[:, :, 0:E], table[:, p, :, 0:2].rearrange("p e v -> p v e"))
                    dve.tensor_copy(slot_w[:], table[:, p, :, 2]).then_inc(S["slots_ready"], 1)

                for t in range(TILES):
                    bank = done(dve, ("sgu", t))
                    dve.wait_ge(ssilu_done, t + 1)
                    if t >= 2:
                        done(dve, ("shT", t - 2))
                    link(dve.tensor_tensor(hid_s[t % 2], sg_s[t], bank[:, F:2 * F], ALU.mult))
                    dve.sem_inc(free[groups[("sgu", t)][0]], 1)
                    dve.sem_inc(shid_ready, 1)
                    if t:
                        shared_tail(t - 1)
                take_slots(MAIN, 0)
                shared_tail(TILES - 1)

                def expert_pass(S, q, p):
                    b, bx = q * E, q * (E + 1)
                    if p:
                        dve.wait_ge(MAIN["pass_done"], 1)
                    if q:
                        dve.wait_ge(S["pass_done"], q)
                    else:
                        dve.sem_inc(S["hid_ready"], 2)
                        dve.sem_inc(S["hT_ready"], 1)
                        dve.sem_inc(S["ys_ready"], 1)
                        dve.sem_inc(S["xT_ready"], 1)
                    if p:
                        take_slots(S, p)
                    dve.wait_ge(S["slots_ready"], q + 1)

                    def rows_out(it, i):
                        s = i % 2
                        dve.wait_ge(S["y_full"], it * UN + (b + i + 1))
                        if not (isinstance(it, int) and it * UN + i < 2):
                            dve.wait_ge(S[f"scattered{s}"], (it * 2 + (i // 2 + q * (E // 2))) * 16)
                        dve.tensor_copy(ys[s][:, 0:CH], psum[5][:, :])
                        dve.tensor_copy(ys[s][:, CH:DM], psum[6][:, :]).then_inc(S["ys_ready"], 1)

                    def low_weights(it, i, j):
                        dve.wait_ge(S["wh_ready"], it * (2 * UN) + (2 * (b + i) + j + 1))
                        half = slice(4 * j, 4 * j + 4)
                        dve.tensor_tensor(w_lo[i % UN][:, half, :], ring_view(i % UN)[:, half, :], w_hi[j].bitcast(F32), ALU.subtract).then_inc(S["wl_ready"], 1)

                    def low_rows(e):
                        dve.wait_ge(S["xh_ready"], e + (bx + 1))
                        for g in range(2):
                            ks = slice(4 * g, 4 * g + 4)
                            ins = dve.tensor_tensor(xT_lo[:, ks, :], psum[2 + g][:, :].rearrange("p (k t) -> p k t", k=4),
                                                    xT_hi[:, ks, :].bitcast(F32), ALU.subtract)
                        ins.then_inc(S["xT_ready"], 1)

                    def turn_of_experts(it):
                        for i in range(UN):
                            e = it * UN + i
                            last = isinstance(it, int) and e == E - 1
                            if not last:
                                low_weights(it, i + 1, 0)
                            dve.wait_ge(S["silu_done"], e + (b + 1))
                            dve.scalar_tensor_tensor(out=hid, in0=sgate, scalar=slot_w[:, e:e + 1] if isinstance(e, int) else slot_w[:, bass.ds(e, 1)],
                                                     in1=psum[i % 2][:, F:2 * F], op0=ALU.mult, op1=ALU.mult).then_inc(S["hid_ready"], 1)
                            dve.wait_ge(S["hT_full"], e + (b + 1))
                            dve.tensor_copy(hT[i % 2], psum[4][:, 0:2 * P].rearrange("p (k t) -> p k t", k=2)).then_inc(S["hT_ready"], 1)
                            low_rows(e + 1)
                            if not last:
                                low_weights(it, i + 1, 1)
                            if not (isinstance(it, int) and e == 0):
                                rows_out(it, i - 1)

                    low_weights(0, 0, 0)
                    low_weights(0, 0, 1)
                    low_rows(0)
                    turn_of_experts(0)
                    with dve.Fori(1, E // UN - 1) as it:
                        turn_of_experts(it)
                    turn_of_experts(E // UN - 1)
                    rows_out(E // UN, -1)

                expert_pass(MAIN, 0, 0)
                dve.wait_ge(most_ready, 1)
                with dve.If(dve.value_load(most[0:1, 0:1], min_val=0, max_val=TOK) > P):
                    expert_pass(OVER, 0, 1)
                    expert_pass(OVER, 1, 2)
                    dve.nop()

                def from_rows(t, z, g):
                    dve.wait_ge(back[t], 16 * len(back_in[t]))
                    for k in (3, 4, 5):
                        link(dve.tensor_tensor(z, z, back_rows[t][k], ALU.add))
                    dve.wait_ge(rows_summed, t + 1)
                    for f in range(2):
                        cols = slice(CH * f, CH * f + CH)
                        ins = dve.tensor_tensor(z[:, cols], z[:, cols], psum[2 * t + f][:, :], ALU.add)
                    link(ins)
                    link(dve.tensor_tensor(z, z, g, ALU.mult))

                norm(1, from_rows)
                dve.wait_ge(x_ready, 4)
                dve.wait_ge(x_pool, 2)

            @blk.scalar
            def _(act):
                def late_rows(i):
                    n = EARLY + i
                    bank = done(act, ("mod", n))
                    if i >= 2:
                        act.wait_ge(stage_sent[n % 2], 16 * (i // 2))
                    act.activation(stage[n % 2], bank[0:2, :], ACT.Copy).then_inc(stage_ready, 1)
                    act.wait_ge(stage_ready, i + 1)
                    act.sem_inc(free[7], 1)
                    act.dma_start(mod_dst(n), stage[n % 2]).then_inc(stage_sent[n % 2], 16)

                act.wait_ge(dneg_ready, 1)
                act.activation(lg, dneg, ACT.Exp).then_inc(act_step, 1)
                act.wait_ge(act_step, 1)
                act.activation(lg, lg, ACT.Ln, bias=1.0).then_inc(softplus_ready, 1)
                bank = done(act, ("gn",))
                give(act.activation(gn, bank[:, :], ACT.Copy), ("gn",))
                act.wait_ge(free[groups[("gn",)][0]], groups[("gn",)][1] + 1)
                act.sem_inc(gn_ready, 1)

                def turned():
                    for t in range(TILES):
                        for g in range(2):
                            name = ("xT", 1, t, g)
                            bank = done(act, name)
                            give(act.activation(xmT[:, 4 * g:4 * g + 4, P * t:P * t + P],
                                                bank[:, :].rearrange("p (k t) -> p k t", k=4), ACT.Copy), name)
                            act.wait_ge(free[groups[name][0]], groups[name][1] + 1)
                            act.sem_inc(xmT_ready, 1)

                def high_win(n, j):
                    s, ks, cols = win_half(n, j)
                    if j == 0:
                        act.wait_ge(ring_ready[s], 16 * ((EARLY + n) // NG + 1))
                    if n and j == 0:
                        act.wait_ge(win_used, n)
                    if n and j == 1:
                        done(act, ("h", n - 1, TILES - 1))
                    act.activation(win_hi[:, ks, cols], ring_view(s)[:, ks, cols], ACT.Copy).then_inc(win_hi_ready, 1)

                high_win(0, 0)
                high_win(0, 1)
                for t in range(TILES):
                    for g in range(2):
                        bank = done(act, ("xT", 0, t, g))
                        act.activation(xmT_hi[:, 4 * g:4 * g + 4, P * t:P * t + P], bank[:, :].rearrange("p (k t) -> p k t", k=4),
                                       ACT.Copy).then_inc(xmT_hi_ready, 1)
                for i, (n, t) in enumerate(HG):
                    if t == 0 and n + 1 < INC:
                        high_win(n + 1, 0)
                    if i % 2 == 1:
                        cols = min(CH, W_IN - CH * n)
                        bank = done(act, ("h", n, t))
                        give(act.activation(h[:, t, CH * n:CH * n + cols], bank[:, 0:cols], ACT.Copy), ("h", n, t))
                        act.wait_ge(free[groups[("h", n, t)][0]], groups[("h", n, t)][1] + 1)
                        act.sem_inc(h_act, 1)
                    if t == TILES - 1 and n + 1 < INC:
                        high_win(n + 1, 1)
                act.wait_ge(lg_ready, 1)
                act.activation(zeta[:, 0:4], lg[:, 0:4], ACT.Exp, scale=const("down")).then_inc(act_step, 1)
                act.activation(zeta[:, 4:8], lg[:, 4:8], ACT.Exp, scale=const("up")).then_inc(act_step, 1)
                act.wait_ge(act_step, 3)
                act.sem_inc(zeta_ready, 1)
                for r, ramp in enumerate(("from_start", "from_end")):
                    for hh in range(H_A):
                        p0 = 64 * (hh % 2)
                        act.activation(qx[p0:p0 + 64, r, hh // 2, :], const(ramp)[p0:p0 + 64, :], ACT.Exp,
                                       scale=lg[p0:p0 + 64, 4 * r + hh:4 * r + hh + 1]).then_inc(act_step, 1)
                act.wait_ge(act_step, 11)
                act.sem_inc(qx_raw, 1)
                for hh in range(H_A):
                    if hh:
                        act.wait_ge(decay_ready, hh)
                    act.activation(decay_f, const("absdiff"), ACT.Exp, scale=lg[:, hh:hh + 1]).then_inc(decay_raw, 1)
                    act.activation(decay_b, const("absdiff"), ACT.Exp, scale=lg[:, 4 + hh:5 + hh]).then_inc(decay_raw, 1)
                    if hh == 0:
                        for g, n in ((0, 4), (1, 1)):
                            bank = done(act, ("kctxT", g))
                            give(act.activation(kctxT[:, 4 * g:4 * g + n, :], bank[:, 0:P * n].rearrange("p (b k) -> p b k", b=n),
                                                ACT.Copy), ("kctxT", g))
                            act.wait_ge(free[groups[("kctxT", g)][0]], groups[("kctxT", g)][1] + 1)
                            act.sem_inc(kctxT_ready, 1)
                act.wait_ge(h_dve, h_on_dve)
                act.activation(h[:, :, GA:GA + 256], h[:, :, GA:GA + 256], ACT.Silu).then_inc(gate_ready, 1)
                late_rows(0)
                act.wait_ge(var_ready, 1)
                act.activation(var, var, ACT.Sqrt).then_inc(root_ready, 1)
                late_rows(1)
                for g in range(len(soft) + 1):
                    if g:
                        m, t, h0 = soft[g - 1]
                        nk = P if t == 0 else 3 * P
                        for i in range(3):
                            bank = done(act, ("pT", g - 1, i))
                            give(act.activation(probT[:, i, 0:nk], bank[:, 0:nk], ACT.Copy), ("pT", g - 1, i))
                            act.wait_ge(free[groups[("pT", g - 1, i)][0]], groups[("pT", g - 1, i)][1] + 1)
                            act.sem_inc(probT_ready, 1)
                    if g < len(soft):
                        m, t, h0 = soft[g]
                        nk = P if t == 0 else 3 * P
                        act.wait_ge(neg_ready, g + 1)
                        for i in range(3):
                            c_ = 3 * g + i
                            bank = psum[groups[("s", g, i)][0]]
                            give(act.activation(prob[:, i, 0:nk], bank[:, 0:nk], ACT.Exp, bias=neg[:, c_:c_ + 1],
                                                accum_out=den[:, c_:c_ + 1]), ("s", g, i))
                        if m == "B":
                            act.wait_ge(sinkx_ready, sum(s[0] == "B" for s in soft[:g + 1]))
                            act.activation(sinke[:, 3 * g:3 * g + 3], sinkx[:, 3 * g:3 * g + 3], ACT.Exp).then_inc(act_step, 1)
                            act.wait_ge(act_step, 11 + sum(s[0] == "B" for s in soft[:g + 1]))
                        for i in range(3):
                            name = ("s", g, i)
                            act.wait_ge(free[groups[name][0]], groups[name][1] + 1)
                        act.sem_inc(exp_done, 1)
                    if g % 2 == 1:
                        late_rows((g + 3) // 2)
                for b in range(8):
                    bank = done(act, ("yT", b))
                    give(act.activation(xmT[:, b, :], bank[:, 0:TOK], ACT.Copy), ("yT", b))
                    act.wait_ge(free[groups[("yT", b)][0]], groups[("yT", b)][1] + 1)
                    act.sem_inc(yT_ready, 1)

                def norm_rows(which):
                    if which:
                        act.wait_ge(x_ready, 2)
                        act.wait_ge(x_pool, 1)
                    else:
                        act.wait_ge(states_stored, 32)
                    for r in range(4):
                        for f in range(2):
                            bank = done(act, ("b", which, r, f))
                            dst = (gateb[:, r, :] if r < 2 else lnb[:, r - 2, :])[:, CH * f:CH * f + CH]
                            give(act.activation(dst, bank[:, :], ACT.Copy), ("b", which, r, f))
                            act.wait_ge(free[groups[("b", which, r, f)][0]], groups[("b", which, r, f)][1] + 1)
                            act.sem_inc(b_ready, 1)

                def norm(which):
                    for t in range(TILES + 1):
                        if t < TILES:
                            act.wait_ge(lvar_ready, TILES * which + t + 1)
                            act.activation(rstd[:, t:t + 1], rstd[:, t:t + 1], ACT.Sqrt).then_inc(lroot_ready, 1)
                        if t:
                            s = t - 1
                            act.wait_ge(shift_ready, TILES * which + t)
                            act.activation(xm[:, s, :], xm[:, s, :], ACT.Identity, scale=rstd[:, s:s + 1], bias=shift[:, s:s + 1]
                                           ).then_inc(normal_ready, 1)

                norm_rows(0)
                norm(0)
                norm_rows(1)
                turned()
                bank = done(act, ("logit",))
                act.activation(score, bank[:, 0:TILES * E].rearrange("p (t e) -> p t e", t=TILES), ACT.Sigmoid).then_inc(score_ready, 1)
                act.wait_ge(score_ready, 1)
                act.sem_inc(free[groups[("logit",)][0]], 1)
                for t in range(TILES):
                    bank = done(act, ("sgu", t))
                    act.activation(sg_s[t], bank[:, 0:F], ACT.Silu).then_inc(ssilu_done, 1)

                def expert_pass(S, q):
                    b, bx = q * E, q * (E + 1)
                    if S is OVER and not q:
                        act.wait_ge(MAIN["pass_done"], 1)

                    def high_rows(m):
                        act.wait_ge(S["xT_full"], m + (bx + 1))
                        act.activation(xT_hi[:, 0:4, :], psum[2][:, :].rearrange("p (k t) -> p k t", k=4), ACT.Copy)
                        act.activation(xT_hi[:, 4:8, :], psum[3][:, :].rearrange("p (k t) -> p k t", k=4), ACT.Copy
                                       ).then_inc(S["xh_ready"], 1)

                    def high_weights(it, i, j):
                        s = i % UN
                        if j == 0:
                            act.wait_ge(S[f"ring_in{s}"], (it + (i // UN + (ring_base[s] if S is MAIN else 0) + q * (E // NG) + 1)) * 16)
                        if not (isinstance(it, int) and b + it * UN + i == 0):
                            act.wait_ge(S["half_used"], it * (2 * UN) + (2 * (b + i) + j - 1))
                        act.activation(w_hi[j], ring_view(s)[:, 4 * j:4 * j + 4, :], ACT.Copy).then_inc(S["wh_ready"], 1)

                    def turn_of_experts(it):
                        for i in range(UN):
                            e = it * UN + i
                            last = isinstance(it, int) and e == E - 1
                            if not last:
                                high_weights(it, i + 1, 0)
                            act.wait_ge(S["half_used"], e * 2 + (2 * b + 2))
                            act.wait_ge(S["hid_ready"], e + (b + 2))
                            act.activation(sgate, psum[i % 2][:, 0:F], ACT.Silu).then_inc(S["silu_done"], 1)
                            high_rows(e + 1)
                            if not last:
                                high_weights(it, i + 1, 1)

                    if S is MAIN:
                        act.wait_ge(entries_ready, 1)
                    high_weights(0, 0, 0)
                    if S is MAIN:
                        done(act, ("sy", 2, 1))
                    high_weights(0, 0, 1)
                    high_rows(0)
                    with act.Fori(0, E // UN - 1) as it:
                        turn_of_experts(it)
                    turn_of_experts(E // UN - 1)

                expert_pass(MAIN, 0)
                act.wait_ge(most_ready, 1)
                with act.If(act.value_load(most[0:1, 0:1], min_val=0, max_val=TOK) > P):
                    expert_pass(OVER, 0)
                    expert_pass(OVER, 1)
                    act.nop()
                norm(1)

            @blk.gpsimd
            def _(pool):
                def mask_bias(t):
                    pool.wait_ge(bias_loaded, 32 * H_C * (t + 1))
                    nm = const("na_mask").unsqueeze(1).to_broadcast([P, H_C, 256])
                    pool.tensor_tensor(nab, nab, nm, ALU.add).then_inc(bias_masked, 1)

                mask_bias(0)
                for hh in range(H_A):
                    pool.wait_ge(decay_raw, 2 * hh + 2)
                    pool.affine_select(out=decay_f, in_=decay_f, compare_op=ALU.is_ge, fill=0.0, base=-P,
                                       pattern=[[1, TOK]], channel_multiplier=-1)
                    pool.affine_select(out=decay_b, in_=decay_b, compare_op=ALU.is_ge, fill=0.0, base=P,
                                       pattern=[[-1, TOK]], channel_multiplier=1).then_inc(decay_cut, 1)
                mask_bias(1)
                def gains(which):
                    pool.wait_ge(normal_ready, TILES * which + 1)
                    pool.tensor_tensor(xm[:, 0, :], xm[:, 0, :], lnb[:, 0, :], ALU.mult).then_inc(scaled_ready, 1)
                    pool.wait_ge(scaled_ready, which + 1)
                    pool.tensor_tensor(x[:, 0, :], xm[:, 0, :], lnb[:, 1, :], ALU.add).then_inc(x_pool, 1)

                gains(0)
                pool.wait_ge(table_empty, 16 * TILES)
                pool.wait_ge(entries_ready, 1)
                for j in range(TILES * TOPK):
                    pool.indirect_dma_start(slots, bass.IndirectOffsetOnAxis(ap=place_i[:, j:j + 1], axis=0),
                                            entry[:, j, :], None, bounds_check=TOK * E - 1, oob_is_err=False
                                            ).then_inc(entries_sent, 16)
                pool.wait_ge(entries_sent, 16 * TILES * TOPK)
                pool.dma_start(table.rearrange("p t e v -> p t (e v)"), slots.rearrange("(t p e) v -> p t (e v)", p=P, e=E)).then_inc(table_loaded, 16)
                pool.wait_ge(yT_ready, 8)
                pool.wait_ge(caches_stored, 64)
                pool.memset(xg[0], 0.0).then_inc(xg_zeroed, 1)
                pool.memset(xg[1], 0.0).then_inc(xg_zeroed, 1)
                pool.wait_ge(xg_zeroed, 2)
                pool.wait_ge(xm_saved, 16)

                def expert_pass(S, q):
                    b, bx, bi = q * E, q * (E + 1), q * (2 * E + 2)
                    pool.wait_ge(S["slots_ready"], q + 1)

                    def gather(par, e, n):
                        pool.tensor_copy(now_idx[par][:], slot_idx[:, 0, e:e + 1] if isinstance(e, int) else slot_idx[:, 0, bass.ds(e, 1)]
                                         ).then_inc(S["idx_set"], 1)
                        pool.wait_ge(S["idx_set"], n)
                        pool.sem_inc(idx_seen, 1)
                        pool.indirect_dma_start(xg[par], None, scratch_x,
                                                bass.IndirectOffsetOnAxis(ap=now_idx[par][:], axis=0),
                                                bounds_check=TOK - 1, oob_is_err=False).then_inc(S[f"gathered{par}"], 16)

                    if q:
                        pool.wait_ge(S["xT_full"], bx)
                    gather(0, 0, bi + 1)
                    gather(1, 1, bi + 2)

                    def scatter(par, e, n):
                        pool.wait_ge(S["ys_ready"], e + (b + 2))
                        pool.tensor_copy(now_idx[2 + par][:], slot_idx[:, 1, e:e + 1] if isinstance(e, int) else slot_idx[:, 1, bass.ds(e, 1)]
                                         ).then_inc(S["idx_set"], 1)
                        pool.wait_ge(S["idx_set"], n)
                        pool.sem_inc(idx_seen, 1)
                        pool.indirect_dma_start(scratch_y, bass.IndirectOffsetOnAxis(ap=now_idx[2 + par][:], axis=0),
                                                ys[par], None, bounds_check=TOK * TOPK - 1, oob_is_err=False
                                                ).then_inc(S[f"scattered{par}"], 16)

                    def turn_of_experts(it):
                        for i in range(UN):
                            e = it * UN + i
                            first = isinstance(it, int) and i == 0
                            pool.wait_ge(S["xT_full"], e + (bx + 1))
                            gather(i % 2, e + 2, e * 2 + (bi + (3 if first else 2)))
                            if not first:
                                scatter((i - 1) % 2, it * UN + (i - 1), e * 2 + (bi + 3))

                    turn_of_experts(0)
                    with pool.Fori(1, E // UN) as it:
                        turn_of_experts(it)
                    scatter(1, E - 1, bi + 2 * E + 2)
                    for par in range(2):
                        pool.wait_ge(S[f"scattered{par}"], 16 * (E // 2) * (q + 1))
                        pool.wait_ge(S[f"gathered{par}"], 16 * 33 * (q + 1))
                    pool.wait_ge(S["xT_full"], bx + E + 1)
                    pool.sem_inc(S["pass_done"], 1)

                expert_pass(MAIN, 0)
                pool.wait_ge(most_ready, 1)
                with pool.If(pool.value_load(most[0:1, 0:1], min_val=0, max_val=TOK) > P):
                    expert_pass(OVER, 0)
                    expert_pass(OVER, 1)
                    pool.nop()
                pool.sem_inc(experts_done, 1)
                gains(1)

            bctx.close()
            numbers = sorted(x.num for x in layer_sems)
            assert numbers == list(range(numbers[0], numbers[-1] + 1))
            nc.gpsimd.dma_reset(range(numbers[0], numbers[-1] + 1))
            nc.gpsimd.sem_clear(range(numbers[0], numbers[-1] + 1))
            nc.all_engine_barrier()

        with ExitStack() as c1:
            tokens_stored = c1.enter_context(nc.semaphore("tokens_stored"))
            blk1 = c1.enter_context(nc.Block())

            @blk1.sync
            def _(sp):
                sp.dma_start(o["y_prompt"][0], x[:, 0, :]).then_inc(tokens_stored, 16)
                sp.dma_start(o["y_sample"][0].rearrange("(t p) d -> p t d", p=P), x[:, 1:3, :]).then_inc(tokens_stored, 16)
                sp.wait_ge(tokens_stored, 32)


INPUTS = ("x_prompt", "x_sample", "state_ret_fwd", "state_ret_bwd", "cache_win_k", "cache_win_v", "cache_na_k",
          "cache_na_v", "c", "c_ctx", "w_in", "w_out", "ret_decay_fwd", "ret_decay_bwd", "ret_gn_g", "ret_gn_b",
          "win_sink", "na_rpb", "w_mod", "b_mod", "ln1_g", "ln1_b", "ln2_g", "ln2_b", "w_router", "b_router",
          "w_expert_gu", "w_expert_down", "w_shared_gu", "w_shared_down")
OUTPUTS = (("y_prompt", (1, P, DM)), ("y_sample", (1, 2 * P, DM)),
           ("new_fwd", (1, DEPTH, H_A, HD, HD)), ("new_bwd", (1, DEPTH, H_A, HD, HD)),
           ("new_win_k", (1, DEPTH, 2, P, HD)), ("new_win_v", (1, DEPTH, 2, P, HD)),
           ("new_na_k", (1, DEPTH, H_C, P, HD)), ("new_na_v", (1, DEPTH, H_C, P, HD)))


def kernel(**inputs):
    import numpy as _np
    import concourse.bacc as _bacc
    from concourse import mybir as _mybir
    from concourse.bass_utils import run_bass_kernel_spmd as _run

    nc = _bacc.Bacc("TRN2", target_bir_lowering=False, num_devices=1)
    arrays, a, o = {}, {}, {}
    for name in INPUTS + ("consts",):
        v = constants() if name == "consts" else _np.ascontiguousarray(inputs[name])
        arrays[f"in_{name}"] = v
        a[name] = nc.dram_tensor(f"in_{name}", v.shape, _mybir.dt.from_np(v.dtype), kind="ExternalInput").ap()
    for name, shape in OUTPUTS:
        o[name] = nc.dram_tensor(f"out_{name}", shape, _mybir.dt.float32, kind="ExternalOutput").ap()
    build(nc, a, o)
    r = _run(nc, [arrays], core_ids=[0])
    return tuple(r.results[0][f"out_{name}"] for name, _ in OUTPUTS)
```
